# Optimizing a Trainium2 kernel written in Bass

```python
import math, functools
import jax
import jax.numpy as jnp
from jax import lax
import numpy as np

D_MODEL = 1024
BATCH = 1
SEQ = 128
DEPTH = 2
DEC_BATCH = 1
DEC_SEQ = 512
PAST_LEN = 128

GRID_W = 64
D_MIX = D_MODEL
HEAD_DIM = 64
D_SSD = D_MIX // 2
SSD_HEADS = D_SSD // HEAD_DIM
SSD_STATE = 64
SSD_GROUPS = 2
SSD_BC = SSD_GROUPS * SSD_STATE
SSD_CHUNK = 128
D_RWKV = D_MIX // 4
RWKV_HEADS = D_RWKV // HEAD_DIM
LORA_W = 32
LORA_A = 32
LORA_G = 64
D_MLSTM = D_MIX // 4
MLSTM_HEADS = D_MLSTM // HEAD_DIM
MLSTM_CHUNK = 128
CONV_W = 3
D_FF = ((8 * D_MODEL + 3 * 256 - 1) // (3 * 256)) * 256
SSD_COLS = 2 * D_SSD + 2 * SSD_BC + 2 * SSD_HEADS
RWKV_COLS = 3 * D_RWKV + 2 * LORA_W + 2 * LORA_A + LORA_G
MLSTM_COLS = 4 * D_MLSTM + 4 * MLSTM_HEADS
D_IN = SSD_COLS + RWKV_COLS + MLSTM_COLS

kernel_name = 'hybrid_ssd_rwkv7_mlstm_diffusion_step'

def _split(u, sizes):
    return jnp.split(u, np.cumsum(sizes)[:-1].tolist(), axis=-1)

def _flip(z):
    return jnp.flip(z, axis=1)

def _rms_norm(x, g, eps=1e-6):
    xf = x.astype(jnp.float32)
    y = xf * lax.rsqrt(jnp.mean(xf * xf, axis=-1, keepdims=True) + eps)
    return (y * g.astype(jnp.float32)).astype(x.dtype)

def _group_norm(y, g, n_groups, center, eps=1e-5):
    shp = y.shape
    yf = y.astype(jnp.float32).reshape(shp[:-1] + (n_groups, shp[-1] // n_groups))
    if center:
        yf = yf - jnp.mean(yf, axis=-1, keepdims=True)
    yf = yf * lax.rsqrt(jnp.mean(yf * yf, axis=-1, keepdims=True) + eps)
    return (yf.reshape(shp) * g.astype(jnp.float32)).astype(y.dtype)

def _dwconv_centred(u, w, b):
    k = w.shape[0]
    out = lax.conv_general_dilated(u, w[:, None, :].astype(u.dtype), window_strides=(1,),
                                   padding=[(k // 2, k // 2)], dimension_numbers=('NWC', 'WIO', 'NWC'),
                                   feature_group_count=u.shape[-1])
    return out + b

def _seq_shift(u):
    b, t, c = u.shape
    g = u.reshape(b, t, c // 2, 2)
    prev = jnp.pad(g[:, :-1, :, 0], ((0, 0), (1, 0), (0, 0)))
    nxt = jnp.pad(g[:, 1:, :, 1], ((0, 0), (0, 1), (0, 0)))
    return jnp.stack([prev, nxt], axis=-1).reshape(b, t, c)

def _grid_shift(u, grid_w):
    b, t, c = u.shape
    rows = t // grid_w
    g = u.reshape(b, rows, grid_w, c // 4, 4)
    left = jnp.pad(g[:, :, :-1, :, 0], ((0, 0), (0, 0), (1, 0), (0, 0)))
    right = jnp.pad(g[:, :, 1:, :, 1], ((0, 0), (0, 0), (0, 1), (0, 0)))
    up = jnp.pad(g[:, :-1, :, :, 2], ((0, 0), (1, 0), (0, 0), (0, 0)))
    down = jnp.pad(g[:, 1:, :, :, 3], ((0, 0), (0, 1), (0, 0), (0, 0)))
    return jnp.stack([left, right, up, down], axis=-1).reshape(b, t, c)

def _bidir(scan_fn, seqs, s0, reverse):
    if reverse:
        y, s = scan_fn(*[_flip(z) for z in seqs], s0)
        return _flip(y), s
    return scan_fn(*seqs, s0)

def _ssd_scan(a, x, dt, bh, ch, s0):
    f32 = jnp.float32
    b, t, nh, p = x.shape
    n = bh.shape[-1]
    L = SSD_CHUNK
    nc = t // L
    la = (dt * a).astype(f32).reshape(b, nc, L, nh)
    xd = (x * dt[..., None]).astype(f32).reshape(b, nc, L, nh, p)
    br = bh.astype(f32).reshape(b, nc, L, nh, n)
    cr = ch.astype(f32).reshape(b, nc, L, nh, n)
    acum = jnp.cumsum(la, axis=2)
    causal = jnp.tril(jnp.ones((L, L), bool))
    seg = acum[:, :, :, None, :] - acum[:, :, None, :, :]
    decay = jnp.exp(jnp.where(causal[None, None, :, :, None], seg, -jnp.inf))
    scores = jnp.einsum('bcthn,bcshn->bctsh', cr, br) * decay
    y = jnp.einsum('bctsh,bcshp->bcthp', scores, xd)
    to_end = jnp.exp(acum[:, :, -1:, :] - acum)
    chunk_states = jnp.einsum('bcsh,bcshn,bcshp->bchpn', to_end, br, xd)
    chunk_decay = jnp.exp(acum[:, :, -1, :])

    def step(s, inp):
        cs, cd = inp
        return s * cd[:, :, None, None] + cs, s

    s_fin, s_start = lax.scan(step, s0.astype(f32),
                              (jnp.moveaxis(chunk_states, 1, 0), jnp.moveaxis(chunk_decay, 1, 0)))
    s_start = jnp.moveaxis(s_start, 0, 1)
    y = y + jnp.einsum('bcthn,bchpn->bcthp', cr, s_start) * jnp.exp(acum)[..., None]
    return y.reshape(b, t, nh, p).astype(x.dtype), s_fin.astype(x.dtype)

def _rwkv7_scan(r, w, k, v, kk, a, s0):
    f32 = jnp.float32
    xs = tuple(jnp.moveaxis(z.astype(f32), 1, 0) for z in (r, w, k, v, kk, a))

    def step(S, inp):
        r_t, w_t, k_t, v_t, kk_t, a_t = inp
        sa = jnp.einsum('bhij,bhj->bhi', S, kk_t)
        S = (S * w_t[:, :, None, :] - sa[..., None] * (kk_t * a_t)[:, :, None, :]
             + v_t[..., None] * k_t[:, :, None, :])
        return S, jnp.einsum('bhij,bhj->bhi', S, r_t)

    s_fin, ys = lax.scan(step, s0.astype(f32), xs)
    return jnp.moveaxis(ys, 0, 1).astype(r.dtype), s_fin.astype(r.dtype)

def _mlstm_chunked(q, k, v, ig, lf, state):
    f32 = jnp.float32
    b, t, nh, dh = q.shape
    L = MLSTM_CHUNK
    nc = t // L
    causal = jnp.tril(jnp.ones((L, L), bool))

    def chunks(z):
        z = z.astype(f32)
        return jnp.moveaxis(z.reshape((b, nc, L) + z.shape[2:]), 1, 0)

    def step(carry, inp):
        c_st, n_st, m_st = carry
        qc, kc, vc, ic, fc = inp
        bcum = jnp.cumsum(fc, axis=1)
        dmat = jnp.where(causal[None, :, :, None],
                         bcum[:, :, None, :] - bcum[:, None, :, :] + ic[:, None, :, :], -jnp.inf)
        inter = bcum + m_st[:, None, :]
        m_t = jnp.maximum(inter, jnp.max(dmat, axis=2))
        wts = jnp.exp(dmat - m_t[:, :, None, :]) * jnp.einsum('bthd,bshd->btsh', qc, kc)
        w_carry = jnp.exp(inter - m_t)
        num = (jnp.einsum('btsh,bshd->bthd', wts, vc)
               + w_carry[..., None] * jnp.einsum('bhij,bthj->bthi', c_st, qc))
        den = jnp.sum(wts, axis=2) + w_carry * jnp.einsum('bhj,bthj->bth', n_st, qc)
        h_t = num / jnp.maximum(jnp.abs(den), jnp.exp(-m_t))[..., None]
        m_new = m_t[:, -1]
        w_end = jnp.exp(bcum[:, -1:] - bcum + ic - m_new[:, None])
        carry_decay = jnp.exp(bcum[:, -1] + m_st - m_new)
        c_new = carry_decay[..., None, None] * c_st + jnp.einsum('bsh,bshi,bshj->bhij', w_end, vc, kc)
        n_new = carry_decay[..., None] * n_st + jnp.einsum('bsh,bshj->bhj', w_end, kc)
        return (c_new, n_new, m_new), h_t

    init = tuple(s.astype(f32) for s in state)
    (c_fin, n_fin, m_fin), hs = lax.scan(step, init, tuple(chunks(z) for z in (q, k, v, ig, lf)))
    h_out = jnp.moveaxis(hs, 0, 1).reshape(b, t, nh, dh).astype(q.dtype)
    return h_out, (c_fin.astype(q.dtype), n_fin.astype(q.dtype), m_fin.astype(q.dtype))

def _ssd_mixer(u, conv_w, conv_b, dt_bias, a_log, d_skip, norm_g, s0):
    b, t, _ = u.shape
    z, xbc, dt_raw = _split(u, [D_SSD, D_SSD + 2 * SSD_BC, 2 * SSD_HEADS])
    xbc = jax.nn.silu(_dwconv_centred(xbc, conv_w, conv_b))
    xs, bm, cm = _split(xbc, [D_SSD, SSD_BC, SSD_BC])
    xs = xs.reshape(b, t, SSD_HEADS, HEAD_DIM)
    rep = SSD_HEADS // SSD_GROUPS
    bh = jnp.repeat(bm.reshape(b, t, SSD_GROUPS, SSD_STATE), rep, axis=2)
    ch = jnp.repeat(cm.reshape(b, t, SSD_GROUPS, SSD_STATE), rep, axis=2)
    dt = jax.nn.softplus(dt_raw.reshape(b, t, 2, SSD_HEADS) + dt_bias)
    a = -jnp.exp(a_log)
    y_f, s_f = _bidir(functools.partial(_ssd_scan, a[0]), (xs, dt[:, :, 0], bh, ch), s0[:, 0], False)
    y_b, s_b = _bidir(functools.partial(_ssd_scan, a[1]), (xs, dt[:, :, 1], bh, ch), s0[:, 1], True)
    y = (y_f + y_b + d_skip[:, None] * xs).reshape(b, t, D_SSD) * jax.nn.silu(z)
    return _group_norm(y, norm_g, SSD_GROUPS, center=False), jnp.stack([s_f, s_b], axis=1)

def _rwkv_mixer(u, grid_w, mu, w0, w2, a0, a2, g2, k_k, k_a, r_k, norm_g, s0):
    b, t, _ = u.shape
    shifted = _grid_shift(u, grid_w) if grid_w else _seq_shift(u)
    u = u + (shifted - u) * mu
    r, k, v, xw, xa, xg = _split(u, [D_RWKV, D_RWKV, D_RWKV, 2 * LORA_W, 2 * LORA_A, LORA_G])

    def heads(z):
        return z.reshape(b, t, RWKV_HEADS, HEAD_DIM)

    w_log = -jax.nn.softplus(-(w0 + jnp.einsum('btdr,drc->btdc', jnp.tanh(xw.reshape(b, t, 2, LORA_W)), w2))) - 0.5
    decay = jnp.exp(-jnp.exp(w_log))
    lr = jax.nn.sigmoid(a0 + jnp.einsum('btdr,drc->btdc', xa.reshape(b, t, 2, LORA_A), a2))
    gate = jax.nn.sigmoid(xg) @ g2
    kkf = heads(k * k_k).astype(jnp.float32)
    kk = (kkf * lax.rsqrt(jnp.sum(kkf * kkf, axis=-1, keepdims=True) + 1e-12)).astype(u.dtype)
    rh, vh, rkh = heads(r), heads(v), r_k.reshape(RWKV_HEADS, HEAD_DIM)

    def direction(d, reverse):
        kd = heads(k * (1 + (lr[:, :, d] - 1) * k_a))
        y, s = _bidir(_rwkv7_scan, (rh, heads(decay[:, :, d]), kd, vh, kk, heads(lr[:, :, d])), s0[:, d], reverse)
        return y + jnp.sum(rh * kd * rkh, axis=-1, keepdims=True) * vh, s

    o_f, s_f = direction(0, False)
    o_b, s_b = direction(1, True)
    y = _group_norm((o_f + o_b).reshape(b, t, D_RWKV), norm_g, RWKV_HEADS, center=True) * gate
    return y, jnp.stack([s_f, s_b], axis=1)

def _mlstm_mixer(u, conv_w, conv_b, i_bias, f_bias, norm_g, c0, n0, m0):
    b, t, _ = u.shape
    qk, v, o, gates = _split(u, [2 * D_MLSTM, D_MLSTM, D_MLSTM, 4 * MLSTM_HEADS])
    q, k = _split(jax.nn.silu(_dwconv_centred(qk, conv_w, conv_b)), [D_MLSTM, D_MLSTM])

    def heads(z):
        return z.reshape(b, t, MLSTM_HEADS, HEAD_DIM)

    q, k, v = heads(q), heads(k) * (HEAD_DIM ** -0.5), heads(v)
    gates = gates.reshape(b, t, 2, 2, MLSTM_HEADS)
    ig = gates[:, :, :, 0] + i_bias
    lf = jax.nn.log_sigmoid(gates[:, :, :, 1] + f_bias)
    h_f, (c_f, n_f, m_f) = _bidir(_mlstm_chunked, (q, k, v, ig[:, :, 0], lf[:, :, 0]),
                                  (c0[:, 0], n0[:, 0], m0[:, 0]), False)
    h_b, (c_b, n_b, m_b) = _bidir(_mlstm_chunked, (q, k, v, ig[:, :, 1], lf[:, :, 1]),
                                  (c0[:, 1], n0[:, 1], m0[:, 1]), True)
    y = _group_norm((h_f + h_b).reshape(b, t, D_MLSTM), norm_g, MLSTM_HEADS, center=True) * jax.nn.sigmoid(o)
    return y, (jnp.stack([c_f, c_b], axis=1), jnp.stack([n_f, n_b], axis=1), jnp.stack([m_f, m_b], axis=1))

def _ada(cond, w, b):
    return jax.nn.silu(cond) @ w + b

def _trunk_layer(x, mod, p, states, grid_w):
    sh1, sc1, g1, sh2, sc2, g2 = jnp.split(mod, 6, axis=-1)
    h = _rms_norm(x, p['norm1_g']) * (1 + sc1) + sh1
    u = h @ p['w_in']
    u_ssd, u_rwkv, u_ml = _split(u, [SSD_COLS, RWKV_COLS, MLSTM_COLS])
    s_ssd, s_rwkv, s_c, s_n, s_m = states
    y_ssd, n_ssd = _ssd_mixer(u_ssd, p['ssd_conv_w'], p['ssd_conv_b'], p['ssd_dt_bias'], p['ssd_a_log'],
                              p['ssd_d'], p['ssd_norm_g'], s_ssd)
    y_rwkv, n_rwkv = _rwkv_mixer(u_rwkv, grid_w, p['rwkv_mu'], p['rwkv_w0'], p['rwkv_w2'], p['rwkv_a0'],
                                 p['rwkv_a2'], p['rwkv_g2'], p['rwkv_k_k'], p['rwkv_k_a'], p['rwkv_r_k'],
                                 p['rwkv_norm_g'], s_rwkv)
    y_ml, (n_c, n_n, n_m) = _mlstm_mixer(u_ml, p['mlstm_conv_w'], p['mlstm_conv_b'], p['mlstm_i_bias'],
                                         p['mlstm_f_bias'], p['mlstm_norm_g'], s_c, s_n, s_m)
    y = jnp.concatenate([y_ssd, y_rwkv, y_ml], axis=-1) @ p['w_out']
    x = x + g1 * y
    h = _rms_norm(x, p['norm2_g']) * (1 + sc2) + sh2
    x = x + g2 * ((jax.nn.silu(h @ p['ffn_w1']) * (h @ p['ffn_w3'])) @ p['ffn_w2'])
    return x, (n_ssd, n_rwkv, n_c, n_n, n_m)

def setup_inputs(seed: int = 0) -> dict:
    key = jax.random.key(seed)
    ks = iter(jax.random.split(key, 64))

    def nrm(shape, scale):
        return scale * jax.random.normal(next(ks), shape, jnp.float32)

    def uni(shape, lo, hi):
        return jax.random.uniform(next(ks), shape, jnp.float32, lo, hi)

    D = D_MODEL
    L2 = (DEPTH, 2)
    dt0 = jnp.exp(uni(L2 + (SSD_HEADS,), math.log(1e-3), math.log(1e-1)))
    return {
        'x_prompt': nrm((BATCH, SEQ, D), 1.0),
        'x_sample': nrm((DEC_BATCH, DEC_SEQ, D), 1.0),
        'state_ssd': nrm((DEC_BATCH, DEPTH, 2, SSD_HEADS, HEAD_DIM, SSD_STATE), 0.1),
        'state_rwkv': nrm((DEC_BATCH, DEPTH, 2, RWKV_HEADS, HEAD_DIM, HEAD_DIM), 0.5),
        'state_mlstm_c': nrm((DEC_BATCH, DEPTH, 2, MLSTM_HEADS, HEAD_DIM, HEAD_DIM), 0.5),
        'state_mlstm_n': nrm((DEC_BATCH, DEPTH, 2, MLSTM_HEADS, HEAD_DIM), 0.5),
        'state_mlstm_m': nrm((DEC_BATCH, DEPTH, 2, MLSTM_HEADS), 1.0),
        'c': nrm((DEC_BATCH, D), 1.0),
        'c_ctx': nrm((D,), 1.0),
        'ada_w': nrm((DEPTH, D, 6 * D), 0.5 * D ** -0.5),
        'ada_b': nrm((DEPTH, 6 * D), 0.02),
        'norm1_g': 1.0 + nrm((DEPTH, D), 0.02),
        'norm2_g': 1.0 + nrm((DEPTH, D), 0.02),
        'w_in': nrm((DEPTH, D, D_IN), D ** -0.5),
        'ssd_conv_w': nrm((DEPTH, CONV_W, D_SSD + 2 * SSD_BC), CONV_W ** -0.5),
        'ssd_conv_b': nrm((DEPTH, D_SSD + 2 * SSD_BC), 0.02),
        'ssd_dt_bias': dt0 + jnp.log(-jnp.expm1(-dt0)),
        'ssd_a_log': jnp.log(uni(L2 + (SSD_HEADS,), 1.0, 16.0)),
        'ssd_d': 1.0 + nrm((DEPTH, SSD_HEADS), 0.1),
        'ssd_norm_g': 1.0 + nrm((DEPTH, D_SSD), 0.02),
        'rwkv_mu': uni((DEPTH, RWKV_COLS), 0.0, 1.0),
        'rwkv_w0': uni(L2 + (D_RWKV,), -3.0, 1.0),
        'rwkv_w2': nrm(L2 + (LORA_W, D_RWKV), 0.5 * LORA_W ** -0.5),
        'rwkv_a0': nrm(L2 + (D_RWKV,), 0.5),
        'rwkv_a2': nrm(L2 + (LORA_A, D_RWKV), 0.5 * LORA_A ** -0.5),
        'rwkv_g2': nrm((DEPTH, LORA_G, D_RWKV), LORA_G ** -0.5),
        'rwkv_k_k': 0.85 + nrm((DEPTH, D_RWKV), 0.05),
        'rwkv_k_a': 1.0 + nrm((DEPTH, D_RWKV), 0.05),
        'rwkv_r_k': nrm((DEPTH, D_RWKV), 0.1),
        'rwkv_norm_g': 1.0 + nrm((DEPTH, D_RWKV), 0.02),
        'mlstm_conv_w': nrm((DEPTH, CONV_W, 2 * D_MLSTM), CONV_W ** -0.5),
        'mlstm_conv_b': nrm((DEPTH, 2 * D_MLSTM), 0.02),
        'mlstm_i_bias': nrm(L2 + (MLSTM_HEADS,), 0.1),
        'mlstm_f_bias': uni(L2 + (MLSTM_HEADS,), 3.0, 6.0),
        'mlstm_norm_g': 1.0 + nrm((DEPTH, D_MLSTM), 0.02),
        'w_out': nrm((DEPTH, D_MIX, D), D_MIX ** -0.5),
        'ffn_w1': nrm((DEPTH, D, D_FF), D ** -0.5),
        'ffn_w3': nrm((DEPTH, D, D_FF), D ** -0.5),
        'ffn_w2': nrm((DEPTH, D_FF, D), D_FF ** -0.5),
        'final_norm_g': 1.0 + nrm((D,), 0.02),
    }

def reference(x_prompt, x_sample, state_ssd, state_rwkv, state_mlstm_c, state_mlstm_n, state_mlstm_m, c,
              c_ctx, ada_w, ada_b, norm1_g, norm2_g, w_in, ssd_conv_w, ssd_conv_b, ssd_dt_bias, ssd_a_log,
              ssd_d, ssd_norm_g, rwkv_mu, rwkv_w0, rwkv_w2, rwkv_a0, rwkv_a2, rwkv_g2, rwkv_k_k, rwkv_k_a,
              rwkv_r_k, rwkv_norm_g, mlstm_conv_w, mlstm_conv_b, mlstm_i_bias, mlstm_f_bias, mlstm_norm_g,
              w_out, ffn_w1, ffn_w3, ffn_w2, final_norm_g):
    bp = x_prompt.shape[0]
    dt_ = x_prompt.dtype
    zero_states = (jnp.zeros((bp, 2, SSD_HEADS, HEAD_DIM, SSD_STATE), dt_),
                   jnp.zeros((bp, 2, RWKV_HEADS, HEAD_DIM, HEAD_DIM), dt_),
                   jnp.zeros((bp, 2, MLSTM_HEADS, HEAD_DIM, HEAD_DIM), dt_),
                   jnp.zeros((bp, 2, MLSTM_HEADS, HEAD_DIM), dt_),
                   jnp.zeros((bp, 2, MLSTM_HEADS), dt_))
    xp, xs = x_prompt, x_sample
    ctx_states = []
    for l in range(DEPTH):
        p = dict(norm1_g=norm1_g[l], norm2_g=norm2_g[l], w_in=w_in[l],
                 ssd_conv_w=ssd_conv_w[l], ssd_conv_b=ssd_conv_b[l], ssd_dt_bias=ssd_dt_bias[l],
                 ssd_a_log=ssd_a_log[l], ssd_d=ssd_d[l], ssd_norm_g=ssd_norm_g[l],
                 rwkv_mu=rwkv_mu[l], rwkv_w0=rwkv_w0[l], rwkv_w2=rwkv_w2[l], rwkv_a0=rwkv_a0[l],
                 rwkv_a2=rwkv_a2[l], rwkv_g2=rwkv_g2[l], rwkv_k_k=rwkv_k_k[l], rwkv_k_a=rwkv_k_a[l],
                 rwkv_r_k=rwkv_r_k[l], rwkv_norm_g=rwkv_norm_g[l],
                 mlstm_conv_w=mlstm_conv_w[l], mlstm_conv_b=mlstm_conv_b[l], mlstm_i_bias=mlstm_i_bias[l],
                 mlstm_f_bias=mlstm_f_bias[l], mlstm_norm_g=mlstm_norm_g[l],
                 w_out=w_out[l], ffn_w1=ffn_w1[l], ffn_w3=ffn_w3[l], ffn_w2=ffn_w2[l])
        mod_ctx = _ada(c_ctx, ada_w[l], ada_b[l])[None, None, :]
        mod_lat = _ada(c, ada_w[l], ada_b[l])[:, None, :]
        xp, st = _trunk_layer(xp, mod_ctx, p, zero_states, None)
        ctx_states.append(st)
        cached = (state_ssd[:, l], state_rwkv[:, l], state_mlstm_c[:, l], state_mlstm_n[:, l], state_mlstm_m[:, l])
        xs, _ = _trunk_layer(xs, mod_lat, p, cached, GRID_W)
    y_prompt = _rms_norm(xp, final_norm_g)
    y_sample = _rms_norm(xs, final_norm_g)
    new_state_ssd = jnp.stack([s[0] for s in ctx_states], axis=1)
    new_state_rwkv = jnp.stack([s[1] for s in ctx_states], axis=1)
    new_state_mlstm_c = jnp.stack([s[2] for s in ctx_states], axis=1)
    new_state_mlstm_n = jnp.stack([s[3] for s in ctx_states], axis=1)
    new_state_mlstm_m = jnp.stack([s[4] for s in ctx_states], axis=1)
    return (y_prompt, y_sample, new_state_ssd, new_state_rwkv, new_state_mlstm_c, new_state_mlstm_n, new_state_mlstm_m)


_drawn_inputs = setup_inputs


def setup_inputs(seed=0):
    import zlib

    import numpy as np

    out = dict(_drawn_inputs(seed))
    spreads = {}
    factors = {'state_rwkv': 8.0,
     'state_mlstm_n': 8.0,
     'state_mlstm_m': 6.312,
     'norm2_g': 7.088,
     'ssd_d': 3.798,
     'ssd_norm_g': 8.0,
     'rwkv_r_k': 8.0,
     'rwkv_norm_g': 43.882,
     'mlstm_norm_g': 42.142,
     'final_norm_g': 7.462}
    for name, (base, spread) in spreads.items():
        noise = np.random.default_rng([zlib.crc32(name.encode()), seed]).standard_normal(out[name].shape)
        drawn = base * np.exp(spread * noise) if base else spread * noise
        out[name] = jnp.asarray(drawn.astype(out[name].dtype))
    for name, factor in factors.items():
        out[name] = (out[name] * factor).astype(out[name].dtype)
    return out
```

```python
from contextlib import ExitStack

import concourse.bass as bass
from concourse import mybir

F32 = mybir.dt.float32
F32R = mybir.dt.float32r
BF16 = mybir.dt.bfloat16
ALU = mybir.AluOpType
ACT = mybir.ActivationFunctionType
AX = mybir.AxisListType

P = 128
D = 1024
DEPTH = 2
CTX, LAT, GRID_W = 128, 512, 64
T = CTX + LAT
NC = T // P
HALF = T // 2
KT = D // P
HD = 64
D_FF = ((8 * D + 3 * 256 - 1) // (3 * 256)) * 256
FT = D_FF // P
SSD_H, RWKV_H, ML_H = 8, 4, 4
SSD_COLS = 2 * 512 + 2 * 128 + 2 * SSD_H
RWKV_COLS = 3 * 256 + 64 + 64 + 64
C_DT = 1280
C_RW = SSD_COLS
C_ML = SSD_COLS + RWKV_COLS
C_GATE = C_ML + 1024
MINUS = -2.0 ** 100
ISQE = 0.6065306597126334

Z, XS, BT_, CT_, RR_, RK_, RV_, LORA, MISC, MQ, MK, MV, MO = 0, 4, 8, 9, 10, 12, 14, 16, 17, 18, 20, 22, 24
NU = 26
U_COL = {m: 128 * m for m in range(10)}
U_COL.update({10 + i: C_RW + 128 * i for i in range(7)})
U_COL.update({18 + i: C_ML + 128 * i for i in range(8)})
ORDER = [MISC] + list(range(4, 10)) + list(range(18, 24)) + list(range(10, 17)) + [24, 25] + list(range(0, 4))
CONV = list(range(4, 10)) + list(range(18, 22))
SHIFT = list(range(10, 18))

PROWS = {}
_at = 0
for _name, _rows in (("ada_b", 48), ("norm1_g", 8), ("norm2_g", 8), ("ssd_conv_w", 18), ("ssd_conv_b", 6),
                     ("mlstm_conv_w", 12), ("mlstm_conv_b", 4), ("ssd_norm_g", 4), ("rwkv_norm_g", 2),
                     ("mlstm_norm_g", 2), ("rwkv_k_k", 2), ("rwkv_k_a", 2), ("rwkv_r_k", 2),
                     ("rwkv_w0", 4), ("rwkv_a0", 4)):
    PROWS[_name] = (_at, _rows)
    _at += _rows
NPROW = _at
MU0 = P

R0, NR = 64, 24
RS = slice(R0, R0 + NR)

RING = 4
NSEM = ["w%d" % i for i in range(RING)] + [
    "par_in", "row_in", "lora_in", "state_in",
    "split_hi", "split_lo", "h_hi", "h_lo", "y_done", "y_hi", "y_lo", "u_hi", "u_lo",
    "par_t", "par_cols", "ada_mm", "mod_ready", "mod_sb", "sq_ready", "sq_used", "std_ready", "xr_ready", "h_ready",
    "pair_mm", "pair_read", "tmp_act", "tmp_dve", "feat_ready", "k_scaled",
    "rows_act", "rows_dve", "kk_sq", "lora_x", "rw_ready",
    "si_t", "si_ready", "ta_mm", "ta_act", "xe_ready", "cs_mm", "cs_read", "states_ready",
    "out_ready", "dec_mm", "dec_diag", "dec_read",
    "bc_mm", "bc_exp", "w_ready", "qk_mm", "xd_ready", "y_mm", "y_comb", "yt_mm", "yt_read",
    "rw_feat", "rw_t", "rw_tok", "rw_prod", "rw_prod2", "rw_masked", "rw_masked2", "pl_ready",
    "inv_mm", "inv_copy", "inv_add", "rhs_mm", "rhs_sb",
    "sa_mm", "sa_sb", "yr_mm", "yr_read", "st_mm", "st_ready", "rs_exp", "rs_dve",
    "g_src", "g_sq", "g_mm", "g_read", "g_std", "g_done", "wo_mm", "wo_read", "ffn_mm", "ffn_silu", "ffn_ready",
    "w2_mm", "w2_read", "rf_ready", "rf_t", "rwo_ready", "act_step", "dve_step", "stored", "stored2",
]


def build(nc, io):
    with ExitStack() as ctx:
        def sb(name, n):
            return ctx.enter_context(nc.sbuf_tensor(name, [P, n], F32))

        s = {n: ctx.enter_context(nc.semaphore(n)) for n in NSEM}
        ring_in = [s[n] for n in NSEM[:RING]]
        first, last_sem = ring_in[0].num, s[NSEM[-1]].num
        assert last_sem - first == len(NSEM) - 1
        setup = {n: ctx.enter_context(nc.semaphore("s_" + n)) for n in
                 ("pool", "in", "cs", "mm", "read", "dve")}
        tail = {n: ctx.enter_context(nc.semaphore("t_" + n)) for n in
                ("sq", "sq_used", "std", "rs", "y", "mm", "read", "stored")}

        PS = ctx.enter_context(nc.psum_tensor("PS", [P, 8, 512], F32))
        x = sb("x", KT * T)
        whi = ctx.enter_context(nc.sbuf_tensor("whi", [P, 2 * KT * P], F32R))
        shared = (("U", NU * T), ("ring", RING * KT * P), ("rwp", 7 * 2 * T), ("arena", 12160))
        with ExitStack() as first_names:
            Ub, ring, rwp, arena = [first_names.enter_context(nc.sbuf_tensor(name, [P, n], F32))
                                    for name, n in shared]
        Ur, ringr, rwpr, arenar = [ctx.enter_context(nc.sbuf_tensor(name + "_r", [P, n], F32R)) for name, n in shared]
        ident, ones, BO, BLK = sb("ident", P), sb("ones", P), sb("BO", P), sb("BLK", P)
        ML = sb("ML", 3 * P)
        NP, PP = sb("NP", 4 * P), sb("PP", 4 * P)
        PC = sb("PC", P + 8)
        MOD, GS = sb("MOD", 96), sb("GS", 32)
        cT, fg = sb("cT", 16), sb("fg", 8)
        OM, MUJ, MU2, PAR = sb("OM", 8), sb("MUJ", 32), sb("MU2", 16), sb("PAR", 6)
        KAO, dcol, RP, RC = sb("KAO", 2), sb("dcol", 4), sb("RP", 8), sb("RC", 8)
        lora = sb("lora", 512)
        SR = sb("SR", 512)
        DEC, DD, DECB = sb("DEC", 5), sb("DD", 120), sb("DECB", 120)
        eps = sb("eps", 4)
        MS5, MC, RE, mfin = sb("MS5", 8), sb("MC", 5), sb("RE", 5), sb("mfin", 4)
        NO, MID, EMID, M16 = sb("NO", 4), sb("MID", 4), sb("EMID", 4), sb("M16", 2 * P)

        identb = ctx.enter_context(nc.sbuf_tensor("identb", [P, P], BF16))
        NEG = ctx.enter_context(nc.sbuf_tensor("NEG", [P, 2 * P], BF16))

        xv = x[:, :].rearrange("p (k t) -> p k t", t=T)
        U = Ub[:, :].rearrange("p (k t) -> p k t", t=T)
        rings = ring[:, :].rearrange("p (r k n) -> p r k n", r=RING, k=KT)
        U_r = Ur[:, :].rearrange("p (k t) -> p k t", t=T)
        rings_r = ringr[:, :].rearrange("p (r k n) -> p r k n", r=RING, k=KT)
        rp_r = rwpr[:, :].rearrange("p (k t) -> p k t", t=T)
        h_r = arenar[:, 0:KT * T].rearrange("p (k t) -> p k t", t=T)
        whis = whi[:, :].rearrange("p (r k n) -> p r k n", r=2, k=KT)
        rp = rwp[:, :].rearrange("p (k t) -> p k t", t=T)
        LW = [rp[:, 2 * d:2 * d + 2, :] for d in range(2)]
        BB = [rp[:, 4 + 2 * d:6 + 2 * d, :] for d in range(2)]
        KD = [rp[:, 8 + 2 * d:10 + 2 * d, :] for d in range(2)]
        KK = rp[:, 12:14, :]

        def ar(at, n):
            return arena[:, at:at + n]

        h = ar(0, KT * T).rearrange("p (k t) -> p k t", t=T)
        rowsA = ar(5120, 3840).rearrange("p (k t) -> p k t", t=T)
        tmp = ar(8960, 1280).rearrange("p (k t) -> p k t", t=T)
        rs = ar(10240, T)
        tanx = ar(10880, T)
        sigx = ar(11520, T)
        Rr, KR, EC, TE, EM, SP = [rowsA[RS, i, :] for i in range(6)]
        zr, t1, t2, LOG, CF, CB, CC, MF, MB = [U[RS, i, :] for i in (0, 1, 2, 3, 24, 25, 14, 15, 16)]
        h_high_r = rp_r[:, 0:KT, :]
        u_high_r = ([U_r[:, i, :] for i in range(FT, NU)] + [rp_r[:, i, :] for i in range(KT, 14)] +
                    [arenar[:, i * T:(i + 1) * T] for i in range(KT, 14)] + [rp_r[:, i, :] for i in range(6)])
        assert len(u_high_r) == FT
        U_EARLY = FT - 6
        S_ssd = ar(0, 2048).rearrange("p (d k n) -> p d k n", d=2, k=4)
        S_ml = ar(2048, 1040).rearrange("p (d k n) -> p d k n", d=2, k=4)
        COLS = ar(3088, 600).rearrange("p (c k r) -> p c k r", c=NC, k=5)
        XT = ar(3688, 512)
        VA = ar(4200, 260).rearrange("p (h n) -> p h n", n=65)
        BK = ar(4460, 384)
        XE = ar(11008, 1024).rearrange("p (d n) -> p d n", d=2)
        VE = ar(8960, 520).rearrange("p (d n) -> p d n", d=2)
        SSI = ar(8960, 1024).rearrange("p (d h n) -> p d h n", d=2, h=4)
        MLI = ar(9984, 512).rearrange("p (d h n) -> p d h n", d=2, h=2)
        RWI = ar(10496, 512).rearrange("p (d h n) -> p d h n", d=2, h=2)
        SO = ar(9484, 512)
        MLO = ar(9996, 512)
        W = ar(5760, 2048).rearrange("p (w n) -> p w n", w=4)
        QKm = ar(7808, 1024).rearrange("p (d n) -> p d n", d=2)
        CBm = ar(8960, 512).rearrange("p (d g n) -> p d g n", d=2, g=2)
        YS, YT = ar(9472, 512), ar(9984, 512)
        NM = ar(4460, 260).rearrange("p (h n) -> p h n", n=65)
        DN = ar(4720, 24)
        SPTE = ar(4860, 16)
        YM = ar(10496, 256)
        YM2 = ar(10752, 256)
        units = []
        for d in range(2):
            o = [6080 * d]

            def take(n):
                o[0] += n
                return ar(o[0] - n, n)
            b = {}
            b["RK"] = take(512).rearrange("p (f w t) -> p f w t", f=2, w=2)
            b["KB"] = take(512).rearrange("p (f w t) -> p f w t", f=2, w=2)
            b["KBT"], b["VT"] = take(512), take(256)
            for n in ("RBT", "BTm", "RKT", "PT", "PL", "Q", "QT", "X"):
                b[n] = take(512).rearrange("p (h t) -> p h t", h=4)
            pl = b["PL"].rearrange("p h t -> p (h t)")
            b["RHS"], b["NSA"] = pl[:, 0:256], pl[:, 256:512]
            for i, n in enumerate(("c", "e1", "e2", "e3", "s")):
                b[n] = Ub[:, 18 * T + 1280 * d + 256 * i:18 * T + 1280 * d + 256 * (i + 1)].rearrange(
                    "p (f t) -> p f t", f=2)
            b["S"] = SR[:, 256 * d:256 * d + 128].rearrange("p (f i) -> p f i", f=2)
            b["Sp"] = SR[:, 256 * d + 128:256 * d + 256].rearrange("p (f i) -> p f i", f=2)
            units.append(b)
        gtmp = ar(0, 8 * T).rearrange("p (k t) -> p k t", t=T)

        def counter():
            n = [0]

            def step():
                n[0] += 1
                return n[0]
            return step

        def col(name, i=0, n=1):
            return PC[:, PROWS[name][0] + i:PROWS[name][0] + i + n]

        def ck(c):
            return slice(c * P, (c + 1) * P)

        with nc.Block() as block:
            @block.gpsimd
            def _(pool):
                g = nc.gpsimd
                step = counter()

                def sel(ap, pattern, cm, base, op, fill=0.0):
                    g.affine_select(out=ap, in_=ap, compare_op=op, fill=fill, base=base,
                                         pattern=pattern, channel_multiplier=cm).then_inc(setup["pool"], 1)
                    pool.wait_ge(setup["pool"], step())

                def blocks(ap, b):
                    g.memset(ap, 1.0).then_inc(setup["pool"], 1)
                    pool.wait_ge(setup["pool"], step())
                    v = ap.rearrange("p (k j) -> p k j", j=b)
                    sel(v, [[-b, P // b], [0, b]], 1, 0, ALU.is_ge)
                    sel(v, [[b, P // b], [0, b]], -1, b - 1, ALU.is_ge)
                g.memset(ring[:, :], 0.0).then_inc(setup["pool"], 1)
                pool.wait_ge(setup["pool"], step())
                g.memset(RP[:, :], 0.0).then_inc(setup["pool"], 1)
                pool.wait_ge(setup["pool"], step())
                g.memset(RC[:, :], 1.0).then_inc(setup["pool"], 1)
                pool.wait_ge(setup["pool"], step())
                g.memset(eps[:, 0:1], 1e-6).then_inc(setup["pool"], 1)
                pool.wait_ge(setup["pool"], step())
                g.memset(eps[:, 1:2], 1e-12).then_inc(setup["pool"], 1)
                pool.wait_ge(setup["pool"], step())
                g.memset(eps[:, 2:3], 1e-5).then_inc(setup["pool"], 1)
                pool.wait_ge(setup["pool"], step())
                g.memset(eps[:, 3:4], 1.0).then_inc(setup["pool"], 1)
                pool.wait_ge(setup["pool"], step())
                g.memset(ones[:, :], 1.0).then_inc(setup["pool"], 1)
                pool.wait_ge(setup["pool"], step())
                g.memset(ident[:, :], 0.0).then_inc(setup["pool"], 1)
                pool.wait_ge(setup["pool"], step())
                sel(ident[:, :], [[-1, P]], 1, 0, ALU.not_equal, 1.0)
                blocks(BLK[:, :], 16)
                blocks(ML[:, 0:P], 32)
                blocks(ML[:, P:2 * P], 64)
                blocks(BO[:, :], 64)
                g.tensor_tensor(ML[:, 2 * P:3 * P], ones[:, :], ML[:, P:2 * P], ALU.subtract).then_inc(setup["pool"], 1)
                pool.wait_ge(setup["pool"], step())
                g.tensor_tensor(ML[:, P:2 * P], ML[:, P:2 * P], ML[:, 0:P], ALU.subtract).then_inc(setup["pool"], 1)
                pool.wait_ge(setup["pool"], step())
                g.tensor_tensor(ML[:, 0:P], ML[:, 0:P], BLK[:, :], ALU.subtract).then_inc(setup["pool"], 1)
                pool.wait_ge(setup["pool"], step())
                for d, sg in ((0, 1), (1, -1)):
                    for M, v in ((NP, -1.0), (PP, 1.0)):
                        a = M[:, 256 * d:256 * d + P]
                        b = M[:, 256 * d + P:256 * d + 2 * P]
                        g.memset(a, v).then_inc(setup["pool"], 1)
                        pool.wait_ge(setup["pool"], step())
                        sel(a, [[sg, P]], -sg, 0, ALU.is_gt)
                        g.memset(b, 1.0).then_inc(setup["pool"], 1)
                        pool.wait_ge(setup["pool"], step())
                        sel(b, [[sg, P]], -sg, 0, ALU.is_ge)
                for c, (lo, hi) in enumerate(((0, 8), (8, 16), (16, 20), (20, 24), (0, 16), (16, 24))):
                    sel(RC[:, c:c + 1], [[0, 1]], 1, -R0 - lo, ALU.is_ge)
                    sel(RC[:, c:c + 1], [[0, 1]], -1, R0 + hi - 1, ALU.is_ge)
                g.tensor_tensor(RC[:, 0:2], RC[:, 0:2], RC[:, 2:4], ALU.add).then_inc(setup["pool"], 1)
                pool.wait_ge(setup["pool"], step())
                g.tensor_scalar(RC[:, 6:8], RC[:, 2:4], -1.0, None, ALU.mult).then_inc(setup["pool"], 1)
                pool.wait_ge(setup["pool"], step())
                g.memset(NEG[:, :], 0.0).then_inc(setup["pool"], 1)
                pool.wait_ge(setup["pool"], step())
                sel(NEG[:, 0:P], [[1, P]], -1, 0, ALU.is_ge, MINUS)
                sel(NEG[:, P:2 * P], [[-1, P]], 1, 0, ALU.is_ge, MINUS)
                g.tensor_copy(identb[:, :], ident[:, :]).then_inc(setup["pool"], 1)
                pool.wait_ge(setup["pool"], step())
                g.memset(Ub[0:8, 2 * P:3 * P], 0.0).then_inc(setup["pool"], 1)
                pool.wait_ge(setup["pool"], step())
                for d in range(2):
                    g.tensor_tensor(M16[:, d * P:(d + 1) * P], NP[:, 256 * d:256 * d + P], BLK[:, :], ALU.mult).then_inc(
                        setup["pool"], 1)
                    pool.wait_ge(setup["pool"], step())

            @block.sync
            def _(sp):
                xi = arena[:, 0:NC * D].rearrange("p (c f) -> p c f", c=NC)
                sp.dma_start(xi[:, 0, :], io["x_prompt"].rearrange("a t f -> (a t) f")).then_inc(setup["in"], 16)
                sp.dma_start(xi[:, 1:NC, :], io["x_sample"].rearrange("a (c p) f -> p (a c) f", p=P)).then_inc(
                    setup["in"], 16)
                sp.dma_start(Ub[0:8, 0:P], io["c_ctx"].rearrange("(k p) -> k p", p=P)).then_inc(setup["in"], 16)
                sp.dma_start(Ub[8:16, 0:P], io["c"].rearrange("a (k p) -> (a k) p", p=P)).then_inc(setup["in"], 16)
                sp.dma_start(Ub[16:24, 0:P], io["final_norm_g"].rearrange("(k p) -> k p", p=P)).then_inc(
                    setup["in"], 16)

            @block.scalar
            def _(act):
                act.wait_ge(setup["in"], 80)
                nc.scalar.activation(Ub[0:16, P:2 * P], Ub[0:16, 0:P], ACT.Silu).then_inc(setup["cs"], 1)

            @block.tensor
            def _(pe):
                pe.wait_ge(setup["in"], 80)
                pe.wait_ge(setup["pool"], 10)
                n = 0
                for c in range(NC):
                    for hf in range(2):
                        if n >= 7:
                            pe.wait_ge(setup["read"], n - 6)
                        for q in range(4):
                            k = 4 * hf + q
                            ins = nc.tensor.transpose(PS[:, n % 7, q * P:(q + 1) * P],
                                                      arena[:, c * D + k * P:c * D + (k + 1) * P], ident[:, :])
                        ins.then_inc(setup["mm"], 1)
                        n += 1
                pe.wait_ge(setup["cs"], 1)
                nc.tensor.transpose(PS[:, 7, 0:16], Ub[0:16, P:2 * P], ident[0:16, 0:16])
                nc.tensor.transpose(PS[:, 7, 32:56], Ub[0:24, 0:P], ident[0:24, 0:24]).then_inc(setup["mm"], 1)

            @block.vector
            def _(dve):
                step = counter()
                for n in range(2 * NC):
                    dve.wait_ge(setup["mm"], n + 1)
                    c, hf = n // 2, n % 2
                    nc.vector.tensor_copy(xv[:, 4 * hf:4 * hf + 4, ck(c)],
                                          PS[:, n % 7, :].rearrange("p (q t) -> p q t", q=4)).then_inc(
                        setup["read"], 1)
                dve.wait_ge(setup["mm"], 2 * NC + 1)
                nc.vector.tensor_copy(cT[:, :], PS[:, 7, 0:16]).then_inc(setup["dve"], 1)
                dve.wait_ge(setup["dve"], step())
                nc.vector.tensor_copy(fg[:, :], PS[:, 7, 48:56]).then_inc(setup["dve"], 1)
                dve.wait_ge(setup["dve"], step())
                dve.wait_ge(setup["pool"], 10)
                nc.vector.tensor_reduce(PAR[:, 2:6], ident[:, :].rearrange("p (k j) -> p j k", j=4),
                                             AX.X, ALU.add).then_inc(setup["dve"], 1)
                dve.wait_ge(setup["dve"], step())
                nc.vector.tensor_tensor(PAR[:, 0:2], PAR[:, 2:4], PAR[:, 4:6], ALU.add).then_inc(setup["dve"], 1)
                dve.wait_ge(setup["dve"], step())

        ADA1 = 16
        BLOCKS = [("ada_w", m) for m in range(ADA1)]
        ADA_AFTER = []
        m_ = ADA1
        for n, m in enumerate(ORDER):
            BLOCKS.append(("w_in", m))
            ADA_AFTER.append(list(range(m_, min(m_ + (2 if n < 6 else 1), 48))))
            m_ += len(ADA_AFTER[-1])
            BLOCKS += [("ada_w", q) for q in ADA_AFTER[-1]]
        assert m_ == 48
        BLOCKS += [("w_out", m) for m in range(KT)]
        for j in range(FT):
            BLOCKS += [("ffn_w1", j), ("ffn_w3", j)]
        W2_PARTS = [(0, 8), (8, 16), (16, FT)]
        BLOCKS += [("ffn_w2", m, k0, k1) for m in range(KT) for k0, k1 in W2_PARTS]
        arrival, used, counts, total = [], [], {}, [0] * RING
        for n, b in enumerate(BLOCKS):
            total[n % RING] += 16 * (6 if b == ("w_in", MISC) else 1)
            arrival.append(total[n % RING])
            name = {"ada_w": "ada_mm", "w_in": "pair_mm", "w_out": "wo_mm", "ffn_w1": "ffn_mm", "ffn_w3": "ffn_mm",
                    "ffn_w2": "w2_mm"}[b[0]]
            counts[name] = counts.get(name, 0) + 1
            used.append((s[name], counts[name]))
        at_block = {b: n for n, b in enumerate(BLOCKS)}
        SPLIT = [n for n, b in enumerate(BLOCKS) if b[0] != "ada_w"]
        Q_WOUT, Q_FFN = NU, NU + KT
        Q_W2 = Q_FFN + 2 * FT

        def size(n):
            return BLOCKS[n][3] - BLOCKS[n][2] if BLOCKS[n][0] == "ffn_w2" else KT

        POST = [m for m in ORDER if m in CONV or m in SHIFT]
        YTILES = [XS, XS + 1, XS + 2, XS + 3, BT_, CT_, MV, MV + 1]
        SHIFTED = {m: i for i, m in enumerate(SHIFT)}

        with nc.Fori(0, DEPTH, 1) as lay:
            def dl(name):
                return io[name][bass.ds(lay, 1)]

            def state(name):
                return io[name][0][bass.ds(lay, 1)]

            with nc.Block() as block:
                @block.sync
                def _(sp):
                    def load(dst, src, sem):
                        sp.dma_start(dst, src, allow_slow_non_contiguous=True).then_inc(sem, 16)

                    def states():
                        sp.wait_ge(s["rw_ready"], 1)
                        for d in range(2):
                            a = state("state_ssd")[:, d].rearrange("a (g h) p n -> p (a h) g n", g=2)
                            for hh in range(4):
                                load(SSI[0:64, d, hh, :].rearrange("p (g n) -> p g n", g=2), a[:, hh], s["state_in"])
                            for buf, nm in ((MLI, "state_mlstm_c"), (RWI, "state_rwkv")):
                                a = state(nm)[:, d].rearrange("a h i j -> i (a h) j")
                                load(buf[0:64, d].rearrange("p f (q j) -> p (f q) j", q=2), a, s["state_in"])
                            a = state("state_mlstm_n")[:, d].rearrange("a (f q) j -> (a q j) f", q=2)
                            load(S_ml[:, d, 0, 64:130:65], a, s["state_in"])
                        sp.wait_ge(s["out_ready"], 1)
                        for d in range(2):
                            o = io["out_2"][0][bass.ds(lay, 1)][:, d].rearrange("a (f q) p n -> (a q p) f n", q=2)
                            load(o, SO[:, 256 * d:256 * d + 256].rearrange("p (f n) -> p f n", f=4), s["stored"])
                            o = io["out_4"][0][bass.ds(lay, 1)][:, d].rearrange("a h i j -> i (a h) j")
                            load(o, MLO[0:64, 256 * d:256 * d + 256].rearrange("p (h j) -> p h j", h=4), s["stored"])
                            o = io["out_5"][0][bass.ds(lay, 1)][:, d].rearrange("a (f q) j -> (a q j) f", q=2)
                            load(o, NO[:, 2 * d:2 * d + 2], s["stored"])
                        o = io["out_6"][0][bass.ds(lay, 1)].rearrange("a d (h o) -> (a d h) o", o=1)
                        load(o, mfin[R0 + 16:R0 + 24, 0:1], s["stored"])
                        sp.wait_ge(s["stored"], 7 * 16)
                        sp.wait_ge(s["rwo_ready"], 2)
                        for d in range(2):
                            o = io["out_3"][0][bass.ds(lay, 1)][:, d].rearrange("a h i j -> i (a h) j")
                            load(o, lora[0:64, 256 * d:256 * d + 256].rearrange("p (h j) -> p h j", h=4), s["stored2"])
                        sp.wait_ge(s["stored2"], 2 * 16)

                    for name, (at, n) in PROWS.items():
                        a = dl(name)
                        dims = " ".join("bcdef"[:len(a.shape) - 1])
                        a = a.rearrange("a %s -> (a %s)" % (dims, dims)).rearrange("(r c) -> r c", c=P)
                        load(Ub[at:at + n, 0:P], a, s["par_in"])
                    mu = dl("rwkv_mu").rearrange("a c -> (a c)")
                    load(Ub[0:7, 2 * P:3 * P], mu[0:7 * P].rearrange("(r c) -> r c", c=P), s["par_in"])
                    load(Ub[7:8, 2 * P:2 * P + 64], mu[7 * P:7 * P + 64].rearrange("(r c) -> r c", r=1), s["par_in"])
                    for cc, r0, r1, a in ((0, 0, 16, dl("ssd_dt_bias")), (0, 16, 24, dl("mlstm_f_bias")),
                                          (1, 16, 24, dl("mlstm_i_bias")), (2, 0, 16, dl("ssd_a_log")),
                                          (3, 16, 24, state("state_mlstm_m"))):
                        load(RP[R0 + r0:R0 + r1, cc:cc + 1], a.rearrange("a d (h o) -> (a d h) o", o=1), s["row_in"])
                    dd = dl("ssd_d").rearrange("a (t q) -> q (a t)", q=2)
                    for q in range(2):
                        load(dcol[64 * q:64 * q + 64, :], dd[q:q + 1, :].broadcast_to((64, 4)), s["row_in"])
                    load(lora[0:64, 0:256], dl("rwkv_w2").rearrange("a d r c -> (a d r) c"), s["lora_in"])
                    load(lora[64:128, 0:256], dl("rwkv_a2").rearrange("a d r c -> (a d r) c"), s["lora_in"])
                    load(lora[0:64, 256:512], dl("rwkv_g2").rearrange("a r c -> (a r) c"), s["lora_in"])
                    for n, blk in enumerate(BLOCKS):
                        if n == at_block["w_out", 0] + RING:
                            states()
                        if n >= RING:
                            sem, value = used[n - RING]
                            sp.wait_ge(sem, value)
                        name, m = blk[0], blk[1]
                        w = dl(name).rearrange("a (k p) n -> p (a k) n", p=P)
                        slot = rings[:, n % RING, :, :]
                        if blk == ("w_in", MISC):
                            gt = C_GATE
                            for at, n_, src in ((0, 64, C_RW + 896), (64, 16, C_DT)):
                                load(slot[:, :, at:at + n_], w[:, :, src:src + n_], ring_in[n % RING])
                            for at, src in ((80, gt + 4), (112, gt)):
                                load(slot[:, :, at:at + 4], w[:, :, src:src + 4], ring_in[n % RING])
                                load(slot[:, :, at + 4:at + 8], w[:, :, src + 8:src + 12], ring_in[n % RING])
                        elif name == "ffn_w2":
                            k0, k1 = blk[2:]
                            load(slot[:, 0:k1 - k0, :], w[:, k0:k1, m * P:(m + 1) * P], ring_in[n % RING])
                        else:
                            at = U_COL[m] if name == "w_in" else m * P
                            load(slot, w[:, :, at:at + P], ring_in[n % RING])

                @block.gpsimd
                def _(pool):
                    for q, n in enumerate(SPLIT):
                        pool.wait_ge(s["split_hi"], q + 1)
                        w = rings[:, n % RING, 0:size(n), :]
                        nc.gpsimd.tensor_tensor(rings_r[:, n % RING, 0:size(n), :], w,
                                                whis[:, q % 2, 0:size(n), :].bitcast(F32),
                                                ALU.subtract).then_inc(s["split_lo"], 1)

                @block.tensor
                def _(pe):
                    mm, tr = nc.tensor.matmul, nc.tensor.transpose

                    def split_block(q):
                        pe.wait_ge(s["split_lo"], q + 1)
                        return whis[:, q % 2, :, :], rings_r[:, SPLIT[q] % RING, :, :]

                    def mm3(out, w, k, hi, lo, cols, start, stop):
                        mm(out, w[0][:, k, :], hi[:, cols], start=start, stop=False)
                        mm(out, w[0][:, k, :], lo[:, cols], start=False, stop=False)
                        return mm(out, w[1][:, k, :], hi[:, cols], start=False, stop=stop)

                    halves = [slice(hf * HALF, (hf + 1) * HALF) for hf in range(2)]

                    def norm_sum(i, k):
                        pe.wait_ge(s["sq_ready"], KT * i + k + 1)
                        for hf in range(2):
                            ins = mm(PS[:, hf, 0:HALF], ones[:, :], tmp[:, k % 2, hf * HALF:(hf + 1) * HALF],
                                     start=k == 0, stop=k == KT - 1)
                        ins.then_inc(s["sq_used"], 1)

                    pe.wait_ge(s["par_in"], 16 * (len(PROWS) + 2))
                    tr(PS[:, 3, 0:NPROW], Ub[0:NPROW, 0:P], ident[0:NPROW, 0:NPROW])
                    tr(PS[:, 3, P:P + 8], Ub[0:8, 2 * P:3 * P], ident[0:8, 0:8]).then_inc(s["par_t"], 1)
                    for k in range(KT):
                        norm_sum(0, k)

                    def ada(m):
                        n = at_block["ada_w", m]
                        pe.wait_ge(ring_in[n % RING], arrival[n])
                        for k in range(KT):
                            ins = mm(PS[:, 2, 2 * m:2 * m + 2], rings[:, n % RING, k, :], cT[:, k:16:8], start=k == 0,
                                     stop=k == KT - 1)
                        ins.then_inc(s["ada_mm"], 1)

                    for m in range(ADA1):
                        ada(m)
                    pair = [0]

                    def pair_banks():
                        n = pair[0]
                        pair[0] += 1
                        if n - 1 > 0:
                            pe.wait_ge(s["pair_read"], n - 1)
                        return 4 + 2 * (n % 2)

                    def pair_mm(b, lhsT, rhs, start=True, stop=True):
                        for hf in range(2):
                            ins = mm(PS[:, b + hf, 0:HALF], lhsT, rhs[:, hf * HALF:(hf + 1) * HALF],
                                     start=start, stop=stop)
                        return ins

                    for n in range(NU):
                        w = split_block(n)
                        b = pair_banks()
                        for k in range(KT):
                            if n == 0:
                                pe.wait_ge(s["h_lo"], k + 1)
                            for hf in range(2):
                                ins = mm3(PS[:, b + hf, 0:HALF], w, k, h_high_r[:, k, :], h_r[:, k, :], halves[hf],
                                          k == 0, k == KT - 1)
                        ins.then_inc(s["pair_mm"], 1)
                        for m in ADA_AFTER[n]:
                            ada(m)

                    for f in range(2):
                        b = pair_banks()
                        pe.wait_ge(s["kk_sq"], f + 1)
                        pair_mm(b, BO[:, :], tmp[:, f, :]).then_inc(s["pair_mm"], 1)
                    pe.wait_ge(s["lora_in"], 48)
                    pe.wait_ge(s["lora_x"], 2)
                    for part, src in ((0, tanx), (64, U[:, LORA, :])):
                        for d in range(2):
                            ps_ = slice(part + 32 * d, part + 32 * d + 32)
                            for f in range(2):
                                b = pair_banks()
                                pair_mm(b, lora[ps_, f * P:(f + 1) * P], src[ps_, :]).then_inc(s["pair_mm"], 1)
                    for f in range(2):
                        b = pair_banks()
                        pair_mm(b, lora[0:64, 256 + f * P:256 + (f + 1) * P], sigx[0:64, :]).then_inc(s["pair_mm"], 1)
                    assert pair[0] == NU + 12

                    pe.wait_ge(s["state_in"], 16 * 14)
                    pe.wait_ge(s["pair_read"], NU + 12)
                    for d in range(2):
                        for q in range(4):
                            tr(PS[:, 6, 256 * d + 64 * q:256 * d + 64 * q + 64], SSI[0:64, d, q, :], ident[0:64, 0:64])
                        for f in range(2):
                            tr(PS[:, 7, 128 * d + 64 * f:128 * d + 64 * f + 64], MLI[0:64, d, f, :], ident[0:64, 0:64])
                            ins = tr(PS[:, 7, 256 + 128 * d + 64 * f:256 + 128 * d + 64 * f + 64],
                                     RWI[0:64, d, f, :], ident[0:64, 0:64])
                    ins.then_inc(s["si_t"], 1)
                    pe.wait_ge(s["dec_diag"], 1)
                    dd = DD[RS, :].rearrange("p (r c) -> p r c", c=5)
                    for q in range(2):
                        o = PS[64 * q:64 * q + 64, 3, 128:188]
                        for d in range(2):
                            mm(o[:, 20 * d:20 * d + 20], ones[RS, 0:64], dd[:, 8 * d + 4 * q:8 * d + 4 * q + 4, :],
                               start=True, stop=True)
                            ins = mm(o[:, 40 + 10 * d:50 + 10 * d], ones[RS, 0:64],
                                     dd[:, 16 + 4 * d + q:20 + 4 * d:2, :], start=True, stop=True)
                    ins.then_inc(s["dec_mm"], 1)
                    pe.wait_ge(s["mod_ready"], 2)
                    pe.wait_ge(s["feat_ready"], len(POST))
                    pe.wait_ge(s["k_scaled"], 2)
                    pe.wait_ge(s["rows_act"], 7)
                    pe.wait_ge(s["dec_read"], 1)
                    for c in range(NC):
                        if 4 * c > 0:
                            pe.wait_ge(s["ta_act"], 4 * c)
                        for q in range(4):
                            tr(PS[:, 0, q * P:(q + 1) * P], U[:, XS + q, ck(c)], ident[:, :])
                        for q, m in enumerate((BT_, MK, MK + 1)):
                            tr(PS[:, 1, q * P:(q + 1) * P], U[:, m, ck(c)], ident[:, :])
                        for q in range(2):
                            tr(PS[:, 2, q * P:(q + 1) * P], U[:, MV + q, ck(c)], ident[:, :])
                        for q, r in enumerate((SP, KR, EC, TE, EM)):
                            ins = tr(PS[:, 3, q * NR:(q + 1) * NR], r[:, ck(c)], ident[RS, R0:R0 + NR])
                        ins.then_inc(s["ta_mm"], 1)
                        pe.wait_ge(s["xe_ready"], c + 1)
                        if c > 0:
                            pe.wait_ge(s["cs_read"], c)
                        pe.wait_ge(s["si_ready"], 6)
                        for d in range(2):
                            if c and not (c < 4 if d == 0 else c > 1):
                                continue
                            for q in range(2):
                                ins = mm(PS[64 * q:64 * q + 64, 4, 256 * d:256 * d + 256], BK[:, 64 * q:64 * q + 64],
                                         XE[:, d, 256 * q:256 * q + 256], start=True, stop=True)
                        for d in range(2):
                            if c and not (c < 4 if d == 0 else c > 1):
                                continue
                            for hh in range(ML_H):
                                f, q = hh // 2, hh % 2
                                ins = mm(PS[64 * q:64 * q + 64, 5, 256 * d + 65 * f:256 * d + 65 * f + 65],
                                         BK[:, P + 64 * hh:P + 64 * hh + 64], VE[:, d, 65 * hh:65 * hh + 65],
                                         start=True, stop=True)
                        if c == 0:
                            for d in range(2):
                                for q in range(4):
                                    mm(PS[:, 6, 256 * d + 64 * q:256 * d + 64 * q + 64],
                                       XE[:, d, q * P:(q + 1) * P], BK[:, 64 * (q // 2):64 * (q // 2) + 64],
                                       start=True, stop=True)
                                for hh in range(ML_H):
                                    ins = mm(PS[0:64, 7, 256 * d + 64 * hh:256 * d + 64 * hh + 64],
                                             VE[:, d, 65 * hh:65 * hh + 64], BK[:, P + 64 * hh:P + 64 * hh + 64],
                                             start=True, stop=True)
                        ins.then_inc(s["cs_mm"], 1)

                    for c in range(NC):
                        if 6 * c > 0:
                            pe.wait_ge(s["bc_exp"], 6 * c)
                        if 3 * c > 0:
                            pe.wait_ge(s["y_comb"], 3 * c)
                        for q in range(4):
                            tr(PS[:, 2, q * P:(q + 1) * P], U[:, XS + q, ck(c)], ident[:, :])
                        for q in range(2):
                            ins = tr(PS[:, 3, q * P:(q + 1) * P], U[:, MV + q, ck(c)], ident[:, :])
                        ins.then_inc(s["ta_mm"], 1)
                        if c == 0:
                            pe.wait_ge(s["ta_act"], 4 * NC)
                            pe.wait_ge(s["states_ready"], 1)
                        for q in range(2):
                            mm(PS[:, q, 0:P], U[64 * q:64 * q + 64, BT_, ck(c)],
                               U[64 * q:64 * q + 64, CT_, ck(c)], start=True, stop=True)
                        for hh in range(ML_H):
                            f, q = hh // 2, hh % 2
                            ins = mm(PS[:, q, (1 + f) * P:(2 + f) * P], U[64 * q:64 * q + 64, MK + f, ck(c)],
                                     U[64 * q:64 * q + 64, MQ + f, ck(c)], start=True, stop=True)
                        ins.then_inc(s["qk_mm"], 1)

                        def row_fill(i):
                            n = 6 * c + i
                            pe.wait_ge(s["ta_act"], 4 * NC + 2 * c + 2)
                            if n - 1 > 0:
                                pe.wait_ge(s["bc_exp"], n - 1)
                            r = (0, 8, 4, 12, 16, 20)[i]
                            for q in range(4):
                                ins = mm(PS[:, 2 + i % 2, q * P:(q + 1) * P],
                                         ident[RS, R0 + r + q:R0 + r + q + 1].broadcast_to((NR, P)), Rr[:, ck(c)],
                                         start=q == 0, stop=False)
                            ins = mm(PS[:, 2 + i % 2, :], identb[:, :],
                                     NEG[:, P * (i % 2):P * (i % 2) + P].unsqueeze(1).broadcast_to((P, 4, P)),
                                     start=False, stop=True)
                            ins.then_inc(s["bc_mm"], 1)

                        def y_ssd(g):
                            pe.wait_ge(s["w_ready"], 6 * c + 2 * g + 2)
                            pe.wait_ge(s["xd_ready"], c + 1)
                            if c > 0:
                                pe.wait_ge(s["yt_read"], c)
                            for q in range(4):
                                hh = 4 * g + q
                                for d in range(2):
                                    ins = mm(PS[:, 4, 64 * hh:64 * hh + 64], W[:, 2 * g + d, q * P:(q + 1) * P],
                                             XE[:, d, 64 * hh:64 * hh + 64], start=d == 0, stop=d == 1)
                            ins.then_inc(s["y_mm"], 1)

                        for i in range(4):
                            row_fill(i)
                        y_ssd(0)
                        for i in range(4, 6):
                            row_fill(i)
                        if c:
                            for d in range(2):
                                k = c - 1 if d == 0 else 4 - c
                                for q in range(2):
                                    mm(PS[:, 5 + q, 256 * d:256 * d + 256], U[64 * q:64 * q + 64, CT_, ck(c)],
                                       S_ssd[64 * q:64 * q + 64, d, k, :], start=True, stop=True)
                        y_ssd(1)
                        for d in range(2):
                            pe.wait_ge(s["w_ready"], 6 * c + 6)
                            num, inter = (7, 0) if d == 0 else (2, 5)
                            if d == 1:
                                pe.wait_ge(s["y_comb"], 3 * c + 1)
                            for hh in range(ML_H):
                                f, q = hh // 2, hh % 2
                                ins = mm(PS[:, num, 65 * hh:65 * hh + 65], W[:, d, hh * P:(hh + 1) * P],
                                         VA[:, hh, :], start=True, stop=True)
                                if c:
                                    k = c - 1 if d == 0 else 4 - c
                                    ins = mm(PS[:, inter + q, 65 * f:65 * f + 65], U[64 * q:64 * q + 64, MQ + f, ck(c)],
                                             S_ml[64 * q:64 * q + 64, d, k, 65 * f:65 * f + 65], start=True, stop=True)
                            ins.then_inc(s["y_mm"], 1)
                        pe.wait_ge(s["y_comb"], 3 * c + 3)
                        for q in range(4):
                            tr(PS[:, 4, q * P:(q + 1) * P], YS[:, q * P:(q + 1) * P], ident[:, :])
                        for q in range(2):
                            ins = tr(PS[:, 6, q * P:(q + 1) * P], YM[:, q * P:(q + 1) * P], ident[:, :])
                        ins.then_inc(s["yt_mm"], 1)

                    def cpos(k, d):
                        return 0 if k == 0 else (k if d == 0 else 5 - k)

                    hq = [(hh // 2, slice(64 * (hh % 2), 64 * (hh % 2) + 64)) for hh in range(RWKV_H)]
                    pe.wait_ge(s["yt_read"], NC)
                    for k in range(NC):
                        for d in range(2):
                            b, a, i = units[d], 4 * d, 2 * k + d
                            pe.wait_ge(s["rw_feat"], i + 1)
                            if i - 1 > 0:
                                pe.wait_ge(s["yr_read"], i - 1)
                            if k == 1:
                                pe.wait_ge(s["rwo_ready"], 2)
                            for w_ in range(2):
                                for f in range(2):
                                    n = 2 * w_ + f
                                    tr(PS[:, a, n * P:(n + 1) * P], b["KB"][:, f, w_, :], ident[:, :])
                            for f in range(2):
                                ins = tr(PS[:, a + 1, f * P:(f + 1) * P], U[:, RV_ + f, ck(cpos(k, d))], ident[:, :])
                            ins.then_inc(s["rw_t"], 1)
                            for hh, (f, q) in enumerate(hq):
                                ins = mm(PS[:, a + 2 + hh % 2, 256 * f:256 * f + 256],
                                         b["KB"][q, f, 1, :], b["RK"][q, f, :, :], start=True, stop=True)
                            ins.then_inc(s["rw_prod"], 1)
                        for d in range(2):
                            b, a, i = units[d], 4 * d, 2 * k + d
                            pe.wait_ge(s["rw_tok"], 2 * i + 2)
                            for hh, (f, q) in enumerate(hq):
                                ins = mm(PS[:, a + hh % 2, f * P:(f + 1) * P], b["RK"][q, f, 0, :], b["KB"][q, f, 1, :],
                                         start=True, stop=True)
                            ins.then_inc(s["rw_prod2"], 1)
                            pe.wait_ge(s["rw_masked"], i + 1)
                            for hh, (f, q) in enumerate(hq):
                                ins = mm(PS[:, a + 2 + hh % 2, 256 * f:256 * f + 256],
                                         b["KB"][q, f, 0, :], b["RK"][q, f, :, :], start=True, stop=True)
                            ins.then_inc(s["rw_prod2"], 1)
                        def each(d, bank, lhs, rhs):
                            b = units[d]
                            for hh in range(RWKV_H):
                                ins = mm(PS[:, 4 * d + bank, hh * P:(hh + 1) * P], b[lhs][:, hh, :], b[rhs][:, hh, :],
                                         start=True, stop=True)
                            return ins

                        def copied(d, r):
                            pe.wait_ge(s["inv_copy"], 12 * k + 2 * r + d + 1)

                        def added(d, r):
                            pe.wait_ge(s["inv_add"], 12 * k + 2 * r + d + 1)

                        for d in range(2):
                            pe.wait_ge(s["rw_masked2"], 2 * k + d + 1)
                            each(d, 0, "QT", "Q")
                            each(d, 3, "Q", "QT").then_inc(s["inv_mm"], 1)
                        for d in range(2):
                            copied(d, 0)
                            each(d, 2, "QT", "X")
                            each(d, 0, "QT", "Q")
                            each(d, 3, "Q", "QT").then_inc(s["inv_mm"], 1)
                        for d in range(2):
                            copied(d, 1)
                            added(d, 0)
                            each(d, 2, "QT", "X")
                            each(d, 3, "Q", "QT").then_inc(s["inv_mm"], 1)
                        for d in range(2):
                            copied(d, 2)
                            added(d, 1)
                            each(d, 2, "QT", "X").then_inc(s["inv_mm"], 1)
                        for l in range(3):
                            for d in range(2):
                                added(d, 2 + l)
                                pe.wait_ge(s["pl_ready"], 6 * k + 2 * l + d + 1)
                                b = units[d]
                                each(d, 0, "PL", "X")
                                for hh in range(RWKV_H):
                                    ins = tr(PS[:, 4 * d + 3, hh * P:(hh + 1) * P], b["X"][:, hh, :], ident[:, :])
                                ins.then_inc(s["inv_mm"], 1)
                            for d in range(2):
                                copied(d, 3 + l)
                                each(d, 2, "QT", "Q").then_inc(s["inv_mm"], 1)
                        for d in range(2):
                            b, a, i = units[d], 4 * d, 2 * k + d
                            for hh, (f, q) in enumerate(hq):
                                o = PS[:, a + hh % 2, 64 * f:64 * f + 64]
                                if k:
                                    mm(o, b["RK"][q, f, 0, :], b["Sp"][q, f, :], start=True, stop=False)
                                ins = mm(o, b["BTm"][:, hh, :], b["VT"][:, 64 * hh:64 * hh + 64], start=not k,
                                         stop=True)
                            ins.then_inc(s["rhs_mm"], 1)
                        for d in range(2):
                            b, a, i = units[d], 4 * d, 2 * k + d
                            added(d, 5)
                            pe.wait_ge(s["rhs_sb"], i + 1)
                            for hh in range(RWKV_H):
                                ins = mm(PS[:, a + 2, 64 * hh:64 * hh + 64], b["X"][:, hh, :],
                                         b["RHS"][:, 64 * hh:64 * hh + 64], start=True, stop=True)
                            ins.then_inc(s["sa_mm"], 1)
                        for d in range(2):
                            b, a, i = units[d], 4 * d, 2 * k + d
                            pe.wait_ge(s["sa_sb"], i + 1)
                            for hh, (f, q) in enumerate(hq):
                                hs = slice(64 * hh, 64 * hh + 64)
                                o = PS[q, a + 3, f * P:(f + 1) * P]
                                if k:
                                    mm(o, b["Sp"][q, f, :], b["RK"][q, f, 1, :], start=True, stop=False)
                                mm(o, b["VT"][:, hs], b["RKT"][:, hh, :], start=not k, stop=False)
                                ins = mm(o, b["NSA"][:, hs], b["RBT"][:, hh, :], start=False, stop=True)
                            ins.then_inc(s["yr_mm"], 1)
                            if k < 4:
                                for hh, (f, q) in enumerate(hq):
                                    hs = slice(64 * hh, 64 * hh + 64)
                                    o = PS[q, a + 1, 64 * f:64 * f + 64]
                                    mm(o, b["KBT"][:, hs], b["VT"][:, hs], start=True, stop=False)
                                    ins = mm(o, b["KBT"][:, 256 + 64 * hh:256 + 64 * hh + 64], b["NSA"][:, hs],
                                             start=False, stop=True)
                                ins.then_inc(s["st_mm"], 1)
                        if k == 0:
                            for d in range(2):
                                pe.wait_ge(s["rf_ready"], d + 1)
                                sf = units[d]["s"].rearrange("p f t -> p (f t)")
                                for f in range(2):
                                    ins = tr(PS[0:64, 4 * d, f * P:(f + 1) * P], sf[:, 64 * f:64 * f + 64],
                                             ident[:, :])
                                ins.then_inc(s["rf_t"], 1)

                    pe.wait_ge(s["yr_read"], 2 * NC)

                    def g_job(j, parts):
                        if j >= 4:
                            o = j - 4
                            pe.wait_ge(s["g_read"], min(o, 5) + 1)
                            if o >= 6:
                                pe.wait_ge(s["g_std"], o - 5)
                        b = 2 * (j % 4)
                        for n, (M, src) in enumerate(parts):
                            for hf in range(2):
                                ins = mm(PS[:, b + hf, 0:HALF], M, src[:, hf * HALF:(hf + 1) * HALF],
                                         start=n == 0, stop=n == len(parts) - 1)
                        ins.then_inc(s["g_mm"], 1)
                    pe.wait_ge(s["rwo_ready"], 2)
                    pe.wait_ge(s["g_src"], 2)
                    g_job(0, [(BO[:, :], gtmp[:, 0, :])])
                    g_job(1, [(BO[:, :], gtmp[:, 1, :])])
                    pe.wait_ge(s["g_src"], 3)
                    for n, t_ in enumerate((BT_, CT_, MV, MV + 1)):
                        g_job(2 + n, [(BO[:, :], U[:, t_, :])])
                    pe.wait_ge(s["g_sq"], 4)
                    g_job(6, [(ones[:, :], gtmp[:, 2, :]), (ones[:, :], gtmp[:, 3, :])])
                    g_job(7, [(ones[:, :], gtmp[:, 4, :]), (ones[:, :], gtmp[:, 5, :])])
                    for n, s_ in enumerate((6, 7, 0, 1)):
                        pe.wait_ge(s["g_sq"], 5 + n)
                        g_job(8 + n, [(BO[:, :], gtmp[:, s_, :])])

                    def residual_mm(b, w, k, hi, lo, start, stop):
                        mm3(PS[:, b, 0:LAT], w, k, hi, lo, slice(CTX, T), start, stop)
                        return mm3(PS[:, b + 1, 0:CTX], w, k, hi, lo, slice(0, CTX), start, stop)

                    for m in range(KT):
                        w = split_block(Q_WOUT + m)
                        if m > 1:
                            pe.wait_ge(s["wo_read"], m - 1)
                        for k, t_ in enumerate(YTILES):
                            if m == 0:
                                pe.wait_ge(s["y_lo"], k + 1)
                            ins = residual_mm(4 + 2 * (m % 2), w, k, rp_r[:, k, :], U_r[:, t_, :], k == 0,
                                              k == KT - 1)
                        ins.then_inc(s["wo_mm"], 1)
                        if m:
                            norm_sum(1, m - 1)
                    norm_sum(1, KT - 1)
                    pe.wait_ge(s["wo_read"], KT)
                    for j in range(FT):
                        for v in range(2):
                            w = split_block(Q_FFN + 2 * j + v)
                            if j > 1:
                                pe.wait_ge(s["ffn_ready"], j - 1)
                            b = 4 * (j % 2) + 2 * v
                            for k in range(KT):
                                if j == 0 and v == 0:
                                    pe.wait_ge(s["h_lo"], KT + k + 1)
                                for hf in range(2):
                                    ins = mm3(PS[:, b + hf, 0:HALF], w, k, h_high_r[:, k, :], h_r[:, k, :], halves[hf],
                                              k == 0, k == KT - 1)
                            ins.then_inc(s["ffn_mm"], 1)
                    pe.wait_ge(s["ffn_ready"], FT)
                    for m in range(KT):
                        if m > 1:
                            pe.wait_ge(s["w2_read"], m - 1)
                        for i, (k0, k1) in enumerate(W2_PARTS):
                            w = split_block(Q_W2 + 3 * m + i)
                            for k in range(k0, k1):
                                if m == 0:
                                    pe.wait_ge(s["u_lo"], k + 1)
                                ins = residual_mm(2 * (m % 2), w, k - k0, u_high_r[k], U_r[:, k, :], k == 0, k == FT - 1)
                            ins.then_inc(s["w2_mm"], 1)

                @block.scalar
                def _(act):
                    A = nc.scalar.activation
                    step = counter()

                    def split(q):
                        if q >= len(SPLIT):
                            return
                        n = SPLIT[q]
                        if q > 1:
                            sem, value = used[SPLIT[q - 2]]
                            act.wait_ge(sem, value)
                        act.wait_ge(ring_in[n % RING], arrival[n])
                        A(whis[:, q % 2, 0:size(n), :], rings[:, n % RING, 0:size(n), :],
                          ACT.Copy).then_inc(s["split_hi"], 1)

                    def norm(i, row0):
                        for k in range(KT):
                            if i:
                                split(Q_WOUT + 2 + k)
                                act.wait_ge(s["wo_read"], k + 1)
                            if KT * i + k - 1 > 0:
                                act.wait_ge(s["sq_used"], KT * i + k - 1)
                            A(tmp[:, k % 2, :], xv[:, k, :], ACT.Square).then_inc(s["sq_ready"], 1)
                        act.wait_ge(s["sq_used"], KT * (i + 1))
                        A(rs.rearrange("p (a t) -> p a t", a=2), PS[:, 0:2, 0:HALF], ACT.Sqrt, bias=eps[:, 0:1],
                          scale=1.0 / D).then_inc(s["std_ready"], 1)
                        act.wait_ge(s["mod_ready"], i + 1)
                        for k in range(KT + 1):
                            if k < KT:
                                act.wait_ge(s["xr_ready"], KT * i + k + 1)
                                for g, ts in ((0, slice(0, CTX)), (1, slice(CTX, T))):
                                    A(h[:, k, ts], h[:, k, ts], ACT.Identity,
                                      bias=MOD[:, 2 * (row0 + k) + g:2 * (row0 + k) + g + 1],
                                      scale=GS[:, 16 * i + 2 * k + g:16 * i + 2 * k + g + 1]).then_inc(
                                        s["h_ready"], 1)
                            if k:
                                act.wait_ge(s["h_ready"], 2 * (KT * i + k))
                                A(h_high_r[:, k - 1, :], h[:, k - 1, :], ACT.Copy).then_inc(s["h_hi"], 1)

                    act.wait_ge(s["par_t"], 1)
                    A(PC[:, 0:NPROW], PS[:, 3, 0:NPROW], ACT.Copy)
                    A(PC[:, P:P + 8], PS[:, 3, P:P + 8], ACT.Copy).then_inc(s["par_cols"], 1)
                    norm(0, 0)
                    act.wait_ge(s["par_cols"], 1)
                    for q in range(2):
                        split(q)

                    def pair_out(n, out, func, **kw):
                        act.wait_ge(s["pair_mm"], n + 1)
                        b = 4 + 2 * (n % 2)
                        A(out.rearrange("p (a t) -> p a t", a=2), PS[:, b:b + 2, 0:HALF], func, **kw).then_inc(
                            s["pair_read"], 1)

                    def post_start(j, n):
                        m = POST[j]
                        act.wait_ge(s["pair_read"], n + 1)
                        pp = slice(0, 64) if m == MISC else slice(0, P)
                        if m in SHIFTED:
                            c = OM[pp, SHIFTED[m]:SHIFTED[m] + 1]
                            A(tmp[pp, j % 2, :], U[pp, m, :], ACT.Identity, scale=c).then_inc(s["tmp_act"], 1)
                        else:
                            nm, i, w_ = ("ssd", m - XS, 6) if m < MISC else ("mlstm", m - MQ, 4)
                            A(tmp[:, j % 2, :], U[:, m, :], ACT.Identity, scale=col(nm + "_conv_w", w_ + i),
                                  bias=col(nm + "_conv_b", i)).then_inc(s["tmp_act"], 1)

                    def post_end(j):
                        m = POST[j]
                        pp = slice(0, 64) if m == MISC else slice(0, P)
                        act.wait_ge(s["tmp_dve"], j + 1)
                        A(U[pp, m, :], tmp[pp, j % 2, :], ACT.Silu if m in CONV else ACT.Copy).then_inc(
                            s["feat_ready"], 1)

                    j = 0
                    for n, m in enumerate(ORDER):
                        func = ACT.Silu if m < XS else ACT.Sigmoid if m >= MO else ACT.Copy
                        pair_out(n, U[:, m, :], func)
                        split(n + 2)
                        if n == 0:
                            act.wait_ge(s["pair_read"], 1)
                            act.wait_ge(s["rows_dve"], 1)
                            A(RP[RS, 6:7], RP[RS, 2:3], ACT.Exp).then_inc(s["rows_act"], 1)
                            A(zr, U[RS, MISC, :], ACT.Identity, scale=RP[RS, 4:5], bias=RP[RS, 5:6]).then_inc(
                                s["rows_act"], 1)
                            A(KR, U[96:96 + NR, MISC, :], ACT.Copy).then_inc(s["rows_act"], 1)
                            act.wait_ge(s["rows_act"], 3)
                            A(t1, zr, ACT.Abs).then_inc(s["act_step"], 1)
                            act.wait_ge(s["act_step"], step())
                            A(t1, t1, ACT.Exp, scale=-1.0).then_inc(s["rows_act"], 1)
                        if n == 1:
                            act.wait_ge(s["rows_dve"], 2)
                            A(CF, t2, ACT.Ln).then_inc(s["rows_act"], 1)
                        if n == 4:
                            act.wait_ge(s["rows_dve"], 3)
                            for c in range(NC):
                                ins = A(DEC[RS, c:c + 1], RE[RS, c:c + 1], ACT.Exp, bias=MC[RS, c:c + 1])
                            ins.then_inc(s["rows_act"], 1)
                            for c in range(NC):
                                A(EC[:, ck(c)], Rr[:, ck(c)], ACT.Exp, bias=MC[RS, c:c + 1])
                                A(TE[:, ck(c)], KR[:, ck(c)], ACT.Exp, bias=RE[RS, c:c + 1])
                            A(EM, EM, ACT.Exp).then_inc(s["rows_act"], 1)
                        if m in POST:
                            post_start(j, n)
                            if j:
                                post_end(j - 1)
                            j += 1
                        elif j == len(POST):
                            post_end(j - 1)
                            j += 1
                            act.wait_ge(s["feat_ready"], len(POST))
                            for f in range(2):
                                A(KK[:, f, :], U[:, RK_ + f, :], ACT.Identity, scale=col("rwkv_k_k", f))
                            A(tanx[0:64, :], U[0:64, LORA, :], ACT.Tanh).then_inc(s["act_step"], 1)
                            act.wait_ge(s["act_step"], step())
                            for f in range(2):
                                A(tmp[:, f, :], KK[:, f, :], ACT.Square).then_inc(s["kk_sq"], 1)
                            A(sigx[0:64, :], U[0:64, MISC, :], ACT.Sigmoid).then_inc(s["lora_x"], 1)
                            A(tanx[0:64, 0:1], tanx[0:64, 0:1], ACT.Copy).then_inc(s["lora_x"], 1)
                    for f in range(2):
                        pair_out(NU + f, tmp[:, f, :], ACT.Sqrt, bias=eps[:, 1:2])
                    n = NU + 2
                    for dst, nm in ((LW, "rwkv_w0"), (BB, "rwkv_a0")):
                        for d in range(2):
                            for f in range(2):
                                pair_out(n, dst[d][:, f, :], ACT.Sigmoid, bias=col(nm, 2 * d + f))
                                n += 1
                    for f in range(2):
                        pair_out(n, U[:, LORA + f, :], ACT.Copy)
                        n += 1
                    act.wait_ge(s["si_t"], 1)
                    for d in range(2):
                        A(S_ssd[:, d, 0, :], PS[:, 6, 256 * d:256 * d + 256], ACT.Copy).then_inc(s["si_ready"], 1)
                        A(S_ml[:, d, 0, :].rearrange("p (f n) -> p f n", f=2)[:, :, 0:64],
                              PS[:, 7, P * d:P * d + P].rearrange("p (f n) -> p f n", f=2), ACT.Copy).then_inc(
                                  s["si_ready"], 1)
                        A(units[d]["S"], PS[:, 7, 256 + P * d:256 + P * d + P].rearrange(
                            "p (f n) -> p f n", f=2), ACT.Copy).then_inc(s["si_ready"], 1)
                    act.wait_ge(s["dec_mm"], 1)
                    A(DECB[:, 0:60], PS[:, 3, 128:188], ACT.Copy).then_inc(s["dec_read"], 1)
                    for c in range(NC):
                        act.wait_ge(s["ta_mm"], c + 1)
                        if c > 0:
                            act.wait_ge(s["xe_ready"], c)
                        if c > 0:
                            act.wait_ge(s["cs_mm"], c)
                        A(XT, PS[:, 0, :], ACT.Copy).then_inc(s["ta_act"], 1)
                        A(BK, PS[:, 1, 0:384], ACT.Copy).then_inc(s["ta_act"], 1)
                        A(VA[:, :, 0:64], PS[:, 2, 0:256].rearrange("p (h n) -> p h n", h=4), ACT.Copy).then_inc(
                            s["ta_act"], 1)
                        A(COLS[:, c].rearrange("p k r -> p (k r)"), PS[:, 3, 0:120], ACT.Copy).then_inc(s["ta_act"], 1)
                        act.wait_ge(s["cs_mm"], c + 1)
                        if c == 0:
                            A(SO, PS[:, 6, :], ACT.Copy)
                            A(MLO[0:64, :], PS[0:64, 7, :], ACT.Copy)
                            for d in range(2):
                                ins = A(NO[:, 2 * d:2 * d + 2], PS[:, 5, 256 * d + 64:256 * d + 130:65], ACT.Copy)
                            ins.then_inc(s["cs_read"], 1)
                            act.wait_ge(s["cs_read"], 1)
                            A(NO[:, 0:1], NO[:, 0:1], ACT.Copy).then_inc(s["out_ready"], 1)
                        else:
                            for d in range(2):
                                if not (c < 4 if d == 0 else c > 1):
                                    continue
                                k = c if d == 0 else 5 - c
                                A(S_ssd[:, d, k, :], PS[:, 4, 256 * d:256 * d + 256], ACT.Copy)
                                ins = A(S_ml[:, d, k, :], PS[:, 5, 256 * d:256 * d + 130], ACT.Copy)
                            ins.then_inc(s["cs_read"], 1)
                    for c in range(NC):
                        act.wait_ge(s["ta_mm"], NC + c + 1)
                        act.wait_ge(s["xe_ready"], NC)
                        if c > 0:
                            act.wait_ge(s["xd_ready"], c)
                        A(XT, PS[:, 2, :], ACT.Copy).then_inc(s["ta_act"], 1)
                        if 4 * c > 0:
                            act.wait_ge(s["y_mm"], 4 * c)
                        A(VA[:, :, 0:64], PS[:, 3, 0:256].rearrange("p (h n) -> p h n", h=4), ACT.Copy).then_inc(
                            s["ta_act"], 1)
                        act.wait_ge(s["ta_act"], 4 * NC)
                        for i in range(6):
                            act.wait_ge(s["bc_mm"], 6 * c + i + 1)
                            if i == 4:
                                act.wait_ge(s["y_mm"], 4 * c + 1)
                            r = (0, 8, 4, 12, 16, 20)[i]
                            for q in range(4):
                                ins = A(W[:, i % 4, q * P:(q + 1) * P], PS[:, 2 + i % 2, q * P:(q + 1) * P], ACT.Exp,
                                        bias=COLS[:, c, 1, r + q:r + q + 1])
                            ins.then_inc(s["bc_exp"], 1)
                    for k in range(NC):
                        for d in range(2):
                            b, i = units[d], 2 * k + d
                            act.wait_ge(s["rs_dve"], i + 1)
                            A(b["e1"], b["c"], ACT.Exp)
                            A(b["e2"], b["c"], ACT.Exp, scale=-1.0)
                            A(b["e3"], b["e3"], ACT.Exp)
                            A(EMID[:, 2 * d:2 * d + 2], MID[:, 2 * d:2 * d + 2], ACT.Exp).then_inc(s["rs_exp"], 1)
                        for d in range(2):
                            b, a, i = units[d], 4 * d, 2 * k + d
                            act.wait_ge(s["rw_t"], i + 1)
                            A(b["KBT"], PS[:, a, :], ACT.Copy).then_inc(s["rw_tok"], 1)
                            A(b["VT"], PS[:, a + 1, 0:256], ACT.Copy).then_inc(s["rw_tok"], 1)

                        def copies(r, q, qt=True):
                            for d in range(2):
                                b, a = units[d], 4 * d
                                act.wait_ge(s["inv_mm"], 20 * k + 2 * r + d + 1)
                                if q:
                                    ins = A(b["Q"], PS[:, a, :].rearrange("p (h t) -> p h t", h=4), ACT.Copy)
                                A(b["QT"], PS[:, a + 3, :].rearrange("p (h t) -> p h t", h=4), ACT.Copy).then_inc(
                                    s["inv_copy"], 1)
                        copies(0, True)
                        copies(1, True)
                        copies(2, False)
                        for l in range(3):
                            copies(4 + 2 * l, True)
                        for d in range(2):
                            act.wait_ge(s["rhs_mm"], 2 * k + d + 1)
                            A(units[d]["RHS"].rearrange("p (f q n) -> p q f n", f=2, q=2),
                                  PS[:, 4 * d:4 * d + 2, 0:P].rearrange("p q (f n) -> p q f n", f=2), ACT.Copy).then_inc(
                                      s["rhs_sb"], 1)
                        for d in range(2):
                            act.wait_ge(s["sa_mm"], 2 * k + d + 1)
                            A(units[d]["NSA"], PS[:, 4 * d + 2, 0:256], ACT.Copy, scale=-1.0).then_inc(s["sa_sb"], 1)
                        if k == 0:
                            for d in range(2):
                                act.wait_ge(s["rf_t"], d + 1)
                                A(lora[0:64, 256 * d:256 * d + 256], PS[0:64, 4 * d, 0:256], ACT.Copy).then_inc(
                                    s["rwo_ready"], 1)
                    act.wait_ge(s["g_src"], 1)
                    for q in range(4):
                        A(gtmp[:, 2 + q, :], U[:, XS + q, :], ACT.Square).then_inc(s["g_sq"], 1)
                    for n, (t_, s_) in enumerate(((BT_, 6), (CT_, 7), (MV, 0), (MV + 1, 1))):
                        act.wait_ge(s["g_read"], 3 + n)
                        A(gtmp[:, s_, :], U[:, t_, :], ACT.Square).then_inc(s["g_sq"], 1)
                    for n, s_ in enumerate((2, 4, 6, 7, 0, 1)):
                        act.wait_ge(s["g_mm"], 7 + n)
                        b = 2 * ((6 + n) % 4)
                        A(gtmp[:, s_, :].rearrange("p (a t) -> p a t", a=2), PS[:, b:b + 2, 0:HALF], ACT.Sqrt,
                              bias=eps[:, 2:3], scale=1.0 / 256 if n < 2 else 1.0 / 64).then_inc(s["g_std"], 1)
                    for k, t_ in enumerate(YTILES):
                        act.wait_ge(s["y_done"], k + 1)
                        A(rp_r[:, k, :], U[:, t_, :], ACT.Copy).then_inc(s["y_hi"], 1)
                    norm(1, 24)

                    def u_split(t_):
                        act.wait_ge(s["ffn_ready"], t_ + 1)
                        A(u_high_r[t_], U[:, t_, :], ACT.Copy).then_inc(s["u_hi"], 1)

                    for j in range(FT):
                        act.wait_ge(s["ffn_mm"], 2 * j + 1)
                        if j > 1:
                            act.wait_ge(s["ffn_ready"], j - 1)
                        b = 4 * (j % 2)
                        A(tmp[:, j % 2, :].rearrange("p (a t) -> p a t", a=2), PS[:, b:b + 2, 0:HALF],
                          ACT.Silu).then_inc(s["ffn_silu"], 1)
                        split(Q_FFN + 2 * j + 2)
                        if 0 < j <= U_EARLY:
                            u_split(j - 1)
                        split(Q_FFN + 2 * j + 3)
                    act.wait_ge(s["ffn_mm"], 2 * FT)
                    for t_ in range(U_EARLY, FT):
                        u_split(t_)
                    for i in range(3 * KT):
                        split(Q_W2 + 2 + i)

                @block.vector
                def _(dve):
                    v = nc.vector
                    step = counter()

                    def norm(i):
                        dve.wait_ge(s["std_ready"], i + 1)
                        v.reciprocal(rs, rs).then_inc(s["dve_step"], 1)
                        dve.wait_ge(s["dve_step"], step())
                        for k in range(KT):
                            v.tensor_tensor(h[:, k, :], xv[:, k, :], rs, ALU.mult).then_inc(s["xr_ready"], 1)

                    def low_parts(i):
                        for k in range(KT):
                            dve.wait_ge(s["h_hi"], KT * i + k + 1)
                            v.tensor_tensor(h_r[:, k, :], h[:, k, :], h_high_r[:, k, :].bitcast(F32),
                                            ALU.subtract).then_inc(s["h_lo"], 1)

                    norm(0)
                    dve.wait_ge(s["par_cols"], 1)
                    mu = PC[:, MU0:MU0 + 8]
                    v.tensor_scalar(OM[:, :], mu, -1.0, 1.0, ALU.mult, ALU.add).then_inc(s["dve_step"], 1)
                    dve.wait_ge(s["dve_step"], step())
                    v.tensor_tensor(MUJ[:, :].rearrange("p (m j) -> p m j", j=4),
                                         mu.unsqueeze(2).broadcast_to((P, 8, 4)),
                                         PAR[:, 2:6].unsqueeze(1).broadcast_to((P, 8, 4)), ALU.mult).then_inc(
                                             s["dve_step"], 1)
                    dve.wait_ge(s["dve_step"], step())
                    v.tensor_tensor(MU2[:, :].rearrange("p (m j) -> p m j", j=2),
                                         mu.unsqueeze(2).broadcast_to((P, 8, 2)),
                                         PAR[:, 0:2].unsqueeze(1).broadcast_to((P, 8, 2)), ALU.mult).then_inc(
                                             s["dve_step"], 1)
                    dve.wait_ge(s["dve_step"], step())
                    v.tensor_scalar(KAO[:, :], col("rwkv_k_a", 0, 2), -1.0, 1.0, ALU.mult, ALU.add).then_inc(
                        s["dve_step"], 1)
                    dve.wait_ge(s["dve_step"], step())

                    modv = MOD[:, :].rearrange("p (m g) -> p m g", g=2)

                    def modulation(m0, m1, i, nm, m):
                        dve.wait_ge(s["ada_mm"], m1)
                        v.tensor_tensor(modv[:, m0:m1, :], PS[:, 2, 2 * m0:2 * m1].rearrange("p (m g) -> p m g", g=2),
                                        col("ada_b", m0, m1 - m0).unsqueeze(2).broadcast_to((P, m1 - m0, 2)),
                                        ALU.add).then_inc(s["dve_step"], 1)
                        dve.wait_ge(s["dve_step"], step())
                        v.scalar_tensor_tensor(
                            out=GS[:, 16 * i:16 * i + 16].rearrange("p (m g) -> p m g", g=2), in0=modv[:, m:m + 8, :],
                            scalar=1.0, in1=col(nm, 0, 8).unsqueeze(2).broadcast_to((P, 8, 2)), op0=ALU.add,
                            op1=ALU.mult).then_inc(s["mod_ready"], 1)

                    modulation(0, ADA1, 0, "norm1_g", 8)
                    low_parts(0)
                    rc = [RC[RS, i:i + 1] for i in range(8)]
                    dve.wait_ge(s["row_in"], 7 * 16)
                    v.tensor_tensor(RP[RS, 4:5], rc[4], rc[5], ALU.subtract).then_inc(s["dve_step"], 1)
                    dve.wait_ge(s["dve_step"], step())
                    v.tensor_tensor(RP[RS, 5:6], RP[RS, 0:1], RP[RS, 4:5], ALU.mult).then_inc(s["rows_dve"], 1)
                    dve.wait_ge(s["rows_act"], 4)
                    v.tensor_scalar(t2, t1, 1.0, None, ALU.add).then_inc(s["dve_step"], 1)
                    dve.wait_ge(s["dve_step"], step())
                    v.tensor_scalar(RP[RS, 7:8], RP[RS, 6:7], -1.0, None, ALU.mult).then_inc(s["rows_dve"], 1)
                    dve.wait_ge(s["rows_act"], 5)
                    v.tensor_scalar(t2, t2, -1.0, 5e-8, ALU.add, ALU.max).then_inc(s["dve_step"], 1)
                    dve.wait_ge(s["dve_step"], step())
                    v.reciprocal(t2, t2).then_inc(s["dve_step"], 1)
                    dve.wait_ge(s["dve_step"], step())
                    v.tensor_tensor(t1, t1, t2, ALU.mult).then_inc(s["dve_step"], 1)
                    dve.wait_ge(s["dve_step"], step())
                    v.tensor_tensor(CF, CF, t1, ALU.mult).then_inc(s["dve_step"], 1)
                    dve.wait_ge(s["dve_step"], step())
                    v.scalar_tensor_tensor(out=SP, in0=zr, scalar=0.0, in1=CF, op0=ALU.max, op1=ALU.add).then_inc(
                        s["dve_step"], 1)
                    dve.wait_ge(s["dve_step"], step())
                    v.tensor_scalar(LOG, SP, RP[RS, 7:8], None, ALU.mult).then_inc(s["dve_step"], 1)
                    dve.wait_ge(s["dve_step"], step())
                    on = ones[RS, 0:P]
                    for c in range(NC):
                        v.tensor_tensor_scan(out=CF[:, ck(c)], data0=on, data1=LOG[:, ck(c)], initial=0.0,
                                             op0=ALU.mult, op1=ALU.add)
                        ins = v.tensor_tensor_scan(out=CB[:, ck(c)][:, ::-1], data0=on, data1=LOG[:, ck(c)][:, ::-1],
                                                   initial=0.0, op0=ALU.mult, op1=ALU.add)
                    ins.then_inc(s["dve_step"], 1)
                    dve.wait_ge(s["dve_step"], step())
                    v.tensor_scalar(CC, CF, rc[0], None, ALU.mult).then_inc(s["dve_step"], 1)
                    dve.wait_ge(s["dve_step"], step())
                    v.scalar_tensor_tensor(out=CC, in0=CB, scalar=rc[1], in1=CC, op0=ALU.mult, op1=ALU.add).then_inc(
                        s["dve_step"], 1)
                    dve.wait_ge(s["dve_step"], step())
                    v.tensor_scalar(KR, KR, rc[5], RP[RS, 1:2], ALU.mult, ALU.add).then_inc(s["dve_step"], 1)
                    dve.wait_ge(s["dve_step"], step())
                    v.tensor_tensor(KR, KR, CC, ALU.subtract).then_inc(s["dve_step"], 1)
                    dve.wait_ge(s["dve_step"], step())
                    v.memset(MC[:, :], 0.0)
                    v.memset(MS5[:, 4:5], 0.0)
                    v.tensor_copy(MS5[RS, 0:1], RP[RS, 3:4]).then_inc(s["dve_step"], 1)
                    dve.wait_ge(s["dve_step"], step())
                    for k in (4, 0, 1, 2, 3):
                        cf, cb = (0, 0) if k == 4 else (k + 1, 4 - k)
                        v.tensor_tensor_scan(out=MF[:, ck(cf)], data0=KR[:, ck(cf)], data1=KR[:, ck(cf)],
                                             initial=MS5[RS, k:k + 1], op0=ALU.max, op1=ALU.max)
                        v.tensor_tensor_scan(out=MB[:, ck(cb)][:, ::-1], data0=KR[:, ck(cb)][:, ::-1],
                                                  data1=KR[:, ck(cb)][:, ::-1], initial=MS5[RS, k:k + 1],
                                                  op0=ALU.max, op1=ALU.max).then_inc(s["dve_step"], 1)
                        dve.wait_ge(s["dve_step"], step())
                        ef, eb = cf * P + P - 1, cb * P
                        v.tensor_tensor(MS5[RS, 5:6], MF[:, ef:ef + 1], CF[:, ef:ef + 1], ALU.add).then_inc(
                            s["dve_step"], 1)
                        dve.wait_ge(s["dve_step"], step())
                        v.tensor_tensor(MS5[RS, 6:7], MB[:, eb:eb + 1], CB[:, eb:eb + 1], ALU.add).then_inc(
                            s["dve_step"], 1)
                        dve.wait_ge(s["dve_step"], step())
                        v.tensor_scalar(MS5[RS, 5:6], MS5[RS, 5:6], rc[2], None, ALU.mult).then_inc(s["dve_step"], 1)
                        dve.wait_ge(s["dve_step"], step())
                        dst = mfin[RS, 0:1] if k == 4 else MS5[RS, 7:8] if k == 3 else MS5[RS, k + 1:k + 2]
                        v.scalar_tensor_tensor(out=dst, in0=MS5[RS, 6:7], scalar=rc[3], in1=MS5[RS, 5:6],
                                                    op0=ALU.mult, op1=ALU.add).then_inc(s["dve_step"], 1)
                        dve.wait_ge(s["dve_step"], step())
                    v.tensor_scalar(MC[RS, 1:5], MS5[RS, 0:4], rc[2], None, ALU.mult).then_inc(s["dve_step"], 1)
                    dve.wait_ge(s["dve_step"], step())
                    v.scalar_tensor_tensor(out=MC[RS, 1:5], in0=MS5[RS, 0:4][:, ::-1], scalar=rc[3],
                                                in1=MC[RS, 1:5], op0=ALU.mult, op1=ALU.add).then_inc(s["dve_step"], 1)
                    dve.wait_ge(s["dve_step"], step())
                    v.tensor_scalar(Rr, MF, rc[6], None, ALU.mult).then_inc(s["dve_step"], 1)
                    dve.wait_ge(s["dve_step"], step())
                    v.scalar_tensor_tensor(out=Rr, in0=MB, scalar=rc[7], in1=Rr, op0=ALU.mult, op1=ALU.add).then_inc(
                        s["dve_step"], 1)
                    dve.wait_ge(s["dve_step"], step())
                    v.scalar_tensor_tensor(out=Rr, in0=CC, scalar=rc[4], in1=Rr, op0=ALU.mult, op1=ALU.add).then_inc(
                        s["dve_step"], 1)
                    dve.wait_ge(s["dve_step"], step())
                    v.tensor_scalar(RE[RS, :], Rr[:, P - 1:T:P], rc[0], None, ALU.mult).then_inc(s["dve_step"], 1)
                    dve.wait_ge(s["dve_step"], step())
                    v.scalar_tensor_tensor(out=RE[RS, :], in0=Rr[:, 0:T:P], scalar=rc[1], in1=RE[RS, :],
                                                op0=ALU.mult, op1=ALU.add).then_inc(s["dve_step"], 1)
                    dve.wait_ge(s["dve_step"], step())
                    v.tensor_tensor(EM, Rr, CC, ALU.subtract).then_inc(s["rows_dve"], 1)

                    for j, m in enumerate(POST):
                        dve.wait_ge(s["tmp_act"], j + 1)
                        pp = slice(0, 64) if m == MISC else slice(0, P)
                        o, u = tmp[pp, j % 2, :], U[pp, m, :]

                        def madd(out, in_, s):
                            return v.scalar_tensor_tensor(out=out, in0=in_, scalar=s, in1=out, op0=ALU.mult,
                                                          op1=ALU.add)
                        if m in CONV:
                            nm, i, w_ = ("ssd", m - XS, 6) if m < MISC else ("mlstm", m - MQ, 4)
                            w0, w2 = col(nm + "_conv_w", i), col(nm + "_conv_w", 2 * w_ + i)
                            madd(o[:, 1:CTX], u[:, 0:CTX - 1], w0)
                            madd(o[:, CTX + 1:T], u[:, CTX:T - 1], w0).then_inc(s["dve_step"], 1)
                            dve.wait_ge(s["dve_step"], step())
                            madd(o[:, 0:CTX - 1], u[:, 1:CTX], w2).then_inc(s["dve_step"], 1)
                            dve.wait_ge(s["dve_step"], step())
                            madd(o[:, CTX:T - 1], u[:, CTX + 1:T], w2).then_inc(s["tmp_dve"], 1)
                        else:
                            i = SHIFTED[m]
                            s2 = [MU2[pp, 2 * i + q:2 * i + q + 1] for q in range(2)]
                            s4 = [MUJ[pp, 4 * i + q:4 * i + q + 1] for q in range(4)]
                            ol = o[:, CTX:T].rearrange("p (r w) -> p r w", w=GRID_W)
                            ul = u[:, CTX:T].rearrange("p (r w) -> p r w", w=GRID_W)
                            madd(o[:, 1:CTX], u[:, 0:CTX - 1], s2[0])
                            madd(ol[:, :, 1:], ul[:, :, :GRID_W - 1], s4[0]).then_inc(s["dve_step"], 1)
                            dve.wait_ge(s["dve_step"], step())
                            madd(o[:, 0:CTX - 1], u[:, 1:CTX], s2[1])
                            madd(ol[:, :, :GRID_W - 1], ul[:, :, 1:], s4[1]).then_inc(s["dve_step"], 1)
                            dve.wait_ge(s["dve_step"], step())
                            madd(ol[:, 1:, :], ul[:, :-1, :], s4[2]).then_inc(s["dve_step"], 1)
                            dve.wait_ge(s["dve_step"], step())
                            madd(ol[:, :-1, :], ul[:, 1:, :], s4[3]).then_inc(s["tmp_dve"], 1)
                    modulation(ADA1, 48, 1, "norm2_g", 32)
                    dve.wait_ge(s["feat_ready"], len(POST))
                    for f in range(2):
                        v.tensor_scalar(U[:, MK + f, :], U[:, MK + f, :], HD ** -0.5, None, ALU.mult).then_inc(
                            s["k_scaled"], 1)
                    dve.wait_ge(s["pair_read"], NU + 2)
                    v.reciprocal(tmp, tmp).then_inc(s["dve_step"], 1)
                    dve.wait_ge(s["dve_step"], step())
                    v.tensor_tensor(KK, KK, tmp, ALU.mult).then_inc(s["dve_step"], 1)
                    dve.wait_ge(s["dve_step"], step())
                    dve.wait_ge(s["pair_read"], NU + 10)
                    for d in range(2):
                        v.tensor_scalar(LW[d], LW[d], -ISQE, None, ALU.mult)
                        for f in range(2):
                            ins = v.tensor_scalar(KD[d][:, f, :], BB[d][:, f, :], col("rwkv_k_a", f), KAO[:, f:f + 1],
                                                  ALU.mult, ALU.add)
                        ins.then_inc(s["dve_step"], 1)
                        dve.wait_ge(s["dve_step"], step())
                        v.tensor_tensor(KD[d], KD[d], U[:, RK_:RK_ + 2, :], ALU.mult)
                        ins = v.tensor_tensor(BB[d], BB[d], KK, ALU.mult)
                    ins.then_inc(s["rw_ready"], 1)
                    dve.wait_ge(s["rw_ready"], 1)
                    dve.wait_ge(s["rows_act"], 6)
                    v.tensor_tensor(DD[RS, :].rearrange("p (r c) -> p r c", c=5),
                                        ident[RS, R0:R0 + NR].unsqueeze(2).broadcast_to((NR, NR, 5)),
                                        DEC[RS, :].unsqueeze(1).broadcast_to((NR, NR, 5)), ALU.mult).then_inc(
                                            s["dec_diag"], 1)
                    v.memset(VA[:, :, 64:65], 1.0).then_inc(s["dve_step"], 1)
                    dve.wait_ge(s["dve_step"], step())

                    def heads(ap, n):
                        return ap.rearrange("p (h n) -> p h n", h=n)

                    def wide(ap, n):
                        return ap.unsqueeze(2).broadcast_to((P, ap.shape[1], n))

                    for c in range(NC):
                        dve.wait_ge(s["ta_act"], 4 * c + 4)
                        v.tensor_tensor(SPTE, COLS[:, c, 0, 0:16], COLS[:, c, 3, 0:16], ALU.mult).then_inc(
                            s["dve_step"], 1)
                        dve.wait_ge(s["dve_step"], step())
                        if c > 0:
                            dve.wait_ge(s["cs_mm"], c)
                        for d in range(2):
                            v.tensor_tensor(heads(XE[:, d, :], 8), heads(XT, 8), wide(SPTE[:, 8 * d:8 * d + 8], 64),
                                            ALU.mult)
                            r = 16 + 4 * d
                            ins = v.tensor_tensor(heads(VE[:, d, :], 4), VA, wide(COLS[:, c, 3, r:r + 4], 65),
                                                  ALU.mult)
                        ins.then_inc(s["xe_ready"], 1)
                    dve.wait_ge(s["cs_read"], NC)
                    dve.wait_ge(s["dec_read"], 1)
                    dve.wait_ge(s["state_in"], 16 * 14)
                    for k in range(1, 4):
                        for d in range(2):
                            c = k if d == 0 else 5 - k
                            dec = DECB[:, 20 * d + c:20 * d + c + 16:5]
                            v.tensor_tensor(heads(XE[:, 0, 0:256], 4), heads(S_ssd[:, d, k - 1, :], 4), wide(dec, 64),
                                                 ALU.mult).then_inc(s["dve_step"], 1)
                            dve.wait_ge(s["dve_step"], step())
                            v.tensor_tensor(S_ssd[:, d, k, :], S_ssd[:, d, k, :], XE[:, 0, 0:256], ALU.add).then_inc(
                                s["dve_step"], 1)
                            dve.wait_ge(s["dve_step"], step())
                            dec = DECB[:, 40 + 10 * d + c:40 + 10 * d + c + 6:5]
                            v.tensor_tensor(heads(XE[:, 0, 0:130], 2), heads(S_ml[:, d, k - 1, :], 2), wide(dec, 65),
                                                 ALU.mult).then_inc(s["dve_step"], 1)
                            dve.wait_ge(s["dve_step"], step())
                            ins = v.tensor_tensor(S_ml[:, d, k, :], S_ml[:, d, k, :], XE[:, 0, 0:130], ALU.add)
                            if (k, d) != (3, 1):
                                ins.then_inc(s["dve_step"], 1)
                                dve.wait_ge(s["dve_step"], step())
                    ins.then_inc(s["states_ready"], 1)
                    dve.wait_ge(s["states_ready"], 1)
                    MI = [PP[:, 256 * d + P:256 * d + 2 * P] for d in range(2)]

                    def over(mask, n):
                        return mask.unsqueeze(1).broadcast_to((P, n, mask.shape[1]))

                    for c in range(NC):
                        dve.wait_ge(s["ta_act"], 4 * NC + 2 * c + 1)
                        if 4 * c > 0:
                            dve.wait_ge(s["y_mm"], 4 * c)
                        for d in range(2):
                            ins = v.tensor_tensor(heads(XE[:, d, :], 8), heads(XT, 8),
                                                  wide(COLS[:, c, 0, 8 * d:8 * d + 8], 64), ALU.mult)
                        ins.then_inc(s["xd_ready"], 1)
                        dve.wait_ge(s["qk_mm"], c + 1)
                        for i in range(6):
                            dve.wait_ge(s["bc_exp"], 6 * c + i + 1)
                            if i < 4:
                                w_ = heads(W[:, i % 4, :], 4)
                                m_ = over(PS[:, i // 2, 0:P], 4)
                            else:
                                w_ = W[:, i % 4, :].rearrange("p (f q n) -> p q f n", f=2, q=2)
                                m_ = PS[:, 0:2, P:3 * P].rearrange("p q (f n) -> p q f n", f=2)
                            v.tensor_tensor(w_, w_, m_, ALU.mult).then_inc(s["w_ready"], 1)
                        dve.wait_ge(s["y_mm"], 4 * c + 2)
                        if c == 0:
                            dve.wait_ge(s["stored"], 7 * 16)
                            v.tensor_copy(YS, PS[:, 4, :]).then_inc(s["y_comb"], 1)
                        else:
                            for d, dst in enumerate((YS, YT)):
                                ec = COLS[:, c, 2, 8 * d:8 * d + 8].rearrange("p (g h) -> p g h", g=2)
                                v.tensor_tensor(
                                    dst.rearrange("p (g h n) -> p g h n", g=2, h=4),
                                    PS[:, 5:7, 256 * d:256 * d + 256].rearrange("p g (h n) -> p g h n", h=4),
                                    ec.unsqueeze(3).broadcast_to((P, 2, 4, 64)), ALU.mult).then_inc(s["dve_step"], 1)
                                dve.wait_ge(s["dve_step"], step())
                            v.tensor_tensor(YS, YS, YT, ALU.add).then_inc(s["dve_step"], 1)
                            dve.wait_ge(s["dve_step"], step())
                            v.tensor_tensor(YS, YS, PS[:, 4, :], ALU.add).then_inc(s["y_comb"], 1)
                        for d in range(2):
                            dve.wait_ge(s["y_mm"], 4 * c + 3 + d)
                            dve.wait_ge(s["y_comb"], 3 * c + 1 + d)
                            num, inter = (7, 0) if d == 0 else (2, 5)
                            nps = heads(PS[:, num, 0:260], 4)
                            r = 16 + 4 * d
                            if c == 0:
                                v.tensor_copy(NM, nps).then_inc(s["dve_step"], 1)
                                dve.wait_ge(s["dve_step"], step())
                            else:
                                ec = COLS[:, c, 2, r:r + 4].rearrange("p (f q) -> p q f", q=2)
                                v.tensor_tensor(
                                    NM.rearrange("p (f q) n -> p q f n", q=2),
                                    PS[:, inter:inter + 2, 0:130].rearrange("p q (f n) -> p q f n", f=2),
                                    ec.unsqueeze(3).broadcast_to((P, 2, 2, 65)), ALU.mult).then_inc(s["dve_step"], 1)
                                dve.wait_ge(s["dve_step"], step())
                                v.tensor_tensor(NM, NM, nps, ALU.add).then_inc(s["dve_step"], 1)
                                dve.wait_ge(s["dve_step"], step())
                            dn = NM[:, :, 64]
                            v.scalar_tensor_tensor(out=DN[:, 0:4], in0=dn, scalar=-1.0, in1=dn, op0=ALU.mult,
                                                        op1=ALU.max).then_inc(s["dve_step"], 1)
                            dve.wait_ge(s["dve_step"], step())
                            v.tensor_tensor(DN[:, 0:4], DN[:, 0:4], COLS[:, c, 4, r:r + 4], ALU.max).then_inc(
                                s["dve_step"], 1)
                            dve.wait_ge(s["dve_step"], step())
                            v.reciprocal(DN[:, 4:8], DN[:, 0:4]).then_inc(s["dve_step"], 1)
                            dve.wait_ge(s["dve_step"], step())
                            y_ = v.tensor_tensor(heads((YM, YM2)[d], 4), NM[:, :, 0:64], wide(DN[:, 4:8], 64), ALU.mult)
                            if d == 0:
                                y_.then_inc(s["y_comb"], 1)
                            else:
                                y_.then_inc(s["dve_step"], 1)
                                dve.wait_ge(s["dve_step"], step())
                                v.tensor_tensor(YM, YM, YM2, ALU.add).then_inc(s["y_comb"], 1)
                        dve.wait_ge(s["yt_mm"], c + 1)
                        for q in range(4):
                            y_ = U[:, XS + q, ck(c)]
                            v.scalar_tensor_tensor(out=y_, in0=y_, scalar=dcol[:, q:q + 1],
                                                   in1=PS[:, 4, q * P:(q + 1) * P], op0=ALU.mult, op1=ALU.add)
                        v.tensor_copy(U[:, MV:MV + 2, ck(c)], heads(PS[:, 6, 0:256], 2)).then_inc(s["yt_read"], 1)
                    v.memset(U[:, BT_:BT_ + 2, :], 0.0).then_inc(s["dve_step"], 1)
                    dve.wait_ge(s["dve_step"], step())
                    for k in range(NC):
                        for d in range(2):
                            b, i = units[d], 2 * k + d
                            c = ck(0 if k == 0 else (k if d == 0 else 5 - k))
                            for f in range(2):
                                o, s_ = b["c"][:, f, :], LW[d][:, f, c]
                                if d:
                                    o, s_ = o[:, ::-1], s_[:, ::-1]
                                ins = v.tensor_tensor_scan(out=o, data0=ones[:, :], data1=s_, initial=0.0,
                                                           op0=ALU.mult, op1=ALU.add)
                            ins.then_inc(s["dve_step"], 1)
                            dve.wait_ge(s["dve_step"], step())
                            v.tensor_copy(MID[:, 2 * d:2 * d + 2], b["c"][:, :, 64]).then_inc(s["dve_step"], 1)
                            dve.wait_ge(s["dve_step"], step())
                            for f in range(2):
                                ins = v.tensor_scalar(b["c"][:, f, :], b["c"][:, f, :],
                                                      MID[:, 2 * d + f:2 * d + f + 1], None, ALU.subtract)
                            ins.then_inc(s["dve_step"], 1)
                            dve.wait_ge(s["dve_step"], step())
                            v.tensor_tensor(b["e3"], b["c"], LW[d][:, :, c], ALU.subtract).then_inc(s["rs_dve"], 1)
                        for d in range(2):
                            b, i = units[d], 2 * k + d
                            c = ck(0 if k == 0 else (k if d == 0 else 5 - k))
                            dve.wait_ge(s["rs_exp"], i + 1)
                            if i - 1 > 0:
                                dve.wait_ge(s["yr_mm"], i - 1)
                            v.tensor_tensor(b["RK"][:, :, 1, :], U[:, RR_:RR_ + 2, c], b["e1"], ALU.mult)
                            v.tensor_tensor(b["RK"][:, :, 0, :], KK[:, :, c], b["e3"], ALU.mult)
                            v.tensor_tensor(b["KB"][:, :, 0, :], KD[d][:, :, c], b["e2"], ALU.mult)
                            ins = v.tensor_tensor(b["KB"][:, :, 1, :], BB[d][:, :, c], b["e2"], ALU.mult)
                            if k:
                                ins = v.tensor_tensor(b["Sp"], b["S"], wide(EMID[:, 2 * d:2 * d + 2], 64), ALU.mult)
                            ins.then_inc(s["rw_feat"], 1)
                        for d in range(2):
                            b, a, i = units[d], 4 * d, 2 * k + d
                            dve.wait_ge(s["rw_prod"], i + 1)
                            for hb in range(2):
                                ps = PS[:, a + 2 + hb, :].rearrange("p (h w t) -> p h w t", h=2, w=2)
                                v.tensor_tensor(b["Q"][:, hb:4:2, :], ps[:, :, 0, :],
                                                over(M16[:, d * P:(d + 1) * P], 2), ALU.mult)
                                ins = v.tensor_tensor(b["RBT"][:, hb:4:2, :], ps[:, :, 1, :],
                                                      over(MI[d], 2), ALU.mult)
                            ins.then_inc(s["rw_masked"], 1)
                        dve.wait_ge(s["rw_masked"], 2 * k + 2)
                        for d in range(2):
                            b, a, i = units[d], 4 * d, 2 * k + d
                            dve.wait_ge(s["rw_prod2"], 2 * i + 1)
                            for hb in range(2):
                                ins = v.tensor_tensor(b["PT"][:, hb:4:2, :], heads(PS[:, a + hb, 0:256], 2),
                                                      over(NP[:, 256 * (1 - d):256 * (1 - d) + P], 2), ALU.mult)
                            ins.then_inc(s["dve_step"], 1)
                            dve.wait_ge(s["dve_step"], step())
                            v.tensor_tensor(b["QT"], b["PT"], over(BLK[:, :], 4), ALU.mult)
                            v.tensor_tensor(b["X"], b["Q"], over(ident[:, :], 4), ALU.add)
                            dve.wait_ge(s["rw_prod2"], 2 * i + 2)
                            for hb in range(2):
                                ps = PS[:, a + 2 + hb, :].rearrange("p (h w t) -> p h w t", h=2, w=2)
                                v.tensor_tensor(b["BTm"][:, hb:4:2, :], ps[:, :, 0, :],
                                                over(PP[:, 256 * d:256 * d + P], 2), ALU.mult)
                                ins = v.tensor_tensor(b["RKT"][:, hb:4:2, :], ps[:, :, 1, :],
                                                      over(MI[d], 2), ALU.mult)
                            ins.then_inc(s["rw_masked2"], 1)

                        def level(l):
                            for d in range(2):
                                b = units[d]
                                if l:
                                    dve.wait_ge(s["inv_mm"], 20 * k + 2 * (2 + 2 * l) + d + 1)
                                v.tensor_tensor(b["PL"], b["PT"], over(ML[:, l * P:(l + 1) * P], 4), ALU.mult).then_inc(
                                    s["pl_ready"], 1)

                        def adds(r, n):
                            for d in range(2):
                                b = units[d]
                                dve.wait_ge(s["inv_mm"], 20 * k + 2 * r + d + 1)
                                if n:
                                    dve.wait_ge(s["inv_add"], 12 * k + 2 * (n - 1) + d + 1)
                                v.tensor_tensor(b["X"], b["X"], heads(PS[:, 4 * d + 2, :], 4), ALU.add).then_inc(
                                    s["inv_add"], 1)
                        dve.wait_ge(s["rw_masked2"], 2 * k + 2)
                        level(0)
                        for r in range(3):
                            adds(1 + r, r)
                        for l in range(3):
                            if l < 2:
                                level(l + 1)
                            adds(5 + 2 * l, 3 + l)
                        for d in range(2):
                            b, a, i = units[d], 4 * d, 2 * k + d
                            c = ck(0 if k == 0 else (k if d == 0 else 5 - k))
                            dve.wait_ge(s["yr_mm"], i + 1)
                            if i > 0:
                                dve.wait_ge(s["yr_read"], i)
                            v.tensor_tensor(U[:, BT_:BT_ + 2, c], U[:, BT_:BT_ + 2, c],
                                                heads(PS[:, a + 3, 0:256], 2), ALU.add).then_inc(s["yr_read"], 1)
                            if k == 4:
                                continue
                            dve.wait_ge(s["st_mm"], i + 1)
                            last = b["e1"][:, :, P - 1 if d == 0 else 0]
                            st = heads(PS[:, a + 1, 0:128], 2)
                            if k == 0:
                                sf = heads(b["s"].rearrange("p f t -> p (f t)")[:, 0:128], 2)
                                v.tensor_tensor(sf, st, wide(last, 64), ALU.mult).then_inc(s["rf_ready"], 1)
                            else:
                                v.tensor_tensor(b["S"], b["Sp"], st, ALU.add).then_inc(s["dve_step"], 1)
                                dve.wait_ge(s["dve_step"], step())
                                v.tensor_tensor(b["S"], b["S"], wide(last, 64), ALU.mult).then_inc(s["dve_step"], 1)
                                dve.wait_ge(s["dve_step"], step())
                    dve.wait_ge(s["pair_read"], NU + 12)
                    v.tensor_tensor(U[:, XS:XS + 4, :], U[:, XS:XS + 4, :], U[:, Z:Z + 4, :], ALU.mult).then_inc(
                        s["g_src"], 1)
                    v.tensor_tensor(gtmp[:, 0:2, :], KD[0], KD[1], ALU.add).then_inc(s["dve_step"], 1)
                    dve.wait_ge(s["dve_step"], step())
                    for f in range(2):
                        ins = v.scalar_tensor_tensor(out=gtmp[:, f, :], in0=gtmp[:, f, :], scalar=col("rwkv_r_k", f),
                                                     in1=U[:, RR_ + f, :], op0=ALU.mult, op1=ALU.mult)
                    ins.then_inc(s["g_src"], 1)

                    def pair(ap):
                        return ap.rearrange("p (a t) -> p a t", a=2)

                    for f in range(2):
                        dve.wait_ge(s["g_mm"], f + 1)
                        v.tensor_tensor(pair(gtmp[:, 6 + f, :]), PS[:, 2 * f:2 * f + 2, 0:HALF],
                                            pair(U[:, RV_ + f, :]), ALU.mult).then_inc(s["g_read"], 1)
                    dve.wait_ge(s["g_read"], 2)
                    v.tensor_tensor(U[:, BT_:BT_ + 2, :], U[:, BT_:BT_ + 2, :], gtmp[:, 6:8, :], ALU.add).then_inc(
                        s["g_src"], 1)
                    dve.wait_ge(s["g_src"], 3)
                    for n, t_ in enumerate((BT_, CT_, MV, MV + 1)):
                        dve.wait_ge(s["g_mm"], 3 + n)
                        b_ = 2 * ((2 + n) % 4)
                        v.scalar_tensor_tensor(out=pair(U[:, t_, :]), in0=PS[:, b_:b_ + 2, 0:HALF],
                                                   scalar=-1.0 / 64, in1=pair(U[:, t_, :]), op0=ALU.mult, op1=ALU.add).then_inc(
                                                       s["g_read"], 1)
                    dve.wait_ge(s["g_read"], 6)
                    def y_low(k):
                        dve.wait_ge(s["y_hi"], k + 1)
                        y_ = U[:, YTILES[k], :]
                        v.tensor_tensor(U_r[:, YTILES[k], :], y_, rp_r[:, k, :].bitcast(F32), ALU.subtract).then_inc(s["y_lo"], 1)

                    for n, s_ in enumerate((2, 4, 6, 7, 0, 1)):
                        dve.wait_ge(s["g_std"], n + 1)
                        v.reciprocal(gtmp[:, s_, :], gtmp[:, s_, :]).then_inc(s["dve_step"], 1)
                        dve.wait_ge(s["dve_step"], step())
                        if n < 2:
                            for q in range(2):
                                y_ = U[:, XS + 2 * n + q, :]
                                v.scalar_tensor_tensor(out=y_, in0=y_, scalar=col("ssd_norm_g", 2 * n + q),
                                                       in1=gtmp[:, s_, :], op0=ALU.mult, op1=ALU.mult).then_inc(
                                    s["y_done"], 1)
                        else:
                            t_, gate, nm, f = ((BT_, LORA, "rwkv_norm_g", 0), (CT_, MISC, "rwkv_norm_g", 1),
                                               (MV, MO, "mlstm_norm_g", 0), (MV + 1, MO + 1, "mlstm_norm_g", 1))[n - 2]
                            y_ = U[:, t_, :]
                            v.scalar_tensor_tensor(out=y_, in0=y_, scalar=col(nm, f), in1=gtmp[:, s_, :],
                                                   op0=ALU.mult, op1=ALU.mult).then_inc(s["dve_step"], 1)
                            dve.wait_ge(s["dve_step"], step())
                            v.tensor_tensor(y_, y_, U[:, gate, :], ALU.mult).then_inc(s["y_done"], 1)
                        for k in ((), (0, 1), (2, 3), (4,), (5,), (6,))[n]:
                            y_low(k)
                    y_low(7)

                    def residual(b, m, row, sem):
                        g = MOD[:, 2 * (row + m):2 * (row + m) + 2]
                        v.scalar_tensor_tensor(out=xv[:, m, CTX:T], in0=PS[:, b, 0:LAT], scalar=g[:, 1:2],
                                               in1=xv[:, m, CTX:T], op0=ALU.mult, op1=ALU.add)
                        v.scalar_tensor_tensor(out=xv[:, m, 0:CTX], in0=PS[:, b + 1, 0:CTX], scalar=g[:, 0:1],
                                                   in1=xv[:, m, 0:CTX], op0=ALU.mult, op1=ALU.add).then_inc(sem, 1)
                    for m in range(KT):
                        dve.wait_ge(s["wo_mm"], m + 1)
                        residual(4 + 2 * (m % 2), m, 16, s["wo_read"])
                    dve.wait_ge(s["wo_read"], KT)
                    norm(1)
                    low_parts(1)

                    def u_low(t_):
                        dve.wait_ge(s["u_hi"], t_ + 1)
                        v.tensor_tensor(U_r[:, t_, :], U[:, t_, :], u_high_r[t_].bitcast(F32),
                                        ALU.subtract).then_inc(s["u_lo"], 1)

                    for j in range(FT):
                        dve.wait_ge(s["ffn_silu"], j + 1)
                        dve.wait_ge(s["ffn_mm"], 2 * j + 2)
                        b_ = 4 * (j % 2) + 2
                        v.tensor_tensor(pair(U[:, j, :]), pair(tmp[:, j % 2, :]), PS[:, b_:b_ + 2, 0:HALF],
                                        ALU.mult).then_inc(s["ffn_ready"], 1)
                        if 0 < j <= U_EARLY:
                            u_low(j - 1)
                    for t_ in range(U_EARLY, FT):
                        u_low(t_)
                    for m in range(KT):
                        dve.wait_ge(s["w2_mm"], 3 * m + 3)
                        residual(2 * (m % 2), m, 40, s["w2_read"])

            nc.all_engine_barrier(sems_to_clear=range(first, last_sem + 1))

        out_p = io["out_0"].rearrange("a t f -> (a t) f")
        out_s = io["out_1"].rearrange("a (c p) f -> (a c) p f", p=P)
        yo = Ub[:, 0:NC * D].rearrange("p (c f) -> p c f", c=NC)
        with nc.Block() as block:
            @block.scalar
            def _(act):
                for k in range(KT):
                    if k >= 2:
                        act.wait_ge(tail["sq_used"], k - 1)
                    nc.scalar.activation(tmp[:, k % 2, :], xv[:, k, :], ACT.Square).then_inc(tail["sq"], 1)
                act.wait_ge(tail["sq_used"], KT)
                nc.scalar.activation(rs.rearrange("p (a t) -> p a t", a=2), PS[:, 0:2, 0:HALF], ACT.Sqrt,
                                     bias=eps[:, 0:1], scale=1.0 / D).then_inc(tail["std"], 1)

            @block.tensor
            def _(pe):
                for k in range(KT):
                    pe.wait_ge(tail["sq"], k + 1)
                    for hf in range(2):
                        ins = nc.tensor.matmul(PS[:, hf, 0:HALF], ones[:, :], tmp[:, k % 2, hf * HALF:(hf + 1) * HALF],
                                               start=k == 0, stop=k == KT - 1)
                    ins.then_inc(tail["sq_used"], 1)
                pe.wait_ge(tail["y"], KT)
                for n in range(2 * NC):
                    c, hf = n // 2, n % 2
                    if n >= 6:
                        pe.wait_ge(tail["read"], n - 5)
                    for q in range(4):
                        ins = nc.tensor.transpose(PS[:, 2 + n % 6, q * P:(q + 1) * P], h[:, 4 * hf + q, ck(c)],
                                                  ident[:, :])
                    ins.then_inc(tail["mm"], 1)

            @block.vector
            def _(dve):
                dve.wait_ge(tail["std"], 1)
                nc.vector.reciprocal(rs, rs).then_inc(tail["rs"], 1)
                dve.wait_ge(tail["rs"], 1)
                for k in range(KT):
                    nc.vector.scalar_tensor_tensor(out=h[:, k, :], in0=xv[:, k, :], scalar=fg[:, k:k + 1], in1=rs,
                                                   op0=ALU.mult, op1=ALU.mult).then_inc(tail["y"], 1)
                for n in range(2 * NC):
                    c, hf = n // 2, n % 2
                    dve.wait_ge(tail["mm"], n + 1)
                    nc.vector.tensor_copy(yo[:, c, 512 * hf:512 * hf + 512], PS[:, 2 + n % 6, :]).then_inc(
                        tail["read"], 1)

            @block.sync
            def _(sp):
                for c in range(NC):
                    sp.wait_ge(tail["read"], 2 * c + 2)
                    dst = out_p if c == 0 else out_s[c - 1]
                    sp.dma_start(dst, yo[:, c, :]).then_inc(tail["stored"], 16)
                sp.wait_ge(tail["stored"], 16 * NC)


_INS = ['x_prompt', 'x_sample', 'state_ssd', 'state_rwkv', 'state_mlstm_c', 'state_mlstm_n', 'state_mlstm_m', 'c',
        'c_ctx', 'ada_w', 'ada_b', 'norm1_g', 'norm2_g', 'w_in', 'ssd_conv_w', 'ssd_conv_b', 'ssd_dt_bias',
        'ssd_a_log', 'ssd_d', 'ssd_norm_g', 'rwkv_mu', 'rwkv_w0', 'rwkv_w2', 'rwkv_a0', 'rwkv_a2', 'rwkv_g2',
        'rwkv_k_k', 'rwkv_k_a', 'rwkv_r_k', 'rwkv_norm_g', 'mlstm_conv_w', 'mlstm_conv_b', 'mlstm_i_bias',
        'mlstm_f_bias', 'mlstm_norm_g', 'w_out', 'ffn_w1', 'ffn_w3', 'ffn_w2', 'final_norm_g']
_OUTS = [(1, CTX, D), (1, LAT, D), (1, DEPTH, 2, SSD_H, HD, 64), (1, DEPTH, 2, RWKV_H, HD, HD),
         (1, DEPTH, 2, ML_H, HD, HD), (1, DEPTH, 2, ML_H, HD), (1, DEPTH, 2, ML_H)]


def kernel(**inputs):
    import numpy as np
    import concourse.bacc as bacc
    from concourse.bass_utils import run_bass_kernel_spmd

    nc = bacc.Bacc("TRN2", target_bir_lowering=False, num_devices=1)
    arrays, io = {}, {}
    for name in _INS:
        a = np.ascontiguousarray(inputs[name])
        arrays["in_" + name] = a
        io[name] = nc.dram_tensor("in_" + name, a.shape, mybir.dt.from_np(a.dtype), kind="ExternalInput").ap()
    for i, shape in enumerate(_OUTS):
        io["out_%d" % i] = nc.dram_tensor("out_%d" % i, shape, F32, kind="ExternalOutput").ap()
    build(nc, io)
    r = run_bass_kernel_spmd(nc, [arrays], core_ids=[0])
    return tuple(r.results[0]["out_%d" % i] for i in range(len(_OUTS)))
```

```python
from contextlib import ExitStack

import concourse.bass as bass
from concourse import mybir

F32 = mybir.dt.float32
F32R = mybir.dt.float32r
BF16 = mybir.dt.bfloat16
ALU = mybir.AluOpType
ACT = mybir.ActivationFunctionType
AX = mybir.AxisListType

P = 128
D = 1024
DEPTH = 2
CTX, LAT, GRID_W = 128, 512, 64
T = CTX + LAT
NC = T // P
HALF = T // 2
KT = D // P
HD = 64
D_FF = ((8 * D + 3 * 256 - 1) // (3 * 256)) * 256
FT = D_FF // P
SSD_H, RWKV_H, ML_H = 8, 4, 4
SSD_COLS = 2 * 512 + 2 * 128 + 2 * SSD_H
RWKV_COLS = 3 * 256 + 64 + 64 + 64
C_DT = 1280
C_RW = SSD_COLS
C_ML = SSD_COLS + RWKV_COLS
C_GATE = C_ML + 1024
MINUS = -2.0 ** 100
ISQE = 0.6065306597126334

Z, XS, BT_, CT_, RR_, RK_, RV_, LORA, MISC, MQ, MK, MV, MO = 0, 4, 8, 9, 10, 12, 14, 16, 17, 18, 20, 22, 24
NU = 26
U_COL = {m: 128 * m for m in range(10)}
U_COL.update({10 + i: C_RW + 128 * i for i in range(7)})
U_COL.update({18 + i: C_ML + 128 * i for i in range(8)})
ORDER = [MISC] + list(range(4, 10)) + list(range(18, 24)) + list(range(10, 17)) + [24, 25] + list(range(0, 4))
CONV = list(range(4, 10)) + list(range(18, 22))
SHIFT = list(range(10, 18))

PROWS = {}
_at = 0
for _name, _rows in (("ada_b", 48), ("norm1_g", 8), ("norm2_g", 8), ("ssd_conv_w", 18), ("ssd_conv_b", 6),
                     ("mlstm_conv_w", 12), ("mlstm_conv_b", 4), ("ssd_norm_g", 4), ("rwkv_norm_g", 2),
                     ("mlstm_norm_g", 2), ("rwkv_k_k", 2), ("rwkv_k_a", 2), ("rwkv_r_k", 2),
                     ("rwkv_w0", 4), ("rwkv_a0", 4)):
    PROWS[_name] = (_at, _rows)
    _at += _rows
NPROW = _at
MU0 = P

R0, NR = 64, 24
RS = slice(R0, R0 + NR)

RING = 4
NSEM = ["w%d" % i for i in range(RING + 2)] + [
    "gated", "bonus", "g_rec", "num_read", "ex_zero", "ex_hi", "ex_lo", "pool_step", "r_hi", "r_lo", "gaps", "mod_mid",
    "par_in", "row_in", "lora_in", "state_in",
    "split_hi", "split_lo", "h_hi", "h_lo", "y_done", "y_hi", "y_lo", "u_hi", "u_lo",
    "par_t", "par_cols", "ada_mm", "mod_ready", "sq_ready", "sq_used", "std_ready", "xr_ready", "h_ready",
    "pair_mm", "pair_read", "tmp_act", "tmp_dve", "feat_ready", "k_scaled",
    "rows_act", "rows_dve", "kk_sq", "lora_x", "rw_ready",
    "si_t", "si_ready", "ta_mm", "ta_act", "xe_ready", "cs_mm", "cs_read", "states_ready",
    "out_ready", "dec_mm", "dec_diag", "dec_read",
    "bc_mm", "bc_exp", "w_ready", "qk_mm", "xd_ready", "y_mm", "y_comb", "yt_mm", "yt_read",
    "rw_feat", "rw_t", "rw_tok", "rw_prod", "rw_prod2", "rw_masked", "rw_masked2", "pl_ready",
    "inv_mm", "inv_copy", "inv_add", "rhs_mm", "rhs_sb",
    "sa_mm", "sa_sb", "yr_mm", "yr_read", "st_mm", "rs_exp", "rs_dve",
    "g_src", "g_sq", "g_mm", "g_read", "g_std", "wo_mm", "wo_read", "ffn_mm", "ffn_silu", "ffn_ready",
    "w2_mm", "w2_read", "rf_ready", "rf_t", "rwo_ready", "act_step", "dve_step", "stored", "stored2",
]


def build(nc, io):
    with ExitStack() as ctx:
        def sb(name, n):
            return ctx.enter_context(nc.sbuf_tensor(name, [P, n], F32))

        s = {n: ctx.enter_context(nc.semaphore(n)) for n in NSEM}
        ring_in = [s[n] for n in NSEM[:RING + 2]]
        first, last_sem = ring_in[0].num, s[NSEM[-1]].num
        assert last_sem - first == len(NSEM) - 1
        setup = {n: ctx.enter_context(nc.semaphore("s_" + n)) for n in
                 ("pool", "in", "cs", "mm", "read", "dve")}
        tail = {n: ctx.enter_context(nc.semaphore("t_" + n)) for n in
                ("sq", "sq_used", "std", "rs", "y", "mm", "read", "stored")}

        PS = ctx.enter_context(nc.psum_tensor("PS", [P, 8, 512], F32))
        x = sb("x", KT * T)
        whi = ctx.enter_context(nc.sbuf_tensor("whi", [P, 2 * KT * P], F32R))
        shared = (("U", NU * T), ("ring", RING * KT * P), ("rwp", 7 * 2 * T), ("arena", 12160))
        with ExitStack() as first_names:
            Ub, ring, rwp, arena = [first_names.enter_context(nc.sbuf_tensor(name, [P, n], F32))
                                    for name, n in shared]
        Ur, ringr, rwpr, arenar = [ctx.enter_context(nc.sbuf_tensor(name + "_r", [P, n], F32R)) for name, n in shared]
        ident, SPREAD, BO, BLK = sb("ident", P), sb("SPREAD", P), sb("BO", P), sb("BLK", P)
        ML = sb("ML", 3 * P)
        NP, PP = sb("NP", 4 * P), sb("PP", 4 * P)
        PC = sb("PC", P + 8)
        MOD, GS = sb("MOD", 96), sb("GS", 32)
        cT, fg = sb("cT", 16), sb("fg", 8)
        OM, MUJ, MU2, PAR = sb("OM", 8), sb("MUJ", 32), sb("MU2", 16), sb("PAR", 6)
        KAO, dcol, RP, RC = sb("KAO", 2), sb("dcol", 4), sb("RP", 8), sb("RC", 8)
        lora = sb("lora", 512)
        SR = sb("SR", 512)
        DEC, DD, DECB = sb("DEC", 5), sb("DD", 120), sb("DECB", 60)
        eps, LAST = sb("eps", 4), sb("LAST", 4)
        onesr = ctx.enter_context(nc.sbuf_tensor("ones", [P, P], F32R))
        ones = onesr[:, :].bitcast(F32)
        MS5, MC, RE, mfin = sb("MS5", 8), sb("MC", 5), sb("RE", 5), sb("mfin", 4)
        NO, MID, EMID, M16 = sb("NO", 4), sb("MID", 4), sb("EMID", 4), sb("M16", 2 * P)

        identb = ctx.enter_context(nc.sbuf_tensor("identb", [P, P], BF16))
        NEG = ctx.enter_context(nc.sbuf_tensor("NEG", [P, 2 * P], BF16))

        xv = x[:, :].rearrange("p (k t) -> p k t", t=T)
        U = Ub[:, :].rearrange("p (k t) -> p k t", t=T)
        rings = ring[:, :].rearrange("p (r k n) -> p r k n", r=RING, k=KT)
        U_r = Ur[:, :].rearrange("p (k t) -> p k t", t=T)
        rings_r = ringr[:, :].rearrange("p (r k n) -> p r k n", r=RING, k=KT)
        rp_r = rwpr[:, :].rearrange("p (k t) -> p k t", t=T)
        h_r = arenar[:, 0:KT * T].rearrange("p (k t) -> p k t", t=T)
        ada_slots = rwp[:, 8 * T:8 * T + 2 * KT * P].rearrange("p (r k n) -> p r k n", r=2, k=KT)
        whis = whi[:, :].rearrange("p (r k n) -> p r k n", r=2, k=KT)
        rp = rwp[:, :].rearrange("p (k t) -> p k t", t=T)
        LW = [rp[:, 2 * d:2 * d + 2, :] for d in range(2)]
        BB = [rp[:, 4 + 2 * d:6 + 2 * d, :] for d in range(2)]
        KD = [rp[:, 8 + 2 * d:10 + 2 * d, :] for d in range(2)]
        KK = rp[:, 12:14, :]

        def ar(at, n):
            return arena[:, at:at + n]

        h = ar(0, KT * T).rearrange("p (k t) -> p k t", t=T)
        rowsA = ar(5120, 3840).rearrange("p (k t) -> p k t", t=T)
        tmp = ar(8960, 1280).rearrange("p (k t) -> p k t", t=T)
        rs = ar(10240, T)
        tanx = ar(10880, T)
        sigx = ar(11520, T)
        Rr, KR, EC, TE, EM, SP = [rowsA[RS, i, :] for i in range(6)]
        zr, t1, t2, LOG, CF, CB, CC, MF, MB = [U[RS, i, :] for i in (0, 1, 2, 3, 24, 25, 14, 15, 16)]
        h_high_r = rp_r[:, 0:KT, :]
        u_high_r = ([U_r[:, i, :] for i in range(FT, NU)] + [rp_r[:, i, :] for i in range(KT, 14)] +
                    [arenar[:, i * T:(i + 1) * T] for i in range(KT, 14)] + [rp_r[:, i, :] for i in range(6)])
        assert len(u_high_r) == FT
        U_EARLY = FT - 6
        S_ssd = ar(0, 2048).rearrange("p (d k n) -> p d k n", d=2, k=4)
        S_ml = ar(2048, 1040).rearrange("p (d k n) -> p d k n", d=2, k=4)
        COLS = ar(3088, 600).rearrange("p (c k r) -> p c k r", c=NC, k=5)
        XT = ar(3688, 512)
        VA = ar(4200, 260).rearrange("p (h n) -> p h n", n=65)
        BK = ar(4460, 384)
        XE = ar(11008, 1024).rearrange("p (d n) -> p d n", d=2)
        VE = ar(8960, 520).rearrange("p (d n) -> p d n", d=2)
        SSI = [S_ssd[:, d, 1:3, :].rearrange("p k n -> p (k n)").rearrange("p (h n) -> p h n", h=4) for d in range(2)]
        MLI = [S_ssd[:, d, 3, :].rearrange("p (h n) -> p h n", h=2) for d in range(2)]
        RWI = [ar(2048 + 520 * d + 130, 256).rearrange("p (h n) -> p h n", h=2) for d in range(2)]
        SO = ar(9484, 512)
        MLO = ar(9996, 512)
        W = ar(5760, 2048).rearrange("p (w n) -> p w n", w=4)
        Rhi, Rlo = [arenar[RS, 7808 + i * T:7808 + (i + 1) * T] for i in range(2)]
        EX = whi[:, :].rearrange("p (n w q t) -> p n w q t", n=2, w=2, q=4)
        HEAD0 = (0, 8, 4, 12, 16, 20)
        scan_tmp = ar(9088, 256)
        YS, YT = ar(9472, 512), ar(9984, 512)
        NM = ar(4460, 260).rearrange("p (h n) -> p h n", n=65)
        DN = ar(4720, 24)
        SPTE = ar(4860, 16)
        YM = ar(10496, 256)
        YM2 = ar(10752, 256)
        units = []
        for d in range(2):
            o = [6080 * d]

            def take(n):
                o[0] += n
                return ar(o[0] - n, n)
            b = {}
            b["RK"] = take(512).rearrange("p (f w t) -> p f w t", f=2, w=2)
            b["KB"] = take(512).rearrange("p (f w t) -> p f w t", f=2, w=2)
            b["KBT"], b["VT"] = take(512), take(256)
            for n in ("RBT", "BTm", "RKT", "PT", "PL", "Q", "QT", "X"):
                b[n] = take(512).rearrange("p (h t) -> p h t", h=4)
            pl = b["PL"].rearrange("p h t -> p (h t)")
            b["RHS"], b["NSA"] = pl[:, 0:256], pl[:, 256:512]
            for i, n in enumerate(("c", "e1", "e2", "e3", "s")):
                b[n] = Ub[:, 18 * T + 1280 * d + 256 * i:18 * T + 1280 * d + 256 * (i + 1)].rearrange(
                    "p (f t) -> p f t", f=2)
            b["S"] = SR[:, 256 * d:256 * d + 128].rearrange("p (f i) -> p f i", f=2)
            b["Sp"] = SR[:, 256 * d + 128:256 * d + 256].rearrange("p (f i) -> p f i", f=2)
            units.append(b)
        gtmp = ar(0, 8 * T).rearrange("p (k t) -> p k t", t=T)
        SQUARES = [gtmp[:, 0, :], gtmp[:, 1, :], U[:, Z + 2, :], U[:, Z + 3, :]]

        def counter():
            n = [0]

            def step():
                n[0] += 1
                return n[0]
            return step

        def col(name, i=0, n=1):
            return PC[:, PROWS[name][0] + i:PROWS[name][0] + i + n]

        def ck(c):
            return slice(c * P, (c + 1) * P)

        def expand(eng, n, w):
            r = R0 + HEAD0[n % 6]
            return eng.tensor_tensor(
                EX[RS, n % 2, w], (Rhi, Rlo)[w][:, ck(n // 6)].bitcast(F32).unsqueeze(1).broadcast_to((NR, 4, P)),
                ident[RS, r:r + 4].unsqueeze(2).broadcast_to((NR, 4, P)), ALU.mult)

        with nc.Block() as block:
            @block.gpsimd
            def _(pool):
                g = nc.gpsimd
                step = counter()

                def sel(ap, pattern, cm, base, op, fill=0.0):
                    g.affine_select(out=ap, in_=ap, compare_op=op, fill=fill, base=base,
                                         pattern=pattern, channel_multiplier=cm).then_inc(setup["pool"], 1)
                    pool.wait_ge(setup["pool"], step())

                def blocks(ap, b):
                    g.memset(ap, 1.0).then_inc(setup["pool"], 1)
                    pool.wait_ge(setup["pool"], step())
                    v = ap.rearrange("p (k j) -> p k j", j=b)
                    sel(v, [[-b, P // b], [0, b]], 1, 0, ALU.is_ge)
                    sel(v, [[b, P // b], [0, b]], -1, b - 1, ALU.is_ge)
                g.memset(ring[:, :], 0.0).then_inc(setup["pool"], 1)
                pool.wait_ge(setup["pool"], step())
                g.memset(RP[:, :], 0.0).then_inc(setup["pool"], 1)
                pool.wait_ge(setup["pool"], step())
                g.memset(RC[:, :], 1.0).then_inc(setup["pool"], 1)
                pool.wait_ge(setup["pool"], step())
                g.memset(eps[:, 0:1], 1e-6).then_inc(setup["pool"], 1)
                pool.wait_ge(setup["pool"], step())
                g.memset(eps[:, 1:2], 1e-12).then_inc(setup["pool"], 1)
                pool.wait_ge(setup["pool"], step())
                g.memset(eps[:, 2:3], 1e-5).then_inc(setup["pool"], 1)
                pool.wait_ge(setup["pool"], step())
                g.memset(eps[:, 3:4], 1.0).then_inc(setup["pool"], 1)
                pool.wait_ge(setup["pool"], step())
                g.memset(ones[:, :], 1.0).then_inc(setup["pool"], 1)
                pool.wait_ge(setup["pool"], step())
                g.memset(ident[:, :], 0.0).then_inc(setup["pool"], 1)
                pool.wait_ge(setup["pool"], step())
                sel(ident[:, :], [[-1, P]], 1, 0, ALU.not_equal, 1.0)
                blocks(BLK[:, :], 16)
                blocks(ML[:, 0:P], 32)
                blocks(ML[:, P:2 * P], 64)
                blocks(BO[:, :], 64)
                g.tensor_tensor(ML[:, 2 * P:3 * P], ones[:, :], ML[:, P:2 * P], ALU.subtract).then_inc(setup["pool"], 1)
                pool.wait_ge(setup["pool"], step())
                g.tensor_tensor(ML[:, P:2 * P], ML[:, P:2 * P], ML[:, 0:P], ALU.subtract).then_inc(setup["pool"], 1)
                pool.wait_ge(setup["pool"], step())
                g.tensor_tensor(ML[:, 0:P], ML[:, 0:P], BLK[:, :], ALU.subtract).then_inc(setup["pool"], 1)
                pool.wait_ge(setup["pool"], step())
                for d, sg in ((0, 1), (1, -1)):
                    for M, v in ((NP, -1.0), (PP, 1.0)):
                        a = M[:, 256 * d:256 * d + P]
                        b = M[:, 256 * d + P:256 * d + 2 * P]
                        g.memset(a, v).then_inc(setup["pool"], 1)
                        pool.wait_ge(setup["pool"], step())
                        sel(a, [[sg, P]], -sg, 0, ALU.is_gt)
                        g.memset(b, 1.0).then_inc(setup["pool"], 1)
                        pool.wait_ge(setup["pool"], step())
                        sel(b, [[sg, P]], -sg, 0, ALU.is_ge)
                for c, (lo, hi) in enumerate(((0, 8), (8, 16), (16, 20), (20, 24), (0, 16), (16, 24))):
                    sel(RC[:, c:c + 1], [[0, 1]], 1, -R0 - lo, ALU.is_ge)
                    sel(RC[:, c:c + 1], [[0, 1]], -1, R0 + hi - 1, ALU.is_ge)
                g.tensor_tensor(RC[:, 0:2], RC[:, 0:2], RC[:, 2:4], ALU.add).then_inc(setup["pool"], 1)
                pool.wait_ge(setup["pool"], step())
                g.tensor_scalar(RC[:, 6:8], RC[:, 2:4], -1.0, None, ALU.mult).then_inc(setup["pool"], 1)
                pool.wait_ge(setup["pool"], step())
                g.memset(NEG[:, :], 0.0).then_inc(setup["pool"], 1)
                pool.wait_ge(setup["pool"], step())
                sel(NEG[:, 0:P], [[1, P]], -1, 0, ALU.is_ge, MINUS)
                sel(NEG[:, P:2 * P], [[-1, P]], 1, 0, ALU.is_ge, MINUS)
                g.memset(SPREAD[:, :], 0.0).then_inc(setup["pool"], 1)
                pool.wait_ge(setup["pool"], step())
                for half in range(2):
                    for q in range(4):
                        sel(SPREAD[:, 64 * half:64 * half + 64], [[0, 64]], 1, -32 * q - 16 * half, ALU.not_equal, 1.0)
                g.tensor_copy(identb[:, :], ident[:, :]).then_inc(setup["pool"], 1)
                pool.wait_ge(setup["pool"], step())
                g.memset(Ub[0:8, 2 * P:3 * P], 0.0).then_inc(setup["pool"], 1)
                pool.wait_ge(setup["pool"], step())
                for d in range(2):
                    g.tensor_tensor(M16[:, d * P:(d + 1) * P], NP[:, 256 * d:256 * d + P], BLK[:, :], ALU.mult).then_inc(
                        setup["pool"], 1)
                    pool.wait_ge(setup["pool"], step())

            @block.sync
            def _(sp):
                xi = arena[:, 0:NC * D].rearrange("p (c f) -> p c f", c=NC)
                sp.dma_start(xi[:, 0, :], io["x_prompt"].rearrange("a t f -> (a t) f")).then_inc(setup["in"], 16)
                sp.dma_start(xi[:, 1:NC, :], io["x_sample"].rearrange("a (c p) f -> p (a c) f", p=P)).then_inc(
                    setup["in"], 16)
                sp.dma_start(Ub[0:8, 0:P], io["c_ctx"].rearrange("(k p) -> k p", p=P)).then_inc(setup["in"], 16)
                sp.dma_start(Ub[8:16, 0:P], io["c"].rearrange("a (k p) -> (a k) p", p=P)).then_inc(setup["in"], 16)
                sp.dma_start(Ub[16:24, 0:P], io["final_norm_g"].rearrange("(k p) -> k p", p=P)).then_inc(
                    setup["in"], 16)

            @block.scalar
            def _(act):
                act.wait_ge(setup["in"], 80)
                nc.scalar.activation(Ub[0:16, P:2 * P], Ub[0:16, 0:P], ACT.Silu).then_inc(setup["cs"], 1)

            @block.tensor
            def _(pe):
                pe.wait_ge(setup["in"], 80)
                pe.wait_ge(setup["pool"], 10)
                n = 0
                for c in range(NC):
                    for hf in range(2):
                        if n >= 7:
                            pe.wait_ge(setup["read"], n - 6)
                        for q in range(4):
                            k = 4 * hf + q
                            ins = nc.tensor.transpose(PS[:, n % 7, q * P:(q + 1) * P],
                                                      arena[:, c * D + k * P:c * D + (k + 1) * P], ident[:, :])
                        ins.then_inc(setup["mm"], 1)
                        n += 1
                pe.wait_ge(setup["cs"], 1)
                nc.tensor.transpose(PS[:, 7, 0:16], Ub[0:16, P:2 * P], ident[0:16, 0:16])
                nc.tensor.transpose(PS[:, 7, 32:56], Ub[0:24, 0:P], ident[0:24, 0:24]).then_inc(setup["mm"], 1)

            @block.vector
            def _(dve):
                step = counter()
                for n in range(2 * NC):
                    dve.wait_ge(setup["mm"], n + 1)
                    c, hf = n // 2, n % 2
                    nc.vector.tensor_copy(xv[:, 4 * hf:4 * hf + 4, ck(c)],
                                          PS[:, n % 7, :].rearrange("p (q t) -> p q t", q=4)).then_inc(
                        setup["read"], 1)
                dve.wait_ge(setup["mm"], 2 * NC + 1)
                nc.vector.tensor_copy(cT[:, :], PS[:, 7, 0:16]).then_inc(setup["dve"], 1)
                dve.wait_ge(setup["dve"], step())
                nc.vector.tensor_copy(fg[:, :], PS[:, 7, 48:56]).then_inc(setup["dve"], 1)
                dve.wait_ge(setup["dve"], step())
                dve.wait_ge(setup["pool"], 10)
                nc.vector.tensor_reduce(PAR[:, 2:6], ident[:, :].rearrange("p (k j) -> p j k", j=4),
                                             AX.X, ALU.add).then_inc(setup["dve"], 1)
                dve.wait_ge(setup["dve"], step())
                nc.vector.tensor_tensor(PAR[:, 0:2], PAR[:, 2:4], PAR[:, 4:6], ALU.add).then_inc(setup["dve"], 1)
                dve.wait_ge(setup["dve"], step())

        ADA1 = 16
        BLOCKS = []
        for k in range(KT):
            BLOCKS += [("ada_w", k), ("ada_w", KT + k)]
            if k == KT // 2:
                BLOCKS += [("w_in", m) for m in ORDER[0:2]]
        ADA_AFTER = []
        m_ = ADA1
        for n, m in enumerate(ORDER):
            if n > 1:
                BLOCKS.append(("w_in", m))
            ADA_AFTER.append(list(range(m_, m_ + (2 if n <= 4 else 1))) if 0 < n <= 20 else [])
            m_ += len(ADA_AFTER[-1])
            BLOCKS += [("ada_w", q) for q in ADA_AFTER[-1]]
        ADA_LATE = [list(range(m_, m_ + 4))]
        for n in (1, 1, 1, 1):
            ADA_LATE.append(list(range(ADA_LATE[-1][-1] + 1, ADA_LATE[-1][-1] + 1 + n)))
        assert ADA_LATE[-1][-1] == 47
        BLOCKS += [("ada_w", q) for part in ADA_LATE for q in part]
        BLOCKS += [("w_out", m) for m in range(KT)]
        for j in range(FT):
            BLOCKS += [("ffn_w1", j), ("ffn_w3", j)]
        W2_PARTS = [(0, 8), (8, 16), (16, FT)]
        BLOCKS += [("ffn_w2", m, k0, k1) for m in range(KT) for k0, k1 in W2_PARTS]
        SLOTS = RING + 2
        arrival, used, counts, total = [], [], {}, [0] * SLOTS
        slot_of, before, last_in, n_split, n_ada = [], [], {}, 0, 0
        for n, b in enumerate(BLOCKS):
            if b[0] == "ada_w":
                slot_of.append(2 + n_ada % RING if n_ada < ADA1 else RING + n_ada % 2 if n_ada < ADA_LATE[0][0] else
                               (NU + n_ada - ADA_LATE[0][0]) % RING)
                n_ada += 1
            else:
                slot_of.append((n_split + (n_ada - ADA_LATE[0][0] if n_ada == 48 else 0)) % RING)
                n_split += 1
            before.append(last_in.get(slot_of[n]))
            last_in[slot_of[n]] = n
            total[slot_of[n]] += 16 * (6 if b == ("w_in", MISC) else 1)
            arrival.append(total[slot_of[n]])
            name = {"ada_w": "ada_mm", "w_in": "pair_mm", "w_out": "wo_mm", "ffn_w1": "ffn_mm", "ffn_w3": "ffn_mm",
                    "ffn_w2": "w2_mm"}[b[0]]
            counts[name] = counts.get(name, 0) + 1
            used.append((s[name], counts[name]))

        def slot(n):
            i = slot_of[n]
            return rings[:, i, :, :] if i < RING else ada_slots[:, i - RING, :, :]

        at_block = {b: n for n, b in enumerate(BLOCKS)}
        SPLIT = [n for n, b in enumerate(BLOCKS) if b[0] != "ada_w"]
        Q_WOUT, Q_FFN = NU, NU + KT
        Q_W2 = Q_FFN + 2 * FT

        def size(n):
            return BLOCKS[n][3] - BLOCKS[n][2] if BLOCKS[n][0] == "ffn_w2" else KT

        POST = [m for m in ORDER if m in CONV or m in SHIFT]
        YTILES = [XS, XS + 1, XS + 2, XS + 3, BT_, CT_, MV, MV + 1]
        SHIFTED = {m: i for i, m in enumerate(SHIFT)}

        with nc.Fori(0, DEPTH, 1) as lay:
            def dl(name):
                return io[name][bass.ds(lay, 1)]

            def state(name):
                return io[name][0][bass.ds(lay, 1)]

            with nc.Block() as block:
                @block.sync
                def _(sp):
                    def load(dst, src, sem):
                        sp.dma_start(dst, src, allow_slow_non_contiguous=True).then_inc(sem, 16)

                    def states_in():
                        sp.wait_ge(s["pair_mm"], NU)
                        for d in range(2):
                            a = state("state_ssd")[:, d].rearrange("a (g h) p n -> p (a h) g n", g=2)
                            for hh in range(4):
                                load(SSI[d][0:64, hh, :].rearrange("p (g n) -> p g n", g=2), a[:, hh], s["state_in"])
                            for buf, nm in ((MLI, "state_mlstm_c"), (RWI, "state_rwkv")):
                                a = state(nm)[:, d].rearrange("a h i j -> i (a h) j")
                                load(buf[d][0:64].rearrange("p f (q j) -> p (f q) j", q=2), a, s["state_in"])
                            a = state("state_mlstm_n")[:, d].rearrange("a (f q) j -> (a q j) f", q=2)
                            load(S_ml[:, d, 0, 64:130:65], a, s["state_in"])

                    def states_out():
                        sp.wait_ge(s["out_ready"], 1)
                        for d in range(2):
                            o = io["out_2"][0][bass.ds(lay, 1)][:, d].rearrange("a (f q) p n -> (a q p) f n", q=2)
                            load(o, SO[:, 256 * d:256 * d + 256].rearrange("p (f n) -> p f n", f=4), s["stored"])
                            o = io["out_4"][0][bass.ds(lay, 1)][:, d].rearrange("a h i j -> i (a h) j")
                            load(o, MLO[0:64, 256 * d:256 * d + 256].rearrange("p (h j) -> p h j", h=4), s["stored"])
                            o = io["out_5"][0][bass.ds(lay, 1)][:, d].rearrange("a (f q) j -> (a q j) f", q=2)
                            load(o, NO[:, 2 * d:2 * d + 2], s["stored"])
                        o = io["out_6"][0][bass.ds(lay, 1)].rearrange("a d (h o) -> (a d h) o", o=1)
                        load(o, mfin[R0 + 16:R0 + 24, 0:1], s["stored"])
                        sp.wait_ge(s["stored"], 7 * 16)
                        sp.wait_ge(s["rwo_ready"], 2)
                        for d in range(2):
                            o = io["out_3"][0][bass.ds(lay, 1)][:, d].rearrange("a h i j -> i (a h) j")
                            load(o, lora[0:64, 256 * d:256 * d + 256].rearrange("p (h j) -> p h j", h=4), s["stored2"])
                        sp.wait_ge(s["stored2"], 2 * 16)

                    for name, (at, n) in PROWS.items():
                        a = dl(name)
                        dims = " ".join("bcdef"[:len(a.shape) - 1])
                        a = a.rearrange("a %s -> (a %s)" % (dims, dims)).rearrange("(r c) -> r c", c=P)
                        load(Ub[at:at + n, 0:P], a, s["par_in"])
                    mu = dl("rwkv_mu").rearrange("a c -> (a c)")
                    load(Ub[0:7, 2 * P:3 * P], mu[0:7 * P].rearrange("(r c) -> r c", c=P), s["par_in"])
                    load(Ub[7:8, 2 * P:2 * P + 64], mu[7 * P:7 * P + 64].rearrange("(r c) -> r c", r=1), s["par_in"])
                    for cc, r0, r1, a in ((0, 0, 16, dl("ssd_dt_bias")), (0, 16, 24, dl("mlstm_f_bias")),
                                          (1, 16, 24, dl("mlstm_i_bias")), (2, 0, 16, dl("ssd_a_log")),
                                          (3, 16, 24, state("state_mlstm_m"))):
                        load(RP[R0 + r0:R0 + r1, cc:cc + 1], a.rearrange("a d (h o) -> (a d h) o", o=1), s["row_in"])
                    dd = dl("ssd_d").rearrange("a (t q) -> q (a t)", q=2)
                    for q in range(2):
                        load(dcol[64 * q:64 * q + 64, :], dd[q:q + 1, :].broadcast_to((64, 4)), s["row_in"])
                    load(lora[0:64, 0:256], dl("rwkv_w2").rearrange("a d r c -> (a d r) c"), s["lora_in"])
                    load(lora[64:128, 0:256], dl("rwkv_a2").rearrange("a d r c -> (a d r) c"), s["lora_in"])
                    load(lora[0:64, 256:512], dl("rwkv_g2").rearrange("a r c -> (a r) c"), s["lora_in"])
                    for n, blk in enumerate(BLOCKS):
                        if n == at_block["ada_w", ADA_LATE[0][0]] + RING:
                            states_in()
                        if n == at_block["w_out", 0] + RING:
                            states_out()
                        if before[n] is not None:
                            sem, value = used[before[n]]
                            sp.wait_ge(sem, value)
                        name, m = blk[0], blk[1]
                        w = dl(name).rearrange("a (k p) n -> p (a k) n", p=P)
                        dst = slot(n)
                        if blk == ("w_in", MISC):
                            gt = C_GATE
                            for at, n_, src in ((0, 64, C_RW + 896), (64, 16, C_DT)):
                                load(dst[:, :, at:at + n_], w[:, :, src:src + n_], ring_in[slot_of[n]])
                            for at, src in ((80, gt + 4), (112, gt)):
                                load(dst[:, :, at:at + 4], w[:, :, src:src + 4], ring_in[slot_of[n]])
                                load(dst[:, :, at + 4:at + 8], w[:, :, src + 8:src + 12], ring_in[slot_of[n]])
                        elif name == "ffn_w2":
                            k0, k1 = blk[2:]
                            load(dst[:, 0:k1 - k0, :], w[:, k0:k1, m * P:(m + 1) * P], ring_in[slot_of[n]])
                        else:
                            at = U_COL[m] if name == "w_in" else m * P
                            load(dst, w[:, :, at:at + P], ring_in[slot_of[n]])

                @block.gpsimd
                def _(pool):
                    g = nc.gpsimd
                    step = counter()

                    def heads(ap, n):
                        return ap.rearrange("p (h n) -> p h n", h=n)

                    def wide(ap, n):
                        return ap.unsqueeze(2).broadcast_to((P, ap.shape[1], n))

                    def start_state(k, d):
                        c = k if d == 0 else 5 - k
                        dec = DECB[:, 20 * d + c:20 * d + c + 16:5]
                        g.tensor_tensor(heads(scan_tmp, 4), heads(S_ssd[:, d, k - 1, :], 4), wide(dec, 64),
                                        ALU.mult).then_inc(s["pool_step"], 1)
                        pool.wait_ge(s["pool_step"], step())
                        g.tensor_tensor(S_ssd[:, d, k, :], S_ssd[:, d, k, :], scan_tmp, ALU.add).then_inc(
                            s["pool_step"], 1)
                        pool.wait_ge(s["pool_step"], step())
                        dec = DECB[:, 40 + 10 * d + c:40 + 10 * d + c + 6:5]
                        g.tensor_tensor(heads(scan_tmp[:, 0:130], 2), heads(S_ml[:, d, k - 1, :], 2), wide(dec, 65),
                                        ALU.mult).then_inc(s["pool_step"], 1)
                        pool.wait_ge(s["pool_step"], step())
                        g.tensor_tensor(S_ml[:, d, k, :], S_ml[:, d, k, :], scan_tmp[:, 0:130], ALU.add).then_inc(
                            s["states_ready"], 1)
                        pool.wait_ge(s["states_ready"], 2 * (k - 1) + d + 1)

                    def gates():
                        pool.wait_ge(s["yt_read"], NC)
                        g.tensor_tensor(U[:, XS:XS + 4, :], U[:, XS:XS + 4, :], U[:, Z:Z + 4, :], ALU.mult).then_inc(
                            s["gated"], 1)
                        pool.wait_ge(s["gated"], 1)
                        pool.wait_ge(s["rw_ready"], 1)
                        both = U[:, Z:Z + 2, :]
                        g.tensor_tensor(both, KD[0], KD[1], ALU.add).then_inc(s["pool_step"], 1)
                        pool.wait_ge(s["pool_step"], step())
                        g.tensor_tensor(both, both, U[:, RR_:RR_ + 2, :], ALU.mult).then_inc(s["pool_step"], 1)
                        pool.wait_ge(s["pool_step"], step())
                        for f in range(2):
                            ins = g.tensor_scalar(U[:, Z + f, :], U[:, Z + f, :], col("rwkv_r_k", f), None, ALU.mult)
                        ins.then_inc(s["bonus"], 1)

                    def scan_rows():
                        pool.wait_ge(s["ta_mm"], NC)
                        pool.wait_ge(s["cs_mm"], NC)
                        g.memset(whi[:, :].bitcast(F32), 0.0).then_inc(s["ex_zero"], 1)
                        pool.wait_ge(s["ex_zero"], 1)
                        pool.wait_ge(s["r_hi"], 1)
                        for n in range(6 * NC):
                            if n > 1:
                                pool.wait_ge(s["bc_mm"], n - 1)
                            expand(g, n, 0).then_inc(s["ex_hi"], 1)
                            pool.wait_ge(s["ex_hi"], n + 1)
                            if n == 1:
                                pool.wait_ge(s["cs_read"], NC)
                                pool.wait_ge(s["dec_read"], 1)
                                pool.wait_ge(s["state_in"], 16 * 14)
                            if 1 <= n <= 6:
                                start_state(1 + (n - 1) // 2, (n - 1) % 2)

                    w = rings[:, 0, :, :]
                    nc.gpsimd.memset(w[:, :, 88:112], 0.0)
                    nc.gpsimd.memset(w[:, :, 120:128], 0.0).then_inc(s["gaps"], 1)
                    for q, n in enumerate(SPLIT):
                        if q == Q_WOUT:
                            scan_rows()
                            gates()
                        pool.wait_ge(s["split_hi"], q + 1)
                        w = slot(n)[:, 0:size(n), :]
                        nc.gpsimd.tensor_tensor(rings_r[:, slot_of[n], 0:size(n), :], w,
                                                whis[:, q % 2, 0:size(n), :].bitcast(F32),
                                                ALU.subtract).then_inc(s["split_lo"], 1)

                @block.tensor
                def _(pe):
                    mm, tr = nc.tensor.matmul, nc.tensor.transpose

                    def split_block(q):
                        pe.wait_ge(s["split_lo"], q + 1)
                        return whis[:, q % 2, :, :], rings_r[:, slot_of[SPLIT[q]], :, :]

                    def mm3(out, w, k, hi, lo, cols, start, stop):
                        mm(out, w[0][:, k, :], hi[:, cols], start=start, stop=False)
                        mm(out, w[0][:, k, :], lo[:, cols], start=False, stop=False)
                        return mm(out, w[1][:, k, :], hi[:, cols], start=False, stop=stop)

                    halves = [slice(hf * HALF, (hf + 1) * HALF) for hf in range(2)]

                    def norm_sum(i, k):
                        pe.wait_ge(s["sq_ready"], KT * i + k + 1)
                        for hf in range(2):
                            ins = mm(PS[:, hf, 0:HALF], ones[:, :], tmp[:, k % 2, hf * HALF:(hf + 1) * HALF],
                                     start=k == 0, stop=k == KT - 1)
                        ins.then_inc(s["sq_used"], 1)

                    pe.wait_ge(s["par_in"], 16 * (len(PROWS) + 2))
                    tr(PS[:, 3, 0:NPROW], Ub[0:NPROW, 0:P], ident[0:NPROW, 0:NPROW])
                    tr(PS[:, 3, P:P + 8], Ub[0:8, 2 * P:3 * P], ident[0:8, 0:8]).then_inc(s["par_t"], 1)
                    for k in range(KT):
                        norm_sum(0, k)

                    def ada(m, bank):
                        n = at_block["ada_w", m]
                        pe.wait_ge(ring_in[slot_of[n]], arrival[n])
                        for k in range(KT):
                            ins = mm(PS[:, bank, 2 * m:2 * m + 2], slot(n)[:, k, :], cT[:, k:16:8], start=k == 0,
                                     stop=k == KT - 1)
                        ins.then_inc(s["ada_mm"], 1)

                    pe.wait_ge(s["par_cols"], 1)
                    for k in range(KT):
                        if k > 1:
                            pe.wait_ge(s["mod_ready"], k - 1)
                        ada(k, 2 + k % 2)
                        ada(KT + k, 2 + k % 2)
                    pair = [0]

                    def pair_banks():
                        n = pair[0]
                        pair[0] += 1
                        if n - 1 > 0:
                            pe.wait_ge(s["pair_read"], n - 1)
                        return 4 + 2 * (n % 2)

                    def pair_mm(b, lhsT, rhs, start=True, stop=True):
                        for hf in range(2):
                            ins = mm(PS[:, b + hf, 0:HALF], lhsT, rhs[:, hf * HALF:(hf + 1) * HALF],
                                     start=start, stop=stop)
                        return ins

                    for n in range(NU):
                        w = split_block(n)
                        b = pair_banks()
                        for k in range(KT):
                            if n == 0:
                                pe.wait_ge(s["h_lo"], k + 1)
                            for hf in range(2):
                                ins = mm3(PS[:, b + hf, 0:HALF], w, k, h_high_r[:, k, :], h_r[:, k, :], halves[hf],
                                          k == 0, k == KT - 1)
                        ins.then_inc(s["pair_mm"], 1)
                        for m in ADA_AFTER[n]:
                            ada(m, 2)

                    for f in range(2):
                        b = pair_banks()
                        pe.wait_ge(s["kk_sq"], f + 1)
                        pair_mm(b, BO[:, :], tmp[:, f, :]).then_inc(s["pair_mm"], 1)
                    pe.wait_ge(s["lora_in"], 48)
                    pe.wait_ge(s["lora_x"], 2)
                    for part, src in ((0, tanx), (64, U[:, LORA, :])):
                        for d in range(2):
                            ps_ = slice(part + 32 * d, part + 32 * d + 32)
                            for f in range(2):
                                b = pair_banks()
                                pair_mm(b, lora[ps_, f * P:(f + 1) * P], src[ps_, :]).then_inc(s["pair_mm"], 1)
                    for f in range(2):
                        b = pair_banks()
                        pair_mm(b, lora[0:64, 256 + f * P:256 + (f + 1) * P], sigx[0:64, :]).then_inc(s["pair_mm"], 1)
                    assert pair[0] == NU + 12

                    for m in ADA_LATE[0]:
                        ada(m, 2)
                    pe.wait_ge(s["state_in"], 16 * 14)
                    pe.wait_ge(s["pair_read"], NU + 12)
                    for d in range(2):
                        for q in range(4):
                            tr(PS[:, 6, 256 * d + 64 * q:256 * d + 64 * q + 64], SSI[d][0:64, q, :], ident[0:64, 0:64])
                        for f in range(2):
                            tr(PS[:, 7, 128 * d + 64 * f:128 * d + 64 * f + 64], MLI[d][0:64, f, :], ident[0:64, 0:64])
                            ins = tr(PS[:, 7, 256 + 128 * d + 64 * f:256 + 128 * d + 64 * f + 64],
                                     RWI[d][0:64, f, :], ident[0:64, 0:64])
                    ins.then_inc(s["si_t"], 1)
                    pe.wait_ge(s["dec_diag"], 1)
                    dd = DD[RS, :].rearrange("p (r c) -> p r c", c=5)
                    for q in range(2):
                        o = PS[64 * q:64 * q + 64, 3, 128:188]
                        for d in range(2):
                            mm(o[:, 20 * d:20 * d + 20], ones[RS, 0:64], dd[:, 8 * d + 4 * q:8 * d + 4 * q + 4, :],
                               start=True, stop=True)
                            ins = mm(o[:, 40 + 10 * d:50 + 10 * d], ones[RS, 0:64],
                                     dd[:, 16 + 4 * d + q:20 + 4 * d:2, :], start=True, stop=True)
                    ins.then_inc(s["dec_mm"], 1)
                    pe.wait_ge(s["mod_mid"], 1)
                    pe.wait_ge(s["feat_ready"], len(POST))
                    pe.wait_ge(s["k_scaled"], 2)
                    pe.wait_ge(s["rows_act"], 7)
                    pe.wait_ge(s["dec_read"], 1)
                    def token_major(c):
                        if c:
                            pe.wait_ge(s["ta_act"], 4 * c)
                        for q in range(4):
                            tr(PS[:, 0, q * P:(q + 1) * P], U[:, XS + q, ck(c)], ident[:, :])
                        for q, m in enumerate((BT_, MK, MK + 1)):
                            tr(PS[:, 1, q * P:(q + 1) * P], U[:, m, ck(c)], ident[:, :])
                        for q in range(2):
                            tr(PS[:, 2, q * P:(q + 1) * P], U[:, MV + q, ck(c)], ident[:, :])
                        for q, r in enumerate((SP, KR, EC, TE, EM)):
                            ins = tr(PS[:, 3, q * NR:(q + 1) * NR], r[:, ck(c)], ident[RS, R0:R0 + NR])
                        ins.then_inc(s["ta_mm"], 1)

                    token_major(0)
                    for c in range(NC):
                        if c < NC - 1:
                            token_major(c + 1)
                        if c:
                            pe.wait_ge(s["cs_read"], c)
                            for m in ADA_LATE[c]:
                                ada(m, 7)
                        pe.wait_ge(s["xe_ready"], c + 1)
                        pe.wait_ge(s["ta_act"], 4 * c + 4)
                        if c > 0:
                            pe.wait_ge(s["cs_read"], c)
                        pe.wait_ge(s["si_ready"], 6)
                        for d in range(2):
                            if c and not (c < 4 if d == 0 else c > 1):
                                continue
                            for q in range(2):
                                ins = mm(PS[64 * q:64 * q + 64, 4, 256 * d:256 * d + 256], BK[:, 64 * q:64 * q + 64],
                                         XE[:, d, 256 * q:256 * q + 256], start=True, stop=True)
                        for d in range(2):
                            if c and not (c < 4 if d == 0 else c > 1):
                                continue
                            for hh in range(ML_H):
                                f, q = hh // 2, hh % 2
                                ins = mm(PS[64 * q:64 * q + 64, 5, 256 * d + 65 * f:256 * d + 65 * f + 65],
                                         BK[:, P + 64 * hh:P + 64 * hh + 64], VE[:, d, 65 * hh:65 * hh + 65],
                                         start=True, stop=True)
                        if c == 0:
                            for d in range(2):
                                for q in range(4):
                                    mm(PS[:, 6, 256 * d + 64 * q:256 * d + 64 * q + 64],
                                       XE[:, d, q * P:(q + 1) * P], BK[:, 64 * (q // 2):64 * (q // 2) + 64],
                                       start=True, stop=True)
                                for hh in range(ML_H):
                                    ins = mm(PS[0:64, 7, 256 * d + 64 * hh:256 * d + 64 * hh + 64],
                                             VE[:, d, 65 * hh:65 * hh + 64], BK[:, P + 64 * hh:P + 64 * hh + 64],
                                             start=True, stop=True)
                        ins.then_inc(s["cs_mm"], 1)

                    pe.wait_ge(s["mod_ready"], KT + 1)
                    def row_fill(c, i):
                        n = 6 * c + i
                        pe.wait_ge(s["ta_act"], 4 * NC + 2 * c + 2)
                        if n - 1 > 0:
                            pe.wait_ge(s["bc_exp"], n - 1)
                        pe.wait_ge(s["ex_hi"], n + 1)
                        pe.wait_ge(s["ex_lo"], n + 1)
                        for w_ in range(2):
                            mm(PS[:, 2 + i % 2, :], onesr[:, :], EX[:, n % 2, w_].rearrange("p q t -> p (q t)"),
                               start=w_ == 0, stop=False)
                        ins = mm(PS[:, 2 + i % 2, :], identb[:, :],
                                 NEG[:, P * (i % 2):P * (i % 2) + P].unsqueeze(1).broadcast_to((P, 4, P)),
                                 start=False, stop=True)
                        ins.then_inc(s["bc_mm"], 1)

                    def y_ssd(c, g):
                        pe.wait_ge(s["w_ready"], 6 * c + 2 * g + 2)
                        pe.wait_ge(s["xd_ready"], c + 1)
                        if c > 0:
                            pe.wait_ge(s["yt_read"], c)
                        for q in range(4):
                            hh = 4 * g + q
                            for d in range(2):
                                ins = mm(PS[:, 4, 64 * hh:64 * hh + 64], W[:, 2 * g + d, q * P:(q + 1) * P],
                                         XE[:, d, 64 * hh:64 * hh + 64], start=d == 0, stop=d == 1)
                        ins.then_inc(s["y_mm"], 1)

                    def chunk_head(c):
                        if 6 * c > 0:
                            pe.wait_ge(s["bc_exp"], 6 * c)
                        if 3 * c > 0:
                            pe.wait_ge(s["num_read"], c)
                        for q in range(4):
                            tr(PS[:, 2, q * P:(q + 1) * P], U[:, XS + q, ck(c)], ident[:, :])
                        for q in range(2):
                            ins = tr(PS[:, 3, q * P:(q + 1) * P], U[:, MV + q, ck(c)], ident[:, :])
                        ins.then_inc(s["ta_mm"], 1)
                        if c == 0:
                            pe.wait_ge(s["ta_act"], 4 * NC)
                        for q in range(2):
                            mm(PS[:, q, 0:P], U[64 * q:64 * q + 64, BT_, ck(c)],
                               U[64 * q:64 * q + 64, CT_, ck(c)], start=True, stop=True)
                        for hh in range(ML_H):
                            f, q = hh // 2, hh % 2
                            ins = mm(PS[:, q, (1 + f) * P:(2 + f) * P], U[64 * q:64 * q + 64, MK + f, ck(c)],
                                     U[64 * q:64 * q + 64, MQ + f, ck(c)], start=True, stop=True)
                        ins.then_inc(s["qk_mm"], 1)

                        for i in range(4):
                            row_fill(c, i)

                    def chunk_products(c):
                        y_ssd(c, 0)
                        for i in range(4, 6):
                            row_fill(c, i)
                        if c == 1:
                            pe.wait_ge(s["states_ready"], 6)
                        if c:
                            for d in range(2):
                                k = c - 1 if d == 0 else 4 - c
                                for q in range(2):
                                    mm(PS[:, 5 + q, 256 * d:256 * d + 256], U[64 * q:64 * q + 64, CT_, ck(c)],
                                       S_ssd[64 * q:64 * q + 64, d, k, :], start=True, stop=True)
                        y_ssd(c, 1)
                        for d in range(2):
                            pe.wait_ge(s["w_ready"], 6 * c + 6)
                            num, inter = (7, 0) if d == 0 else (2, 5)
                            if d == 1:
                                pe.wait_ge(s["y_comb"], 3 * c + 1)
                            for hh in range(ML_H):
                                f, q = hh // 2, hh % 2
                                ins = mm(PS[:, num, 65 * hh:65 * hh + 65], W[:, d, hh * P:(hh + 1) * P],
                                         VA[:, hh, :], start=True, stop=True)
                                if c:
                                    k = c - 1 if d == 0 else 4 - c
                                    ins = mm(PS[:, inter + q, 65 * f:65 * f + 65], U[64 * q:64 * q + 64, MQ + f, ck(c)],
                                             S_ml[64 * q:64 * q + 64, d, k, 65 * f:65 * f + 65], start=True, stop=True)
                            ins.then_inc(s["y_mm"], 1)

                    def chunk_tail(c):
                        pe.wait_ge(s["y_comb"], 3 * c + 3)
                        for q in range(4):
                            tr(PS[:, 4, q * P:(q + 1) * P], YS[:, q * P:(q + 1) * P], ident[:, :])
                        for q in range(2):
                            ins = tr(PS[:, 6, q * P:(q + 1) * P], YM[:, q * P:(q + 1) * P], ident[:, :])
                        ins.then_inc(s["yt_mm"], 1)

                    chunk_head(0)
                    for c in range(NC):
                        chunk_products(c)
                        if c < NC - 1:
                            chunk_head(c + 1)
                        chunk_tail(c)

                    def cpos(k, d):
                        return 0 if k == 0 else (k if d == 0 else 5 - k)

                    hq = [(hh // 2, slice(64 * (hh % 2), 64 * (hh % 2) + 64)) for hh in range(RWKV_H)]
                    pe.wait_ge(s["yt_read"], NC)
                    for k in range(NC):
                        for d in range(2):
                            b, a, i = units[d], 4 * d, 2 * k + d
                            pe.wait_ge(s["rw_feat"], i + 1)
                            if i - 1 > 0:
                                pe.wait_ge(s["yr_read"], i - 1)
                            if k == 1:
                                pe.wait_ge(s["rwo_ready"], 2)
                            for w_ in range(2):
                                for f in range(2):
                                    n = 2 * w_ + f
                                    tr(PS[:, a, n * P:(n + 1) * P], b["KB"][:, f, w_, :], ident[:, :])
                            for f in range(2):
                                ins = tr(PS[:, a + 1, f * P:(f + 1) * P], U[:, RV_ + f, ck(cpos(k, d))], ident[:, :])
                            ins.then_inc(s["rw_t"], 1)
                            for hh, (f, q) in enumerate(hq):
                                ins = mm(PS[:, a + 2 + hh % 2, 256 * f:256 * f + 256],
                                         b["KB"][q, f, 1, :], b["RK"][q, f, :, :], start=True, stop=True)
                            ins.then_inc(s["rw_prod"], 1)
                        for d in range(2):
                            b, a, i = units[d], 4 * d, 2 * k + d
                            pe.wait_ge(s["rw_tok"], 2 * i + 2)
                            for hh, (f, q) in enumerate(hq):
                                ins = mm(PS[:, a + hh % 2, f * P:(f + 1) * P], b["RK"][q, f, 0, :], b["KB"][q, f, 1, :],
                                         start=True, stop=True)
                            ins.then_inc(s["rw_prod2"], 1)
                            pe.wait_ge(s["rw_masked"], i + 1)
                            for hh, (f, q) in enumerate(hq):
                                ins = mm(PS[:, a + 2 + hh % 2, 256 * f:256 * f + 256],
                                         b["KB"][q, f, 0, :], b["RK"][q, f, :, :], start=True, stop=True)
                            ins.then_inc(s["rw_prod2"], 1)
                        def each(d, bank, lhs, rhs):
                            b = units[d]
                            for hh in range(RWKV_H):
                                ins = mm(PS[:, 4 * d + bank, hh * P:(hh + 1) * P], b[lhs][:, hh, :], b[rhs][:, hh, :],
                                         start=True, stop=True)
                            return ins

                        def copied(d, r):
                            pe.wait_ge(s["inv_copy"], 12 * k + 2 * r + d + 1)

                        def added(d, r):
                            pe.wait_ge(s["inv_add"], 12 * k + 2 * r + d + 1)

                        for d in range(2):
                            pe.wait_ge(s["rw_masked2"], 2 * k + d + 1)
                            each(d, 0, "QT", "Q")
                            each(d, 3, "Q", "QT").then_inc(s["inv_mm"], 1)
                        for d in range(2):
                            copied(d, 0)
                            each(d, 2, "QT", "X")
                            each(d, 0, "QT", "Q")
                            each(d, 3, "Q", "QT").then_inc(s["inv_mm"], 1)
                        for d in range(2):
                            copied(d, 1)
                            added(d, 0)
                            each(d, 2, "QT", "X")
                            each(d, 3, "Q", "QT").then_inc(s["inv_mm"], 1)
                        for d in range(2):
                            copied(d, 2)
                            added(d, 1)
                            each(d, 2, "QT", "X").then_inc(s["inv_mm"], 1)
                        for l in range(3):
                            for d in range(2):
                                added(d, 2 + l)
                                pe.wait_ge(s["pl_ready"], 6 * k + 2 * l + d + 1)
                                b = units[d]
                                each(d, 0, "PL", "X")
                                for hh in range(RWKV_H):
                                    ins = tr(PS[:, 4 * d + 3, hh * P:(hh + 1) * P], b["X"][:, hh, :], ident[:, :])
                                ins.then_inc(s["inv_mm"], 1)
                            for d in range(2):
                                copied(d, 3 + l)
                                each(d, 2, "QT", "Q").then_inc(s["inv_mm"], 1)
                        for d in range(2):
                            b, a, i = units[d], 4 * d, 2 * k + d
                            for hh, (f, q) in enumerate(hq):
                                o = PS[:, a + hh % 2, 64 * f:64 * f + 64]
                                if k:
                                    mm(o, b["RK"][q, f, 0, :], b["Sp"][q, f, :], start=True, stop=False)
                                ins = mm(o, b["BTm"][:, hh, :], b["VT"][:, 64 * hh:64 * hh + 64], start=not k,
                                         stop=True)
                            ins.then_inc(s["rhs_mm"], 1)
                        for d in range(2):
                            b, a, i = units[d], 4 * d, 2 * k + d
                            added(d, 5)
                            pe.wait_ge(s["rhs_sb"], i + 1)
                            for hh in range(RWKV_H):
                                ins = mm(PS[:, a + 2, 64 * hh:64 * hh + 64], b["X"][:, hh, :],
                                         b["RHS"][:, 64 * hh:64 * hh + 64], start=True, stop=True)
                            ins.then_inc(s["sa_mm"], 1)
                        for d in range(2):
                            b, a, i = units[d], 4 * d, 2 * k + d
                            pe.wait_ge(s["sa_sb"], i + 1)
                            for hh, (f, q) in enumerate(hq):
                                hs = slice(64 * hh, 64 * hh + 64)
                                o = PS[q, a + 3, f * P:(f + 1) * P]
                                if k:
                                    mm(o, b["Sp"][q, f, :], b["RK"][q, f, 1, :], start=True, stop=False)
                                mm(o, b["VT"][:, hs], b["RKT"][:, hh, :], start=not k, stop=False)
                                ins = mm(o, b["NSA"][:, hs], b["RBT"][:, hh, :], start=False, stop=True)
                            ins.then_inc(s["yr_mm"], 1)
                            if k < 4:
                                for hh, (f, q) in enumerate(hq):
                                    hs = slice(64 * hh, 64 * hh + 64)
                                    o = PS[q, a + 1, 64 * f:64 * f + 64]
                                    mm(o, b["KBT"][:, hs], b["VT"][:, hs], start=True, stop=False)
                                    ins = mm(o, b["KBT"][:, 256 + 64 * hh:256 + 64 * hh + 64], b["NSA"][:, hs],
                                             start=False, stop=True)
                                ins.then_inc(s["st_mm"], 1)
                        if k == 0:
                            for d in range(2):
                                pe.wait_ge(s["rf_ready"], d + 1)
                                sf = units[d]["s"].rearrange("p f t -> p (f t)")
                                for f in range(2):
                                    ins = tr(PS[0:64, 4 * d, f * P:(f + 1) * P], sf[:, 64 * f:64 * f + 64],
                                             ident[:, :])
                                ins.then_inc(s["rf_t"], 1)

                    pe.wait_ge(s["yr_read"], 2 * NC)

                    def g_job(b, parts, rows=slice(0, P)):
                        for n, (M, src) in enumerate(parts):
                            for hf in range(2):
                                ins = mm(PS[rows, b + hf, 0:HALF], M, src[:, hf * HALF:(hf + 1) * HALF],
                                         start=n == 0, stop=n == len(parts) - 1)
                        return ins

                    pe.wait_ge(s["rwo_ready"], 2)
                    pe.wait_ge(s["bonus"], 1)
                    for n, t_ in enumerate((Z, Z + 1, MV, MV + 1)):
                        g_job(2 * n, [(BO[:, :], U[:, t_, :])]).then_inc(s["g_mm"], 1)
                    pe.wait_ge(s["g_read"], 4)
                    pe.wait_ge(s["g_sq"], 4)
                    for n in range(2):
                        ins = g_job(6, [(ones[:, 0:32], gtmp[:, 2 + 2 * n, :]), (ones[:, 0:32], gtmp[:, 3 + 2 * n, :])],
                                    slice(32 * n, 32 * n + 32))
                    ins.then_inc(s["g_mm"], 1)
                    pe.wait_ge(s["g_src"], 1)
                    for n, t_ in enumerate((BT_, CT_)):
                        g_job(2 * n, [(BO[:, :], U[:, t_, :])]).then_inc(s["g_mm"], 1)
                    for i, src in enumerate(SQUARES):
                        pe.wait_ge(s["g_sq"], (7, 8, 5, 6)[i])
                        ins = g_job(4, [(BO[:, 48:80], src)], slice(32 * i, 32 * i + 32))
                    ins.then_inc(s["g_mm"], 1)
                    pe.wait_ge(s["g_rec"], 1)
                    for n in range(2):
                        pe.wait_ge(s["g_read"], 5 + n)
                        g_job(2 * n, [(ones[32 * n:32 * n + 1, :], gtmp[32 * n:32 * n + 1, 2, :])]).then_inc(
                            s["g_mm"], 1)
                    pe.wait_ge(s["g_rec"], 2)
                    for i in range(4):
                        if i > 1:
                            pe.wait_ge(s["y_done"], 2 * (i - 1))
                        rows = slice(32 * i, 32 * i + 32)
                        g_job(2 * ((2 + i) % 4), [(SPREAD[rows, :], gtmp[rows, 3, :])]).then_inc(s["g_mm"], 1)

                    def residual_mm(b, w, k, hi, lo, start, stop):
                        for hf in range(2):
                            ins = mm3(PS[:, b + hf, 0:HALF], w, k, hi, lo, halves[hf], start, stop)
                        return ins

                    for m in range(KT):
                        w = split_block(Q_WOUT + m)
                        if m > 1:
                            pe.wait_ge(s["wo_read"], m - 1)
                        else:
                            pe.wait_ge(s["y_done"], 5 + m)
                        for k, t_ in enumerate(YTILES):
                            if m == 0:
                                pe.wait_ge(s["y_lo"], k + 1)
                            ins = residual_mm(4 + 2 * (m % 2), w, k, rp_r[:, k, :], U_r[:, t_, :], k == 0,
                                              k == KT - 1)
                        ins.then_inc(s["wo_mm"], 1)
                        if m:
                            norm_sum(1, m - 1)
                    norm_sum(1, KT - 1)
                    pe.wait_ge(s["wo_read"], KT)
                    for j in range(FT):
                        for v in range(2):
                            w = split_block(Q_FFN + 2 * j + v)
                            if j > 1:
                                pe.wait_ge(s["ffn_ready"], j - 1)
                            b = 4 * (j % 2) + 2 * v
                            for k in range(KT):
                                if j == 0 and v == 0:
                                    pe.wait_ge(s["h_lo"], KT + k + 1)
                                for hf in range(2):
                                    ins = mm3(PS[:, b + hf, 0:HALF], w, k, h_high_r[:, k, :], h_r[:, k, :], halves[hf],
                                              k == 0, k == KT - 1)
                            ins.then_inc(s["ffn_mm"], 1)
                    pe.wait_ge(s["ffn_ready"], FT)
                    for m in range(KT):
                        if m > 1:
                            pe.wait_ge(s["w2_read"], m - 1)
                        for i, (k0, k1) in enumerate(W2_PARTS):
                            w = split_block(Q_W2 + 3 * m + i)
                            for k in range(k0, k1):
                                if m == 0:
                                    pe.wait_ge(s["u_lo"], k + 1)
                                ins = residual_mm(2 * (m % 2), w, k - k0, u_high_r[k], U_r[:, k, :], k == 0, k == FT - 1)
                            ins.then_inc(s["w2_mm"], 1)

                @block.scalar
                def _(act):
                    A = nc.scalar.activation
                    step = counter()

                    def split(q):
                        if q >= len(SPLIT):
                            return
                        n = SPLIT[q]
                        if q > 1:
                            sem, value = used[SPLIT[q - 2]]
                            act.wait_ge(sem, value)
                        act.wait_ge(ring_in[slot_of[n]], arrival[n])
                        if q == 0:
                            act.wait_ge(s["gaps"], 1)
                        A(whis[:, q % 2, 0:size(n), :], slot(n)[:, 0:size(n), :],
                          ACT.Copy).then_inc(s["split_hi"], 1)

                    def norm(i, row0):
                        for k in range(KT):
                            if i:
                                split(Q_WOUT + 2 + k)
                                act.wait_ge(s["wo_read"], k + 1)
                            if KT * i + k - 1 > 0:
                                act.wait_ge(s["sq_used"], KT * i + k - 1)
                            A(tmp[:, k % 2, :], xv[:, k, :], ACT.Square).then_inc(s["sq_ready"], 1)
                        act.wait_ge(s["sq_used"], KT * (i + 1))
                        A(rs.rearrange("p (a t) -> p a t", a=2), PS[:, 0:2, 0:HALF], ACT.Sqrt, bias=eps[:, 0:1],
                          scale=1.0 / D).then_inc(s["std_ready"], 1)
                        for k in range(KT + 1):
                            if i == 0 and k == KT - 1:
                                split(0)
                                split(1)
                            if k < KT:
                                act.wait_ge(s["mod_ready"], k + 1 if i == 0 else KT + 1)
                                act.wait_ge(s["xr_ready"], KT * i + k + 1)
                                for g, ts in ((0, slice(0, CTX)), (1, slice(CTX, T))):
                                    A(h[:, k, ts], h[:, k, ts], ACT.Identity,
                                      bias=MOD[:, 2 * (row0 + k) + g:2 * (row0 + k) + g + 1],
                                      scale=GS[:, 16 * i + 2 * k + g:16 * i + 2 * k + g + 1]).then_inc(
                                        s["h_ready"], 1)
                            if k:
                                act.wait_ge(s["h_ready"], 2 * (KT * i + k))
                                A(h_high_r[:, k - 1, :], h[:, k - 1, :], ACT.Copy).then_inc(s["h_hi"], 1)

                    act.wait_ge(s["par_t"], 1)
                    A(PC[:, 0:NPROW], PS[:, 3, 0:NPROW], ACT.Copy)
                    A(PC[:, P:P + 8], PS[:, 3, P:P + 8], ACT.Copy).then_inc(s["par_cols"], 1)
                    norm(0, 0)
                    act.wait_ge(s["par_cols"], 1)

                    def pair_out(n, out, func, **kw):
                        act.wait_ge(s["pair_mm"], n + 1)
                        b = 4 + 2 * (n % 2)
                        A(out.rearrange("p (a t) -> p a t", a=2), PS[:, b:b + 2, 0:HALF], func, **kw).then_inc(
                            s["pair_read"], 1)

                    def post_start(j, n):
                        m = POST[j]
                        act.wait_ge(s["pair_read"], n + 1)
                        pp = slice(0, 64) if m == MISC else slice(0, P)
                        if m in SHIFTED:
                            c = OM[pp, SHIFTED[m]:SHIFTED[m] + 1]
                            A(tmp[pp, j % 2, :], U[pp, m, :], ACT.Identity, scale=c).then_inc(s["tmp_act"], 1)
                        else:
                            nm, i, w_ = ("ssd", m - XS, 6) if m < MISC else ("mlstm", m - MQ, 4)
                            A(tmp[:, j % 2, :], U[:, m, :], ACT.Identity, scale=col(nm + "_conv_w", w_ + i),
                                  bias=col(nm + "_conv_b", i)).then_inc(s["tmp_act"], 1)

                    def post_end(j):
                        m = POST[j]
                        pp = slice(0, 64) if m == MISC else slice(0, P)
                        act.wait_ge(s["tmp_dve"], j + 1)
                        A(U[pp, m, :], tmp[pp, j % 2, :], ACT.Silu if m in CONV else ACT.Copy).then_inc(
                            s["feat_ready"], 1)

                    j = 0
                    for n, m in enumerate(ORDER):
                        func = ACT.Silu if m < XS else ACT.Sigmoid if m >= MO else ACT.Copy
                        pair_out(n, U[:, m, :], func)
                        if n + 2 < NU:
                            split(n + 2)
                        if n == 0:
                            act.wait_ge(s["pair_read"], 1)
                            act.wait_ge(s["rows_dve"], 1)
                            A(RP[RS, 6:7], RP[RS, 2:3], ACT.Exp).then_inc(s["rows_act"], 1)
                            A(zr, U[RS, MISC, :], ACT.Identity, scale=RP[RS, 4:5], bias=RP[RS, 5:6]).then_inc(
                                s["rows_act"], 1)
                            A(KR, U[96:96 + NR, MISC, :], ACT.Copy).then_inc(s["rows_act"], 1)
                            act.wait_ge(s["rows_act"], 3)
                            A(t1, zr, ACT.Abs).then_inc(s["act_step"], 1)
                            act.wait_ge(s["act_step"], step())
                            A(t1, t1, ACT.Exp, scale=-1.0).then_inc(s["rows_act"], 1)
                        if n == 1:
                            act.wait_ge(s["rows_dve"], 2)
                            A(CF, t2, ACT.Ln).then_inc(s["rows_act"], 1)
                        if n == 16:
                            act.wait_ge(s["rows_dve"], 3)
                            for c in range(NC):
                                ins = A(DEC[RS, c:c + 1], RE[RS, c:c + 1], ACT.Exp, bias=MC[RS, c:c + 1])
                            ins.then_inc(s["rows_act"], 1)
                            for c in range(NC):
                                A(EC[:, ck(c)], Rr[:, ck(c)], ACT.Exp, bias=MC[RS, c:c + 1])
                                A(TE[:, ck(c)], KR[:, ck(c)], ACT.Exp, bias=RE[RS, c:c + 1])
                            A(EM, EM, ACT.Exp).then_inc(s["rows_act"], 1)
                        if m in POST:
                            post_start(j, n)
                            if j:
                                post_end(j - 1)
                            j += 1
                        elif j == len(POST):
                            post_end(j - 1)
                            j += 1
                            act.wait_ge(s["feat_ready"], len(POST))
                            for f in range(2):
                                A(KK[:, f, :], U[:, RK_ + f, :], ACT.Identity, scale=col("rwkv_k_k", f))
                            A(tanx[0:64, :], U[0:64, LORA, :], ACT.Tanh).then_inc(s["act_step"], 1)
                            act.wait_ge(s["act_step"], step())
                            for f in range(2):
                                A(tmp[:, f, :], KK[:, f, :], ACT.Square).then_inc(s["kk_sq"], 1)
                            A(sigx[0:64, :], U[0:64, MISC, :], ACT.Sigmoid).then_inc(s["lora_x"], 1)
                            A(tanx[0:64, 0:1], tanx[0:64, 0:1], ACT.Copy).then_inc(s["lora_x"], 1)
                    for f in range(2):
                        pair_out(NU + f, tmp[:, f, :], ACT.Sqrt, bias=eps[:, 1:2])
                    n = NU + 2
                    for dst, nm in ((LW, "rwkv_w0"), (BB, "rwkv_a0")):
                        for d in range(2):
                            for f in range(2):
                                pair_out(n, dst[d][:, f, :], ACT.Sigmoid, bias=col(nm, 2 * d + f))
                                n += 1
                    for f in range(2):
                        pair_out(n, U[:, LORA + f, :], ACT.Copy)
                        n += 1
                    act.wait_ge(s["si_t"], 1)
                    for d in range(2):
                        A(S_ssd[:, d, 0, :], PS[:, 6, 256 * d:256 * d + 256], ACT.Copy).then_inc(s["si_ready"], 1)
                        A(S_ml[:, d, 0, :].rearrange("p (f n) -> p f n", f=2)[:, :, 0:64],
                              PS[:, 7, P * d:P * d + P].rearrange("p (f n) -> p f n", f=2), ACT.Copy).then_inc(
                                  s["si_ready"], 1)
                        A(units[d]["S"], PS[:, 7, 256 + P * d:256 + P * d + P].rearrange(
                            "p (f n) -> p f n", f=2), ACT.Copy).then_inc(s["si_ready"], 1)
                    act.wait_ge(s["dec_mm"], 1)
                    A(DECB[:, 0:60], PS[:, 3, 128:188], ACT.Copy).then_inc(s["dec_read"], 1)
                    def chunk_states(c):
                        act.wait_ge(s["cs_mm"], c + 1)
                        if c == 0:
                            A(SO, PS[:, 6, :], ACT.Copy)
                            A(MLO[0:64, :], PS[0:64, 7, :], ACT.Copy)
                            for d in range(2):
                                ins = A(NO[:, 2 * d:2 * d + 2], PS[:, 5, 256 * d + 64:256 * d + 130:65], ACT.Copy)
                            ins.then_inc(s["cs_read"], 1)
                            act.wait_ge(s["cs_read"], 1)
                            A(NO[:, 0:1], NO[:, 0:1], ACT.Copy).then_inc(s["out_ready"], 1)
                        else:
                            for d in range(2):
                                if not (c < 4 if d == 0 else c > 1):
                                    continue
                                k = c if d == 0 else 5 - c
                                A(S_ssd[:, d, k, :], PS[:, 4, 256 * d:256 * d + 256], ACT.Copy)
                                ins = A(S_ml[:, d, k, :], PS[:, 5, 256 * d:256 * d + 130], ACT.Copy)
                            ins.then_inc(s["cs_read"], 1)

                    for c in range(NC):
                        act.wait_ge(s["ta_mm"], c + 1)
                        if c > 0:
                            act.wait_ge(s["xe_ready"], c)
                        A(XT, PS[:, 0, :], ACT.Copy).then_inc(s["ta_act"], 1)
                        A(VA[:, :, 0:64], PS[:, 2, 0:256].rearrange("p (h n) -> p h n", h=4), ACT.Copy).then_inc(
                            s["ta_act"], 1)
                        A(COLS[:, c].rearrange("p k r -> p (k r)"), PS[:, 3, 0:120], ACT.Copy).then_inc(s["ta_act"], 1)
                        if c > 0:
                            chunk_states(c - 1)
                        A(BK, PS[:, 1, 0:384], ACT.Copy).then_inc(s["ta_act"], 1)
                    chunk_states(NC - 1)
                    A(Rhi, Rr, ACT.Copy).then_inc(s["r_hi"], 1)
                    for c in range(NC):
                        act.wait_ge(s["ta_mm"], NC + c + 1)
                        act.wait_ge(s["xe_ready"], NC)
                        if c > 0:
                            act.wait_ge(s["xd_ready"], c)
                        A(XT, PS[:, 2, :], ACT.Copy).then_inc(s["ta_act"], 1)
                        if 4 * c > 0:
                            act.wait_ge(s["y_mm"], 4 * c)
                        A(VA[:, :, 0:64], PS[:, 3, 0:256].rearrange("p (h n) -> p h n", h=4), ACT.Copy).then_inc(
                            s["ta_act"], 1)
                        act.wait_ge(s["ta_act"], 4 * NC)
                        for i in range(6):
                            act.wait_ge(s["bc_mm"], 6 * c + i + 1)
                            if i == 4:
                                act.wait_ge(s["y_mm"], 4 * c + 1)
                            r = HEAD0[i]
                            for q in range(4):
                                ins = A(W[:, i % 4, q * P:(q + 1) * P], PS[:, 2 + i % 2, q * P:(q + 1) * P], ACT.Exp,
                                        bias=COLS[:, c, 1, r + q:r + q + 1])
                            ins.then_inc(s["bc_exp"], 1)
                    def decays(k):
                        for d in range(2):
                            b, i = units[d], 2 * k + d
                            act.wait_ge(s["rs_dve"], i + 1)
                            A(b["e1"], b["c"], ACT.Exp)
                            A(b["e2"], b["c"], ACT.Exp, scale=-1.0)
                            A(b["e3"], b["e3"], ACT.Exp)
                            A(EMID[:, 2 * d:2 * d + 2], MID[:, 2 * d:2 * d + 2], ACT.Exp).then_inc(s["rs_exp"], 1)

                    decays(0)
                    for k in range(NC):
                        for d in range(2):
                            b, a, i = units[d], 4 * d, 2 * k + d
                            act.wait_ge(s["rw_t"], i + 1)
                            A(b["KBT"], PS[:, a, :], ACT.Copy).then_inc(s["rw_tok"], 1)
                            A(b["VT"], PS[:, a + 1, 0:256], ACT.Copy).then_inc(s["rw_tok"], 1)

                        def copies(r, q, qt=True):
                            for d in range(2):
                                b, a = units[d], 4 * d
                                act.wait_ge(s["inv_mm"], 20 * k + 2 * r + d + 1)
                                if q:
                                    ins = A(b["Q"], PS[:, a, :].rearrange("p (h t) -> p h t", h=4), ACT.Copy)
                                A(b["QT"], PS[:, a + 3, :].rearrange("p (h t) -> p h t", h=4), ACT.Copy).then_inc(
                                    s["inv_copy"], 1)
                        copies(0, True)
                        copies(1, True)
                        copies(2, False)
                        if k < NC - 1:
                            decays(k + 1)
                        for l in range(3):
                            copies(4 + 2 * l, True)
                        for d in range(2):
                            act.wait_ge(s["rhs_mm"], 2 * k + d + 1)
                            A(units[d]["RHS"].rearrange("p (f q n) -> p q f n", f=2, q=2),
                                  PS[:, 4 * d:4 * d + 2, 0:P].rearrange("p q (f n) -> p q f n", f=2), ACT.Copy).then_inc(
                                      s["rhs_sb"], 1)
                        for d in range(2):
                            act.wait_ge(s["sa_mm"], 2 * k + d + 1)
                            A(units[d]["NSA"], PS[:, 4 * d + 2, 0:256], ACT.Copy, scale=-1.0).then_inc(s["sa_sb"], 1)
                        if k == 0:
                            for d in range(2):
                                act.wait_ge(s["rf_t"], d + 1)
                                A(lora[0:64, 256 * d:256 * d + 256], PS[0:64, 4 * d, 0:256], ACT.Copy).then_inc(
                                    s["rwo_ready"], 1)
                    split(Q_WOUT)
                    split(Q_WOUT + 1)
                    act.wait_ge(s["gated"], 1)
                    act.wait_ge(s["yr_read"], 2 * NC)
                    for q in range(4):
                        A(gtmp[:, 2 + q, :], U[:, XS + q, :], ACT.Square).then_inc(s["g_sq"], 1)
                    for n in (2, 3):
                        act.wait_ge(s["g_read"], 1 + n)
                        A(SQUARES[n], U[:, MV + n - 2, :], ACT.Square).then_inc(s["g_sq"], 1)
                    for n, t_ in enumerate((BT_, CT_)):
                        act.wait_ge(s["g_read"], 5 + n)
                        A(SQUARES[n], U[:, t_, :], ACT.Square).then_inc(s["g_sq"], 1)
                    act.wait_ge(s["g_mm"], 5)
                    A(gtmp[0:64, 2, :].rearrange("p (a t) -> p a t", a=2), PS[0:64, 6:8, 0:HALF], ACT.Sqrt,
                      bias=eps[0:64, 2:3], scale=1.0 / 256).then_inc(s["g_std"], 1)
                    act.wait_ge(s["g_mm"], 8)
                    A(gtmp[:, 3, :].rearrange("p (a t) -> p a t", a=2), PS[:, 4:6, 0:HALF], ACT.Sqrt,
                      bias=eps[:, 2:3], scale=1.0 / 64).then_inc(s["g_std"], 1)
                    for k, t_ in enumerate(YTILES):
                        act.wait_ge(s["y_done"], k + 1)
                        A(rp_r[:, k, :], U[:, t_, :], ACT.Copy).then_inc(s["y_hi"], 1)
                    norm(1, 24)

                    def u_split(t_):
                        act.wait_ge(s["ffn_ready"], t_ + 1)
                        A(u_high_r[t_], U[:, t_, :], ACT.Copy).then_inc(s["u_hi"], 1)

                    for j in range(FT):
                        act.wait_ge(s["ffn_mm"], 2 * j + 1)
                        if j > 1:
                            act.wait_ge(s["ffn_ready"], j - 1)
                        b = 4 * (j % 2)
                        A(tmp[:, j % 2, :].rearrange("p (a t) -> p a t", a=2), PS[:, b:b + 2, 0:HALF],
                          ACT.Silu).then_inc(s["ffn_silu"], 1)
                        split(Q_FFN + 2 * j + 2)
                        if 0 < j <= U_EARLY:
                            u_split(j - 1)
                        split(Q_FFN + 2 * j + 3)
                    act.wait_ge(s["ffn_mm"], 2 * FT)
                    for t_ in range(U_EARLY, FT):
                        u_split(t_)
                    for i in range(3 * KT):
                        split(Q_W2 + 2 + i)

                @block.vector
                def _(dve):
                    v = nc.vector
                    step = counter()

                    def norm(i):
                        dve.wait_ge(s["std_ready"], i + 1)
                        v.reciprocal(rs, rs).then_inc(s["dve_step"], 1)
                        dve.wait_ge(s["dve_step"], step())
                        for k in range(KT):
                            v.tensor_tensor(h[:, k, :], xv[:, k, :], rs, ALU.mult).then_inc(s["xr_ready"], 1)

                    def low_part(i, k):
                        dve.wait_ge(s["h_hi"], KT * i + k + 1)
                        v.tensor_tensor(h_r[:, k, :], h[:, k, :], h_high_r[:, k, :].bitcast(F32),
                                        ALU.subtract).then_inc(s["h_lo"], 1)

                    norm(0)
                    dve.wait_ge(s["par_cols"], 1)
                    mu = PC[:, MU0:MU0 + 8]
                    v.tensor_scalar(OM[:, :], mu, -1.0, 1.0, ALU.mult, ALU.add).then_inc(s["dve_step"], 1)
                    dve.wait_ge(s["dve_step"], step())
                    v.tensor_tensor(MUJ[:, :].rearrange("p (m j) -> p m j", j=4),
                                         mu.unsqueeze(2).broadcast_to((P, 8, 4)),
                                         PAR[:, 2:6].unsqueeze(1).broadcast_to((P, 8, 4)), ALU.mult).then_inc(
                                             s["dve_step"], 1)
                    dve.wait_ge(s["dve_step"], step())
                    v.tensor_tensor(MU2[:, :].rearrange("p (m j) -> p m j", j=2),
                                         mu.unsqueeze(2).broadcast_to((P, 8, 2)),
                                         PAR[:, 0:2].unsqueeze(1).broadcast_to((P, 8, 2)), ALU.mult).then_inc(
                                             s["dve_step"], 1)
                    dve.wait_ge(s["dve_step"], step())
                    v.tensor_scalar(KAO[:, :], col("rwkv_k_a", 0, 2), -1.0, 1.0, ALU.mult, ALU.add).then_inc(
                        s["dve_step"], 1)
                    dve.wait_ge(s["dve_step"], step())

                    modv = MOD[:, :].rearrange("p (m g) -> p m g", g=2)

                    def biased(bank, m):
                        return v.tensor_tensor(modv[:, m, :],
                                               PS[:, bank, 0:96].rearrange("p (m g) -> p m g", g=2)[:, m, :],
                                               biases[:, m, :], ALU.add)

                    def modulation(bank, m, scale, i, nm, k, n):
                        biased(bank, m).then_inc(s["dve_step"], 1)
                        dve.wait_ge(s["dve_step"], step())
                        v.scalar_tensor_tensor(
                            out=GS[:, 16 * i + 2 * k:16 * i + 2 * k + 2 * n].rearrange("p (m g) -> p m g", g=2),
                            in0=modv[:, scale:scale + n, :], scalar=1.0,
                            in1=col(nm, k, n).unsqueeze(2).broadcast_to((P, n, 2)), op0=ALU.add,
                            op1=ALU.mult).then_inc(s["mod_ready"], 1)

                    biases = col("ada_b", 0, 48).unsqueeze(2).broadcast_to((P, 48, 2))
                    for k in range(KT):
                        dve.wait_ge(s["ada_mm"], 2 * k + 2)
                        modulation(2 + k % 2, slice(k, k + KT + 1, KT), KT + k, 0, "norm1_g", k, 1)
                        if k:
                            low_part(0, k - 1)
                    low_part(0, KT - 1)
                    def post(j):
                        m = POST[j]
                        dve.wait_ge(s["tmp_act"], j + 1)
                        pp = slice(0, 64) if m == MISC else slice(0, P)
                        o, u = tmp[pp, j % 2, :], U[pp, m, :]

                        def madd(out, in_, s):
                            return v.scalar_tensor_tensor(out=out, in0=in_, scalar=s, in1=out, op0=ALU.mult,
                                                          op1=ALU.add)
                        if m in CONV:
                            nm, i, w_ = ("ssd", m - XS, 6) if m < MISC else ("mlstm", m - MQ, 4)
                            w0, w2 = col(nm + "_conv_w", i), col(nm + "_conv_w", 2 * w_ + i)
                            madd(o[:, 1:CTX], u[:, 0:CTX - 1], w0)
                            madd(o[:, CTX + 1:T], u[:, CTX:T - 1], w0).then_inc(s["dve_step"], 1)
                            dve.wait_ge(s["dve_step"], step())
                            madd(o[:, 0:CTX - 1], u[:, 1:CTX], w2).then_inc(s["dve_step"], 1)
                            dve.wait_ge(s["dve_step"], step())
                            madd(o[:, CTX:T - 1], u[:, CTX + 1:T], w2).then_inc(s["tmp_dve"], 1)
                        else:
                            i = SHIFTED[m]
                            s2 = [MU2[pp, 2 * i + q:2 * i + q + 1] for q in range(2)]
                            s4 = [MUJ[pp, 4 * i + q:4 * i + q + 1] for q in range(4)]
                            ol = o[:, CTX:T].rearrange("p (r w) -> p r w", w=GRID_W)
                            ul = u[:, CTX:T].rearrange("p (r w) -> p r w", w=GRID_W)
                            madd(o[:, 1:CTX], u[:, 0:CTX - 1], s2[0])
                            madd(ol[:, :, 1:], ul[:, :, :GRID_W - 1], s4[0]).then_inc(s["dve_step"], 1)
                            dve.wait_ge(s["dve_step"], step())
                            madd(o[:, 0:CTX - 1], u[:, 1:CTX], s2[1])
                            madd(ol[:, :, :GRID_W - 1], ul[:, :, 1:], s4[1]).then_inc(s["dve_step"], 1)
                            dve.wait_ge(s["dve_step"], step())
                            madd(ol[:, 1:, :], ul[:, :-1, :], s4[2]).then_inc(s["dve_step"], 1)
                            dve.wait_ge(s["dve_step"], step())
                            madd(ol[:, :-1, :], ul[:, 1:, :], s4[3]).then_inc(s["tmp_dve"], 1)

                    rc = [RC[RS, i:i + 1] for i in range(8)]
                    dve.wait_ge(s["row_in"], 7 * 16)
                    v.tensor_tensor(RP[RS, 4:5], rc[4], rc[5], ALU.subtract).then_inc(s["dve_step"], 1)
                    dve.wait_ge(s["dve_step"], step())
                    v.tensor_tensor(RP[RS, 5:6], RP[RS, 0:1], RP[RS, 4:5], ALU.mult).then_inc(s["rows_dve"], 1)
                    dve.wait_ge(s["rows_act"], 4)
                    v.tensor_scalar(t2, t1, 1.0, None, ALU.add).then_inc(s["dve_step"], 1)
                    dve.wait_ge(s["dve_step"], step())
                    v.tensor_scalar(RP[RS, 7:8], RP[RS, 6:7], -1.0, None, ALU.mult).then_inc(s["rows_dve"], 1)
                    post(0)
                    dve.wait_ge(s["rows_act"], 5)
                    v.tensor_scalar(t2, t2, -1.0, 5e-8, ALU.add, ALU.max).then_inc(s["dve_step"], 1)
                    dve.wait_ge(s["dve_step"], step())
                    v.reciprocal(t2, t2).then_inc(s["dve_step"], 1)
                    dve.wait_ge(s["dve_step"], step())
                    post(1)
                    v.tensor_tensor(t1, t1, t2, ALU.mult).then_inc(s["dve_step"], 1)
                    dve.wait_ge(s["dve_step"], step())
                    v.tensor_tensor(CF, CF, t1, ALU.mult).then_inc(s["dve_step"], 1)
                    dve.wait_ge(s["dve_step"], step())
                    v.scalar_tensor_tensor(out=SP, in0=zr, scalar=0.0, in1=CF, op0=ALU.max, op1=ALU.add).then_inc(
                        s["dve_step"], 1)
                    dve.wait_ge(s["dve_step"], step())
                    v.tensor_scalar(LOG, SP, RP[RS, 7:8], None, ALU.mult).then_inc(s["dve_step"], 1)
                    dve.wait_ge(s["dve_step"], step())
                    post(2)
                    on = ones[RS, 0:P]
                    for c in range(NC):
                        v.tensor_tensor_scan(out=CF[:, ck(c)], data0=on, data1=LOG[:, ck(c)], initial=0.0,
                                             op0=ALU.mult, op1=ALU.add)
                        ins = v.tensor_tensor_scan(out=CB[:, ck(c)][:, ::-1], data0=on, data1=LOG[:, ck(c)][:, ::-1],
                                                   initial=0.0, op0=ALU.mult, op1=ALU.add)
                    ins.then_inc(s["dve_step"], 1)
                    dve.wait_ge(s["dve_step"], step())
                    post(3)
                    v.tensor_scalar(CC, CF, rc[0], None, ALU.mult).then_inc(s["dve_step"], 1)
                    dve.wait_ge(s["dve_step"], step())
                    v.scalar_tensor_tensor(out=CC, in0=CB, scalar=rc[1], in1=CC, op0=ALU.mult, op1=ALU.add).then_inc(
                        s["dve_step"], 1)
                    dve.wait_ge(s["dve_step"], step())
                    v.tensor_scalar(KR, KR, rc[5], RP[RS, 1:2], ALU.mult, ALU.add).then_inc(s["dve_step"], 1)
                    dve.wait_ge(s["dve_step"], step())
                    v.tensor_tensor(KR, KR, CC, ALU.subtract).then_inc(s["dve_step"], 1)
                    dve.wait_ge(s["dve_step"], step())
                    post(4)
                    v.memset(MC[:, :], 0.0)
                    v.memset(MS5[:, 4:5], 0.0)
                    v.tensor_copy(MS5[RS, 0:1], RP[RS, 3:4]).then_inc(s["dve_step"], 1)
                    dve.wait_ge(s["dve_step"], step())
                    for k in (4, 0, 1, 2, 3):
                        cf, cb = (0, 0) if k == 4 else (k + 1, 4 - k)
                        v.tensor_tensor_scan(out=MF[:, ck(cf)], data0=KR[:, ck(cf)], data1=KR[:, ck(cf)],
                                             initial=MS5[RS, k:k + 1], op0=ALU.max, op1=ALU.max)
                        v.tensor_tensor_scan(out=MB[:, ck(cb)][:, ::-1], data0=KR[:, ck(cb)][:, ::-1],
                                                  data1=KR[:, ck(cb)][:, ::-1], initial=MS5[RS, k:k + 1],
                                                  op0=ALU.max, op1=ALU.max).then_inc(s["dve_step"], 1)
                        dve.wait_ge(s["dve_step"], step())
                        ef, eb = cf * P + P - 1, cb * P
                        v.tensor_tensor(MS5[RS, 5:6], MF[:, ef:ef + 1], CF[:, ef:ef + 1], ALU.add).then_inc(
                            s["dve_step"], 1)
                        dve.wait_ge(s["dve_step"], step())
                        v.tensor_tensor(MS5[RS, 6:7], MB[:, eb:eb + 1], CB[:, eb:eb + 1], ALU.add).then_inc(
                            s["dve_step"], 1)
                        dve.wait_ge(s["dve_step"], step())
                        v.tensor_scalar(MS5[RS, 5:6], MS5[RS, 5:6], rc[2], None, ALU.mult).then_inc(s["dve_step"], 1)
                        dve.wait_ge(s["dve_step"], step())
                        dst = mfin[RS, 0:1] if k == 4 else MS5[RS, 7:8] if k == 3 else MS5[RS, k + 1:k + 2]
                        v.scalar_tensor_tensor(out=dst, in0=MS5[RS, 6:7], scalar=rc[3], in1=MS5[RS, 5:6],
                                                    op0=ALU.mult, op1=ALU.add).then_inc(s["dve_step"], 1)
                        dve.wait_ge(s["dve_step"], step())
                        post(5 + (0 if k == 4 else k + 1))
                    v.tensor_scalar(MC[RS, 1:5], MS5[RS, 0:4], rc[2], None, ALU.mult).then_inc(s["dve_step"], 1)
                    dve.wait_ge(s["dve_step"], step())
                    v.scalar_tensor_tensor(out=MC[RS, 1:5], in0=MS5[RS, 0:4][:, ::-1], scalar=rc[3],
                                                in1=MC[RS, 1:5], op0=ALU.mult, op1=ALU.add).then_inc(s["dve_step"], 1)
                    dve.wait_ge(s["dve_step"], step())
                    v.tensor_scalar(Rr, MF, rc[6], None, ALU.mult).then_inc(s["dve_step"], 1)
                    dve.wait_ge(s["dve_step"], step())
                    post(10)
                    v.scalar_tensor_tensor(out=Rr, in0=MB, scalar=rc[7], in1=Rr, op0=ALU.mult, op1=ALU.add).then_inc(
                        s["dve_step"], 1)
                    dve.wait_ge(s["dve_step"], step())
                    v.scalar_tensor_tensor(out=Rr, in0=CC, scalar=rc[4], in1=Rr, op0=ALU.mult, op1=ALU.add).then_inc(
                        s["dve_step"], 1)
                    dve.wait_ge(s["dve_step"], step())
                    v.tensor_scalar(RE[RS, :], Rr[:, P - 1:T:P], rc[0], None, ALU.mult).then_inc(s["dve_step"], 1)
                    dve.wait_ge(s["dve_step"], step())
                    v.scalar_tensor_tensor(out=RE[RS, :], in0=Rr[:, 0:T:P], scalar=rc[1], in1=RE[RS, :],
                                                op0=ALU.mult, op1=ALU.add).then_inc(s["dve_step"], 1)
                    dve.wait_ge(s["dve_step"], step())
                    v.tensor_tensor(EM, Rr, CC, ALU.subtract).then_inc(s["rows_dve"], 1)

                    for j in range(11, len(POST)):
                        post(j)
                    dve.wait_ge(s["feat_ready"], len(POST))
                    for f in range(2):
                        v.tensor_scalar(U[:, MK + f, :], U[:, MK + f, :], HD ** -0.5, None, ALU.mult).then_inc(
                            s["k_scaled"], 1)
                    dve.wait_ge(s["pair_read"], NU + 2)
                    v.reciprocal(tmp, tmp).then_inc(s["dve_step"], 1)
                    dve.wait_ge(s["dve_step"], step())
                    v.tensor_tensor(KK, KK, tmp, ALU.mult).then_inc(s["dve_step"], 1)
                    dve.wait_ge(s["dve_step"], step())
                    dve.wait_ge(s["pair_read"], NU + 10)
                    for d in range(2):
                        v.tensor_scalar(LW[d], LW[d], -ISQE, None, ALU.mult)
                        for f in range(2):
                            ins = v.tensor_scalar(KD[d][:, f, :], BB[d][:, f, :], col("rwkv_k_a", f), KAO[:, f:f + 1],
                                                  ALU.mult, ALU.add)
                        ins.then_inc(s["dve_step"], 1)
                        dve.wait_ge(s["dve_step"], step())
                        v.tensor_tensor(KD[d], KD[d], U[:, RK_:RK_ + 2, :], ALU.mult)
                        ins = v.tensor_tensor(BB[d], BB[d], KK, ALU.mult)
                    ins.then_inc(s["rw_ready"], 1)
                    dve.wait_ge(s["rw_ready"], 1)
                    dve.wait_ge(s["rows_act"], 6)
                    v.tensor_tensor(DD[RS, :].rearrange("p (r c) -> p r c", c=5),
                                        ident[RS, R0:R0 + NR].unsqueeze(2).broadcast_to((NR, NR, 5)),
                                        DEC[RS, :].unsqueeze(1).broadcast_to((NR, NR, 5)), ALU.mult).then_inc(
                                            s["dec_diag"], 1)
                    v.memset(VA[:, :, 64:65], 1.0).then_inc(s["dve_step"], 1)
                    dve.wait_ge(s["dve_step"], step())
                    dve.wait_ge(s["ada_mm"], ADA_LATE[1][0])
                    biased(2, slice(ADA1, ADA_LATE[1][0])).then_inc(s["mod_mid"], 1)
                    dve.wait_ge(s["mod_mid"], 1)

                    def heads(ap, n):
                        return ap.rearrange("p (h n) -> p h n", h=n)

                    def wide(ap, n):
                        return ap.unsqueeze(2).broadcast_to((P, ap.shape[1], n))

                    for c in range(NC):
                        dve.wait_ge(s["ta_act"], 4 * c + 3)
                        v.tensor_tensor(SPTE, COLS[:, c, 0, 0:16], COLS[:, c, 3, 0:16], ALU.mult).then_inc(
                            s["dve_step"], 1)
                        dve.wait_ge(s["dve_step"], step())
                        if c > 0:
                            dve.wait_ge(s["cs_mm"], c)
                        for d in range(2):
                            v.tensor_tensor(heads(XE[:, d, :], 8), heads(XT, 8), wide(SPTE[:, 8 * d:8 * d + 8], 64),
                                            ALU.mult)
                            r = 16 + 4 * d
                            ins = v.tensor_tensor(heads(VE[:, d, :], 4), VA, wide(COLS[:, c, 3, r:r + 4], 65),
                                                  ALU.mult)
                        ins.then_inc(s["xe_ready"], 1)
                    dve.wait_ge(s["ada_mm"], 48)
                    modulation(7, slice(ADA_LATE[1][0], 48), 4 * KT, 1, "norm2_g", 0, KT)
                    dve.wait_ge(s["cs_read"], NC)
                    dve.wait_ge(s["r_hi"], 1)
                    v.tensor_tensor(Rlo, Rr, Rhi.bitcast(F32), ALU.subtract).then_inc(s["r_lo"], 1)
                    dve.wait_ge(s["r_lo"], 1)
                    dve.wait_ge(s["ex_zero"], 1)
                    for n in range(2):
                        expand(v, n, 1).then_inc(s["ex_lo"], 1)
                    MI = [PP[:, 256 * d + P:256 * d + 2 * P] for d in range(2)]

                    def over(mask, n):
                        return mask.unsqueeze(1).broadcast_to((P, n, mask.shape[1]))

                    def y_back(c):
                        dve.wait_ge(s["yt_mm"], c + 1)
                        for q in range(4):
                            y_ = U[:, XS + q, ck(c)]
                            v.scalar_tensor_tensor(out=y_, in0=y_, scalar=dcol[:, q:q + 1],
                                                   in1=PS[:, 4, q * P:(q + 1) * P], op0=ALU.mult, op1=ALU.add)
                        v.tensor_copy(U[:, MV:MV + 2, ck(c)], heads(PS[:, 6, 0:256], 2)).then_inc(s["yt_read"], 1)

                    for c in range(NC):
                        dve.wait_ge(s["ta_act"], 4 * NC + 2 * c + 1)
                        if 4 * c > 0:
                            dve.wait_ge(s["y_mm"], 4 * c)
                        for d in range(2):
                            ins = v.tensor_tensor(heads(XE[:, d, :], 8), heads(XT, 8),
                                                  wide(COLS[:, c, 0, 8 * d:8 * d + 8], 64), ALU.mult)
                        ins.then_inc(s["xd_ready"], 1)
                        dve.wait_ge(s["qk_mm"], c + 1)
                        for i in range(6):
                            if 6 * c + i + 2 < 6 * NC:
                                dve.wait_ge(s["bc_mm"], 6 * c + i + 1)
                                expand(v, 6 * c + i + 2, 1).then_inc(s["ex_lo"], 1)
                            dve.wait_ge(s["bc_exp"], 6 * c + i + 1)
                            if i < 4:
                                w_ = heads(W[:, i % 4, :], 4)
                                m_ = over(PS[:, i // 2, 0:P], 4)
                            else:
                                w_ = W[:, i % 4, :].rearrange("p (f q n) -> p q f n", f=2, q=2)
                                m_ = PS[:, 0:2, P:3 * P].rearrange("p q (f n) -> p q f n", f=2)
                            v.tensor_tensor(w_, w_, m_, ALU.mult).then_inc(s["w_ready"], 1)
                            if i == 1 and c:
                                y_back(c - 1)
                        dve.wait_ge(s["y_mm"], 4 * c + 2)
                        if c == 0:
                            dve.wait_ge(s["stored"], 7 * 16)
                            v.tensor_copy(YS, PS[:, 4, :]).then_inc(s["y_comb"], 1)
                        else:
                            for d, dst in enumerate((YS, YT)):
                                ec = COLS[:, c, 2, 8 * d:8 * d + 8].rearrange("p (g h) -> p g h", g=2)
                                v.tensor_tensor(
                                    dst.rearrange("p (g h n) -> p g h n", g=2, h=4),
                                    PS[:, 5:7, 256 * d:256 * d + 256].rearrange("p g (h n) -> p g h n", h=4),
                                    ec.unsqueeze(3).broadcast_to((P, 2, 4, 64)), ALU.mult).then_inc(s["dve_step"], 1)
                                dve.wait_ge(s["dve_step"], step())
                            v.tensor_tensor(YS, YS, YT, ALU.add).then_inc(s["dve_step"], 1)
                            dve.wait_ge(s["dve_step"], step())
                            v.tensor_tensor(YS, YS, PS[:, 4, :], ALU.add).then_inc(s["y_comb"], 1)
                        for d in range(2):
                            dve.wait_ge(s["y_mm"], 4 * c + 3 + d)
                            dve.wait_ge(s["y_comb"], 3 * c + 1 + d)
                            num, inter = (7, 0) if d == 0 else (2, 5)
                            nps = heads(PS[:, num, 0:260], 4)
                            r = 16 + 4 * d
                            nm_sem = s["num_read"] if d else s["dve_step"]
                            if c == 0:
                                v.tensor_copy(NM, nps).then_inc(nm_sem, 1)
                            else:
                                ec = COLS[:, c, 2, r:r + 4].rearrange("p (f q) -> p q f", q=2)
                                v.tensor_tensor(
                                    NM.rearrange("p (f q) n -> p q f n", q=2),
                                    PS[:, inter:inter + 2, 0:130].rearrange("p q (f n) -> p q f n", f=2),
                                    ec.unsqueeze(3).broadcast_to((P, 2, 2, 65)), ALU.mult).then_inc(s["dve_step"], 1)
                                dve.wait_ge(s["dve_step"], step())
                                v.tensor_tensor(NM, NM, nps, ALU.add).then_inc(nm_sem, 1)
                            dve.wait_ge(nm_sem, c + 1 if d else step())
                            dn = NM[:, :, 64]
                            v.scalar_tensor_tensor(out=DN[:, 0:4], in0=dn, scalar=-1.0, in1=dn, op0=ALU.mult,
                                                        op1=ALU.max).then_inc(s["dve_step"], 1)
                            dve.wait_ge(s["dve_step"], step())
                            v.tensor_tensor(DN[:, 0:4], DN[:, 0:4], COLS[:, c, 4, r:r + 4], ALU.max).then_inc(
                                s["dve_step"], 1)
                            dve.wait_ge(s["dve_step"], step())
                            v.reciprocal(DN[:, 4:8], DN[:, 0:4]).then_inc(s["dve_step"], 1)
                            dve.wait_ge(s["dve_step"], step())
                            y_ = v.tensor_tensor(heads((YM, YM2)[d], 4), NM[:, :, 0:64], wide(DN[:, 4:8], 64), ALU.mult)
                            if d == 0:
                                y_.then_inc(s["y_comb"], 1)
                            else:
                                y_.then_inc(s["dve_step"], 1)
                                dve.wait_ge(s["dve_step"], step())
                                v.tensor_tensor(YM, YM, YM2, ALU.add).then_inc(s["y_comb"], 1)
                    def prep_scan(k):
                        for d in range(2):
                            b, i = units[d], 2 * k + d
                            c = ck(0 if k == 0 else (k if d == 0 else 5 - k))
                            for f in range(2):
                                o, s_ = b["c"][:, f, :], LW[d][:, f, c]
                                if d:
                                    o, s_ = o[:, ::-1], s_[:, ::-1]
                                ins = v.tensor_tensor_scan(out=o, data0=ones[:, :], data1=s_, initial=0.0,
                                                           op0=ALU.mult, op1=ALU.add)
                            ins.then_inc(s["dve_step"], 1)
                            dve.wait_ge(s["dve_step"], step())
                            v.tensor_copy(MID[:, 2 * d:2 * d + 2], b["c"][:, :, 64]).then_inc(s["dve_step"], 1)
                            dve.wait_ge(s["dve_step"], step())
                            for f in range(2):
                                ins = v.tensor_scalar(b["c"][:, f, :], b["c"][:, f, :],
                                                      MID[:, 2 * d + f:2 * d + f + 1], None, ALU.subtract)
                            ins.then_inc(s["dve_step"], 1)
                            dve.wait_ge(s["dve_step"], step())
                            v.tensor_tensor(b["e3"], b["c"], LW[d][:, :, c], ALU.subtract).then_inc(s["rs_dve"], 1)

                    def prep_keys(k):
                        for d in range(2):
                            b, i = units[d], 2 * k + d
                            c = ck(0 if k == 0 else (k if d == 0 else 5 - k))
                            dve.wait_ge(s["rs_exp"], i + 1)
                            if k:
                                dve.wait_ge(s["rw_prod2"], 2 * i - 2)
                            v.tensor_tensor(b["KB"][:, :, 0, :], KD[d][:, :, c], b["e2"], ALU.mult)
                            ins = v.tensor_tensor(b["KB"][:, :, 1, :], BB[d][:, :, c], b["e2"], ALU.mult)
                        ins.then_inc(s["dve_step"], 1)
                        dve.wait_ge(s["dve_step"], step())

                    prep_scan(0)
                    y_back(NC - 1)
                    prep_keys(0)
                    v.memset(U[:, BT_:BT_ + 2, :], 0.0).then_inc(s["dve_step"], 1)
                    dve.wait_ge(s["dve_step"], step())
                    for k in range(NC):
                        for d in range(2):
                            b, i = units[d], 2 * k + d
                            c = ck(0 if k == 0 else (k if d == 0 else 5 - k))
                            if k == 1:
                                dve.wait_ge(s["rf_ready"], 2)
                            if i - 1 > 0:
                                dve.wait_ge(s["yr_mm"], i - 1)
                            v.tensor_tensor(b["RK"][:, :, 1, :], U[:, RR_:RR_ + 2, c], b["e1"], ALU.mult)
                            v.tensor_tensor(b["RK"][:, :, 0, :], KK[:, :, c], b["e3"], ALU.mult)
                            ins = v.tensor_copy(LAST[:, 2 * d:2 * d + 2], b["e1"][:, :, P - 1 if d == 0 else 0])
                            if k:
                                ins = v.tensor_tensor(b["Sp"], b["S"], wide(EMID[:, 2 * d:2 * d + 2], 64), ALU.mult)
                            ins.then_inc(s["rw_feat"], 1)
                        dve.wait_ge(s["rw_feat"], 2 * k + 2)
                        for d in range(2):
                            b, a, i = units[d], 4 * d, 2 * k + d
                            dve.wait_ge(s["rw_prod"], i + 1)
                            for hb in range(2):
                                ps = PS[:, a + 2 + hb, :].rearrange("p (h w t) -> p h w t", h=2, w=2)
                                v.tensor_tensor(b["Q"][:, hb:4:2, :], ps[:, :, 0, :],
                                                over(M16[:, d * P:(d + 1) * P], 2), ALU.mult)
                                ins = v.tensor_tensor(b["RBT"][:, hb:4:2, :], ps[:, :, 1, :],
                                                      over(MI[d], 2), ALU.mult)
                            ins.then_inc(s["rw_masked"], 1)
                        dve.wait_ge(s["rw_masked"], 2 * k + 2)
                        for d in range(2):
                            b, a, i = units[d], 4 * d, 2 * k + d
                            dve.wait_ge(s["rw_prod2"], 2 * i + 1)
                            for hb in range(2):
                                ins = v.tensor_tensor(b["PT"][:, hb:4:2, :], heads(PS[:, a + hb, 0:256], 2),
                                                      over(NP[:, 256 * (1 - d):256 * (1 - d) + P], 2), ALU.mult)
                            ins.then_inc(s["dve_step"], 1)
                            dve.wait_ge(s["dve_step"], step())
                            v.tensor_tensor(b["QT"], b["PT"], over(BLK[:, :], 4), ALU.mult)
                            v.tensor_tensor(b["X"], b["Q"], over(ident[:, :], 4), ALU.add)
                            dve.wait_ge(s["rw_prod2"], 2 * i + 2)
                            for hb in range(2):
                                ps = PS[:, a + 2 + hb, :].rearrange("p (h w t) -> p h w t", h=2, w=2)
                                v.tensor_tensor(b["BTm"][:, hb:4:2, :], ps[:, :, 0, :],
                                                over(PP[:, 256 * d:256 * d + P], 2), ALU.mult)
                                ins = v.tensor_tensor(b["RKT"][:, hb:4:2, :], ps[:, :, 1, :],
                                                      over(MI[d], 2), ALU.mult)
                            ins.then_inc(s["rw_masked2"], 1)

                        def level(l):
                            for d in range(2):
                                b = units[d]
                                if l:
                                    dve.wait_ge(s["inv_mm"], 20 * k + 2 * (2 + 2 * l) + d + 1)
                                v.tensor_tensor(b["PL"], b["PT"], over(ML[:, l * P:(l + 1) * P], 4), ALU.mult).then_inc(
                                    s["pl_ready"], 1)

                        def adds(r, n):
                            for d in range(2):
                                b = units[d]
                                dve.wait_ge(s["inv_mm"], 20 * k + 2 * r + d + 1)
                                if n:
                                    dve.wait_ge(s["inv_add"], 12 * k + 2 * (n - 1) + d + 1)
                                v.tensor_tensor(b["X"], b["X"], heads(PS[:, 4 * d + 2, :], 4), ALU.add).then_inc(
                                    s["inv_add"], 1)
                        dve.wait_ge(s["rw_masked2"], 2 * k + 2)
                        level(0)
                        for r in range(3):
                            adds(1 + r, r)
                            if r == 0 and k < NC - 1:
                                prep_scan(k + 1)
                        for l in range(3):
                            if l < 2:
                                level(l + 1)
                            adds(5 + 2 * l, 3 + l)
                            if l == 0 and k < NC - 1:
                                prep_keys(k + 1)
                        for d in range(2):
                            b, a, i = units[d], 4 * d, 2 * k + d
                            c = ck(0 if k == 0 else (k if d == 0 else 5 - k))
                            dve.wait_ge(s["yr_mm"], i + 1)
                            if i > 0:
                                dve.wait_ge(s["yr_read"], i)
                            v.tensor_tensor(U[:, BT_:BT_ + 2, c], U[:, BT_:BT_ + 2, c],
                                                heads(PS[:, a + 3, 0:256], 2), ALU.add).then_inc(s["yr_read"], 1)
                            if k == 4:
                                continue
                            dve.wait_ge(s["st_mm"], i + 1)
                            last = LAST[:, 2 * d:2 * d + 2]
                            st = heads(PS[:, a + 1, 0:128], 2)
                            if k == 0:
                                sf = heads(b["s"].rearrange("p f t -> p (f t)")[:, 0:128], 2)
                                v.tensor_tensor(sf, st, wide(last, 64), ALU.mult).then_inc(s["rf_ready"], 1)
                            else:
                                v.tensor_tensor(b["S"], b["Sp"], st, ALU.add).then_inc(s["dve_step"], 1)
                                dve.wait_ge(s["dve_step"], step())
                                v.tensor_tensor(b["S"], b["S"], wide(last, 64), ALU.mult).then_inc(s["dve_step"], 1)
                                dve.wait_ge(s["dve_step"], step())

                    def pair(ap):
                        return ap.rearrange("p (a t) -> p a t", a=2)

                    for f in range(2):
                        dve.wait_ge(s["g_mm"], f + 1)
                        v.tensor_tensor(pair(gtmp[:, 6 + f, :]), PS[:, 2 * f:2 * f + 2, 0:HALF],
                                        pair(U[:, RV_ + f, :]), ALU.mult).then_inc(s["g_read"], 1)

                    def centre(t_, b, n):
                        dve.wait_ge(s["g_mm"], n)
                        v.scalar_tensor_tensor(out=pair(U[:, t_, :]), in0=PS[:, b:b + 2, 0:HALF], scalar=-1.0 / 64,
                                               in1=pair(U[:, t_, :]), op0=ALU.mult, op1=ALU.add).then_inc(
                            s["g_read"], 1)
                    for n in range(2):
                        centre(MV + n, 4 + 2 * n, 3 + n)
                    dve.wait_ge(s["g_read"], 2)
                    v.tensor_tensor(U[:, BT_:BT_ + 2, :], U[:, BT_:BT_ + 2, :], gtmp[:, 6:8, :], ALU.add).then_inc(
                        s["g_src"], 1)
                    dve.wait_ge(s["g_src"], 1)
                    for n in range(2):
                        centre(BT_ + n, 2 * n, 6 + n)
                    for n, rows in enumerate((slice(0, 64), slice(0, P))):
                        dve.wait_ge(s["g_std"], n + 1)
                        v.reciprocal(gtmp[rows, 2 + n, :], gtmp[rows, 2 + n, :]).then_inc(s["g_rec"], 1)
                    dve.wait_ge(s["g_read"], 6)

                    def y_low(k):
                        dve.wait_ge(s["y_hi"], k + 1)
                        v.tensor_tensor(U_r[:, YTILES[k], :], U[:, YTILES[k], :], rp_r[:, k, :].bitcast(F32),
                                        ALU.subtract).then_inc(s["y_lo"], 1)

                    for n in range(6):
                        b_ = 2 * (n % 4)
                        dve.wait_ge(s["g_mm"], 9 + n)
                        for t_, gate, nm, f in (
                                ((XS + 2 * n, None, "ssd_norm_g", 2 * n), (XS + 2 * n + 1, None, "ssd_norm_g", 2 * n + 1))
                                if n < 2 else
                                (((BT_, LORA, "rwkv_norm_g", 0), (CT_, MISC, "rwkv_norm_g", 1),
                                  (MV, MO, "mlstm_norm_g", 0), (MV + 1, MO + 1, "mlstm_norm_g", 1))[n - 2],)):
                            y_ = U[:, t_, :]
                            ins = v.scalar_tensor_tensor(out=pair(y_), in0=pair(y_), scalar=col(nm, f),
                                                         in1=PS[:, b_:b_ + 2, 0:HALF], op0=ALU.mult, op1=ALU.mult)
                            if gate is not None:
                                ins.then_inc(s["dve_step"], 1)
                                dve.wait_ge(s["dve_step"], step())
                                ins = v.tensor_tensor(y_, y_, U[:, gate, :], ALU.mult)
                            ins.then_inc(s["y_done"], 1)
                        for k in ((), (0, 1), (2, 3), (4,), (5,), (6,))[n]:
                            y_low(k)
                    y_low(7)

                    def residual(b, m, row, sem):
                        g = MOD[:, 2 * (row + m):2 * (row + m) + 2]
                        for bank, c0, t0, t1, cond in ((b, 0, 0, CTX, 0), (b, CTX, CTX, HALF, 1),
                                                       (b + 1, 0, HALF, T, 1)):
                            ins = v.scalar_tensor_tensor(out=xv[:, m, t0:t1], in0=PS[:, bank, c0:c0 + t1 - t0],
                                                         scalar=g[:, cond:cond + 1], in1=xv[:, m, t0:t1],
                                                         op0=ALU.mult, op1=ALU.add)
                        ins.then_inc(sem, 1)
                    for m in range(KT):
                        dve.wait_ge(s["wo_mm"], m + 1)
                        residual(4 + 2 * (m % 2), m, 16, s["wo_read"])
                    dve.wait_ge(s["wo_read"], KT)
                    norm(1)
                    for k in range(KT):
                        low_part(1, k)

                    def u_low(t_):
                        dve.wait_ge(s["u_hi"], t_ + 1)
                        v.tensor_tensor(U_r[:, t_, :], U[:, t_, :], u_high_r[t_].bitcast(F32),
                                        ALU.subtract).then_inc(s["u_lo"], 1)

                    for j in range(FT):
                        dve.wait_ge(s["ffn_silu"], j + 1)
                        dve.wait_ge(s["ffn_mm"], 2 * j + 2)
                        b_ = 4 * (j % 2) + 2
                        v.tensor_tensor(pair(U[:, j, :]), pair(tmp[:, j % 2, :]), PS[:, b_:b_ + 2, 0:HALF],
                                        ALU.mult).then_inc(s["ffn_ready"], 1)
                        if 0 < j <= U_EARLY:
                            u_low(j - 1)
                    for t_ in range(U_EARLY, FT):
                        u_low(t_)
                    for m in range(KT):
                        dve.wait_ge(s["w2_mm"], 3 * m + 3)
                        residual(2 * (m % 2), m, 40, s["w2_read"])

            nc.all_engine_barrier(sems_to_clear=range(first, last_sem + 1))

        out_p = io["out_0"].rearrange("a t f -> (a t) f")
        out_s = io["out_1"].rearrange("a (c p) f -> (a c) p f", p=P)
        yo = Ub[:, 0:NC * D].rearrange("p (c f) -> p c f", c=NC)
        with nc.Block() as block:
            @block.scalar
            def _(act):
                for k in range(KT):
                    if k >= 2:
                        act.wait_ge(tail["sq_used"], k - 1)
                    nc.scalar.activation(tmp[:, k % 2, :], xv[:, k, :], ACT.Square).then_inc(tail["sq"], 1)
                act.wait_ge(tail["sq_used"], KT)
                nc.scalar.activation(rs.rearrange("p (a t) -> p a t", a=2), PS[:, 0:2, 0:HALF], ACT.Sqrt,
                                     bias=eps[:, 0:1], scale=1.0 / D).then_inc(tail["std"], 1)

            @block.tensor
            def _(pe):
                for k in range(KT):
                    pe.wait_ge(tail["sq"], k + 1)
                    for hf in range(2):
                        ins = nc.tensor.matmul(PS[:, hf, 0:HALF], ones[:, :], tmp[:, k % 2, hf * HALF:(hf + 1) * HALF],
                                               start=k == 0, stop=k == KT - 1)
                    ins.then_inc(tail["sq_used"], 1)
                pe.wait_ge(tail["y"], KT)
                for n in range(2 * NC):
                    c, hf = n // 2, n % 2
                    if n >= 6:
                        pe.wait_ge(tail["read"], n - 5)
                    for q in range(4):
                        ins = nc.tensor.transpose(PS[:, 2 + n % 6, q * P:(q + 1) * P], h[:, 4 * hf + q, ck(c)],
                                                  ident[:, :])
                    ins.then_inc(tail["mm"], 1)

            @block.vector
            def _(dve):
                dve.wait_ge(tail["std"], 1)
                nc.vector.reciprocal(rs, rs).then_inc(tail["rs"], 1)
                dve.wait_ge(tail["rs"], 1)
                for k in range(KT):
                    nc.vector.scalar_tensor_tensor(out=h[:, k, :], in0=xv[:, k, :], scalar=fg[:, k:k + 1], in1=rs,
                                                   op0=ALU.mult, op1=ALU.mult).then_inc(tail["y"], 1)
                for n in range(2 * NC):
                    c, hf = n // 2, n % 2
                    dve.wait_ge(tail["mm"], n + 1)
                    nc.vector.tensor_copy(yo[:, c, 512 * hf:512 * hf + 512], PS[:, 2 + n % 6, :]).then_inc(
                        tail["read"], 1)

            @block.sync
            def _(sp):
                for c in range(NC):
                    sp.wait_ge(tail["read"], 2 * c + 2)
                    dst = out_p if c == 0 else out_s[c - 1]
                    sp.dma_start(dst, yo[:, c, :]).then_inc(tail["stored"], 16)
                sp.wait_ge(tail["stored"], 16 * NC)


_INS = ['x_prompt', 'x_sample', 'state_ssd', 'state_rwkv', 'state_mlstm_c', 'state_mlstm_n', 'state_mlstm_m', 'c',
        'c_ctx', 'ada_w', 'ada_b', 'norm1_g', 'norm2_g', 'w_in', 'ssd_conv_w', 'ssd_conv_b', 'ssd_dt_bias',
        'ssd_a_log', 'ssd_d', 'ssd_norm_g', 'rwkv_mu', 'rwkv_w0', 'rwkv_w2', 'rwkv_a0', 'rwkv_a2', 'rwkv_g2',
        'rwkv_k_k', 'rwkv_k_a', 'rwkv_r_k', 'rwkv_norm_g', 'mlstm_conv_w', 'mlstm_conv_b', 'mlstm_i_bias',
        'mlstm_f_bias', 'mlstm_norm_g', 'w_out', 'ffn_w1', 'ffn_w3', 'ffn_w2', 'final_norm_g']
_OUTS = [(1, CTX, D), (1, LAT, D), (1, DEPTH, 2, SSD_H, HD, 64), (1, DEPTH, 2, RWKV_H, HD, HD),
         (1, DEPTH, 2, ML_H, HD, HD), (1, DEPTH, 2, ML_H, HD), (1, DEPTH, 2, ML_H)]


def kernel(**inputs):
    import numpy as np
    import concourse.bacc as bacc
    from concourse.bass_utils import run_bass_kernel_spmd

    nc = bacc.Bacc("TRN2", target_bir_lowering=False, num_devices=1)
    arrays, io = {}, {}
    for name in _INS:
        a = np.ascontiguousarray(inputs[name])
        arrays["in_" + name] = a
        io[name] = nc.dram_tensor("in_" + name, a.shape, mybir.dt.from_np(a.dtype), kind="ExternalInput").ap()
    for i, shape in enumerate(_OUTS):
        io["out_%d" % i] = nc.dram_tensor("out_%d" % i, shape, F32, kind="ExternalOutput").ap()
    build(nc, io)
    r = run_bass_kernel_spmd(nc, [arrays], core_ids=[0])
    return tuple(r.results[0]["out_%d" % i] for i in range(len(_OUTS)))
```
